# Optimizing a Trainium2 kernel written in Bass

```python
import math
import jax, jax.numpy as jnp
from jax import lax
import numpy as np

D_MODEL = 1024
BATCH = 1
SEQ = 256
DEPTH = 1

HEAD_DIM = 64
FOX_HEADS = 8
DIFF_HEADS = 4
FOX_WIDTH = FOX_HEADS * HEAD_DIM
DIFF_WIDTH = DIFF_HEADS * 2 * HEAD_DIM
MIX_WIDTH = FOX_WIDTH + DIFF_WIDTH
IN_WIDTH = 3 * FOX_WIDTH + FOX_HEADS + 3 * DIFF_WIDTH
D_FF = ((8 * D_MODEL // 3 + 255) // 256) * 256
BLOCK_Q = 128
EPS = 1e-6


def _rms(x, g):
    xf = x.astype(jnp.float32)
    y = xf * lax.rsqrt(jnp.mean(xf * xf, axis=-1, keepdims=True) + EPS)
    return (y * g.astype(jnp.float32)).astype(x.dtype)

def _to_blocks(t):
    b, h, s = t.shape[:3]
    nb = s // BLOCK_Q
    t = t.reshape((b, h, nb, BLOCK_Q) + t.shape[3:])
    return jnp.moveaxis(t, 2, 0)

def _from_blocks(t):
    nb, b, h, bq, d = t.shape
    return jnp.moveaxis(t, 0, 2).reshape(b, h, nb * bq, d)

def _fox_attention(q, k, v, log_f):
    s_len = q.shape[2]
    scale = 1.0 / math.sqrt(q.shape[-1])
    cum = jnp.cumsum(log_f, axis=-1)
    key_pos = jnp.arange(s_len)
    starts = jnp.arange(s_len // BLOCK_Q) * BLOCK_Q

    def one_block(args):
        qi, ci, st = args
        s = jnp.einsum('bhqd,bhkd->bhqk', qi, k, preferred_element_type=jnp.float32) * scale
        s = s + ci[..., :, None] - cum[..., None, :]
        qpos = st + jnp.arange(BLOCK_Q)
        mask = key_pos[None, :] <= qpos[:, None]
        p = jax.nn.softmax(jnp.where(mask, s, -jnp.inf), axis=-1)
        return jnp.einsum('bhqk,bhkd->bhqd', p.astype(v.dtype), v)

    out = lax.map(one_block, (_to_blocks(q), _to_blocks(cum), starts))
    return _from_blocks(out)

def _diff_attention(q1, q2, k1, k2, v, lam, slopes):
    s_len = q1.shape[2]
    scale = 1.0 / math.sqrt(q1.shape[-1])
    key_pos = jnp.arange(s_len)
    starts = jnp.arange(s_len // BLOCK_Q) * BLOCK_Q

    def one_block(args):
        q1i, q2i, st = args
        qpos = st + jnp.arange(BLOCK_Q)
        dist = (qpos[:, None] - key_pos[None, :]).astype(jnp.float32)
        alibi = -slopes[:, None, None] * dist
        mask = dist >= 0
        s1 = jnp.einsum('bhqd,bhkd->bhqk', q1i, k1, preferred_element_type=jnp.float32) * scale + alibi
        s2 = jnp.einsum('bhqd,bhkd->bhqk', q2i, k2, preferred_element_type=jnp.float32) * scale + alibi
        p = (jax.nn.softmax(jnp.where(mask, s1, -jnp.inf), axis=-1)
             - lam * jax.nn.softmax(jnp.where(mask, s2, -jnp.inf), axis=-1))
        return jnp.einsum('bhqk,bhkd->bhqd', p.astype(v.dtype), v)

    out = lax.map(one_block, (_to_blocks(q1), _to_blocks(q2), starts))
    return _from_blocks(out)

def _modulate(x, g, shift, scale):
    return _rms(x, g) * (1.0 + scale[:, None, :]) + shift[:, None, :]

def first_inputs(seed: int = 0) -> dict:
    key = jax.random.key(seed)
    ks = jax.random.split(key, 20)
    f32 = jnp.float32
    nrm = lambda k, shape, s: jax.random.normal(k, shape, f32) * s
    d = D_MODEL
    return {
        "x": nrm(ks[0], (BATCH, SEQ, d), 1.0),
        "c": nrm(ks[1], (BATCH, d), 1.0),
        "ln1_g": 1.0 + nrm(ks[2], (DEPTH, d), 0.02),
        "ln2_g": 1.0 + nrm(ks[3], (DEPTH, d), 0.02),
        "w_ada": nrm(ks[4], (DEPTH, d, 6 * d), 0.5 * d ** -0.5),
        "b_ada": nrm(ks[5], (DEPTH, 6 * d), 0.02),
        "w_in": nrm(ks[6], (DEPTH, d, IN_WIDTH), d ** -0.5),
        "b_f": 1.5 + nrm(ks[7], (DEPTH, FOX_HEADS), 0.1),
        "fox_qk_g": 1.0 + nrm(ks[8], (DEPTH, 2, HEAD_DIM), 0.02),
        "diff_qk_g": 1.0 + nrm(ks[9], (DEPTH, 2, HEAD_DIM), 0.02),
        "diff_lam": nrm(ks[10], (DEPTH, 4, HEAD_DIM), 0.1),
        "diff_norm_g": 1.0 + nrm(ks[11], (DEPTH, 2 * HEAD_DIM), 0.02),
        "w_out": nrm(ks[12], (DEPTH, MIX_WIDTH, d), MIX_WIDTH ** -0.5),
        "w_gate": nrm(ks[13], (DEPTH, d, D_FF), d ** -0.5),
        "w_up": nrm(ks[14], (DEPTH, d, D_FF), d ** -0.5),
        "w_down": nrm(ks[15], (DEPTH, D_FF, d), D_FF ** -0.5),
    }

def first_block(x, c, ln1_g, ln2_g, w_ada, b_ada, w_in, b_f, fox_qk_g, diff_qk_g,
              diff_lam, diff_norm_g, w_out, w_gate, w_up, w_down):
    b, s, d = x.shape
    cond = jax.nn.silu(c)
    slopes = 2.0 ** (-8.0 * jnp.arange(1, DIFF_HEADS + 1, dtype=jnp.float32) / DIFF_HEADS)
    splits = np.cumsum([FOX_WIDTH, FOX_WIDTH, FOX_WIDTH, FOX_HEADS,
                        DIFF_WIDTH, DIFF_WIDTH]).tolist()

    for l in range(DEPTH):
        mod = cond @ w_ada[l] + b_ada[l]
        sh1, sc1, g1, sh2, sc2, g2 = jnp.split(mod, 6, axis=-1)

        h = _modulate(x, ln1_g[l], sh1, sc1)
        u = h @ w_in[l]
        fq, fk, fv, fg, dq, dk, dv = jnp.split(u, splits, axis=-1)

        heads = lambda t, n, hd: t.reshape(b, s, n, hd).transpose(0, 2, 1, 3)
        fq = _rms(heads(fq, FOX_HEADS, HEAD_DIM), fox_qk_g[l, 0])
        fk = _rms(heads(fk, FOX_HEADS, HEAD_DIM), fox_qk_g[l, 1])
        fv = heads(fv, FOX_HEADS, HEAD_DIM)
        log_f = jax.nn.log_sigmoid(fg.astype(jnp.float32) + b_f[l].astype(jnp.float32))
        log_f = log_f.transpose(0, 2, 1)
        fox_out = _fox_attention(fq, fk, fv, log_f)

        dq = dq.reshape(b, s, DIFF_HEADS, 2, HEAD_DIM).transpose(0, 2, 3, 1, 4)
        dk = dk.reshape(b, s, DIFF_HEADS, 2, HEAD_DIM).transpose(0, 2, 3, 1, 4)
        dq = _rms(dq, diff_qk_g[l, 0])
        dk = _rms(dk, diff_qk_g[l, 1])
        dv = heads(dv, DIFF_HEADS, 2 * HEAD_DIM)
        lam_init = 0.8 - 0.6 * math.exp(-0.3 * l)
        lv = diff_lam[l].astype(jnp.float32)
        lam = jnp.exp(jnp.sum(lv[0] * lv[1])) - jnp.exp(jnp.sum(lv[2] * lv[3])) + lam_init
        diff_out = _diff_attention(dq[:, :, 0], dq[:, :, 1], dk[:, :, 0], dk[:, :, 1], dv, lam, slopes)
        diff_out = _rms(diff_out, diff_norm_g[l]) * (1.0 - lam_init)

        mixed = jnp.concatenate([
            fox_out.transpose(0, 2, 1, 3).reshape(b, s, FOX_WIDTH),
            diff_out.transpose(0, 2, 1, 3).reshape(b, s, DIFF_WIDTH)], axis=-1)
        x = x + g1[:, None, :] * (mixed @ w_out[l])

        h2 = _modulate(x, ln2_g[l], sh2, sc2)
        y = (jax.nn.silu(h2 @ w_gate[l]) * (h2 @ w_up[l])) @ w_down[l]
        x = x + g2[:, None, :] * y
    return x


PLE_DIM = 256
SGU_CHUNK = 128
SGU_GROUPS = 8
SGU_WIDTH = D_MODEL
SGU_GROUP_DIM = SGU_WIDTH // SGU_GROUPS
ATT_HEADS = 16
ATT_WIDTH = ATT_HEADS * HEAD_DIM
MOBA_BLOCK = 256
MOBA_TOPK = 3
Q_CHUNK = 64
REL_BUCKETS = 32
REL_MAX_DIST = 1024
D_FF_2 = 4 * D_MODEL
SPLITS = (SGU_WIDTH, SGU_WIDTH, ATT_WIDTH, ATT_WIDTH, ATT_WIDTH, D_MODEL, D_MODEL)
IN_COLS = sum(SPLITS)


def rms_norm(x, g):
    xf = x.astype(jnp.float32)
    y = xf * lax.rsqrt(jnp.mean(xf * xf, axis=-1, keepdims=True) + EPS)
    return (y * g.astype(jnp.float32)).astype(x.dtype)

def layer_norm(x, g, b):
    xf = x.astype(jnp.float32)
    mu = jnp.mean(xf, axis=-1, keepdims=True)
    xc = xf - mu
    y = xc * lax.rsqrt(jnp.mean(xc * xc, axis=-1, keepdims=True) + EPS)
    return (y * g.astype(jnp.float32) + b.astype(jnp.float32)).astype(x.dtype)

def rel_bucket(dist):
    n = jnp.maximum(dist, 0)
    max_exact = REL_BUCKETS // 2
    nf = jnp.maximum(n, max_exact).astype(jnp.float32)
    large = max_exact + (jnp.log(nf / max_exact) / math.log(REL_MAX_DIST / max_exact)
                         * (REL_BUCKETS - max_exact)).astype(jnp.int32)
    large = jnp.minimum(large, REL_BUCKETS - 1)
    return jnp.where(n < max_exact, n, large)

def sgu_mixer(u, v, w_s, b_s, ln_g, ln_b):
    B, S, _ = u.shape
    nc = S // SGU_CHUNK
    v = layer_norm(v, ln_g, ln_b)
    vg = v.reshape(B, nc, SGU_CHUNK, SGU_GROUPS, SGU_GROUP_DIM)
    causal = jnp.tril(jnp.ones((SGU_CHUNK, SGU_CHUNK), dtype=bool))
    w = jnp.where(causal, w_s, 0).astype(v.dtype)
    mixed = jnp.einsum('gts,bnsgc->bntgc', w, vg) + b_s.T[None, None, :, :, None].astype(v.dtype)
    return u * mixed.reshape(B, S, SGU_WIDTH)

_gather_blocks = jax.vmap(jax.vmap(lambda blocks, idx: blocks[idx]))

def moba_attention(q, k, v, rel_bias):
    B, H, S, dh = q.shape
    nb = S // MOBA_BLOCK
    topk = min(MOBA_TOPK, nb)
    kb = k.reshape(B, H, nb, MOBA_BLOCK, dh)
    vb = v.reshape(B, H, nb, MOBA_BLOCK, dh)
    k_mean = jnp.mean(kb.astype(jnp.float32), axis=3).astype(k.dtype)
    scale = dh ** -0.5
    table = rel_bias.T
    h_idx = jnp.arange(H)[None, :, None, None, None]
    pos_in_block = jnp.arange(MOBA_BLOCK)
    n_chunks = S // Q_CHUNK
    q_chunks = q.reshape(B, H, n_chunks, Q_CHUNK, dh).transpose(2, 0, 1, 3, 4)
    n_sel = topk * MOBA_BLOCK

    def one_chunk(args):
        c, q_c = args
        q_pos = c * Q_CHUNK + jnp.arange(Q_CHUNK)
        own = (c * Q_CHUNK) // MOBA_BLOCK
        gate = jnp.einsum('bhqd,bhnd->bhqn', q_c, k_mean).astype(jnp.float32)
        gate = jnp.where(jnp.arange(nb) < own, gate, -jnp.inf)
        _, sel = lax.top_k(gate, topk)
        sel_valid = sel < own
        k_sel = _gather_blocks(kb, sel)
        v_sel = _gather_blocks(vb, sel)
        s_sel = jnp.einsum('bhqd,bhqkmd->bhqkm', q_c, k_sel).astype(jnp.float32) * scale
        k_pos_sel = sel[..., None] * MOBA_BLOCK + pos_in_block
        dist_sel = q_pos[:, None, None] - k_pos_sel
        s_sel = s_sel + table[h_idx, rel_bucket(dist_sel)].astype(jnp.float32)
        s_sel = jnp.where(sel_valid[..., None], s_sel, -jnp.inf)
        k_own = lax.dynamic_index_in_dim(kb, own, axis=2, keepdims=False)
        v_own = lax.dynamic_index_in_dim(vb, own, axis=2, keepdims=False)
        s_own = jnp.einsum('bhqd,bhmd->bhqm', q_c, k_own).astype(jnp.float32) * scale
        dist_own = q_pos[:, None] - (own * MOBA_BLOCK + pos_in_block)[None, :]
        s_own = s_own + table[:, rel_bucket(dist_own)].astype(jnp.float32)
        s_own = jnp.where(dist_own >= 0, s_own, -jnp.inf)
        s_all = jnp.concatenate([s_sel.reshape(B, H, Q_CHUNK, n_sel), s_own], axis=-1)
        probs = jax.nn.softmax(s_all, axis=-1).astype(v.dtype)
        p_sel = probs[..., :n_sel].reshape(B, H, Q_CHUNK, topk, MOBA_BLOCK)
        p_own = probs[..., n_sel:]
        return (jnp.einsum('bhqkm,bhqkmd->bhqd', p_sel, v_sel)
                + jnp.einsum('bhqm,bhmd->bhqd', p_own, v_own))

    out = lax.map(one_chunk, (jnp.arange(n_chunks), q_chunks))
    return out.transpose(1, 2, 0, 3, 4).reshape(B, H, S, dh)

def second_inputs(seed: int = 0) -> dict:
    key = jax.random.key(seed)
    ks = jax.random.split(key, 20)
    f32 = jnp.float32
    nrm = lambda k, shape, s: jax.random.normal(k, shape, f32) * s
    L = DEPTH
    return {
        "x": nrm(ks[0], (BATCH, SEQ, D_MODEL), 1.0),
        "p": nrm(ks[1], (DEPTH, BATCH, SEQ, PLE_DIM), 1.0),
        "norm_mix_g": 1.0 + nrm(ks[2], (L, D_MODEL), 0.05),
        "w_in": nrm(ks[3], (L, D_MODEL, IN_COLS), D_MODEL ** -0.5),
        "w_sgu_spatial": nrm(ks[4], (L, SGU_GROUPS, SGU_CHUNK, SGU_CHUNK), SGU_CHUNK ** -0.5),
        "b_sgu_spatial": 1.0 + nrm(ks[5], (L, SGU_GROUPS, SGU_CHUNK), 0.1),
        "ln_v_g": 1.0 + nrm(ks[6], (L, SGU_WIDTH), 0.05),
        "ln_v_b": nrm(ks[7], (L, SGU_WIDTH), 0.02),
        "rel_bias": nrm(ks[8], (REL_BUCKETS, ATT_HEADS), 0.5),
        "w_out": nrm(ks[9], (L, D_MODEL, D_MODEL), D_MODEL ** -0.5),
        "norm_ffn_g": 1.0 + nrm(ks[10], (L, D_MODEL), 0.05),
        "w_ff1": nrm(ks[11], (L, D_MODEL, D_FF_2), D_MODEL ** -0.5),
        "w_ff2": nrm(ks[12], (L, D_FF_2, D_MODEL), D_FF_2 ** -0.5),
        "norm_ple_g": 1.0 + nrm(ks[13], (L, D_MODEL), 0.05),
        "w_ple_gate": nrm(ks[14], (L, D_MODEL, D_MODEL), D_MODEL ** -0.5),
        "w_ple_proj": nrm(ks[15], (L, PLE_DIM, D_MODEL), PLE_DIM ** -0.5),
        "norm_final_g": 1.0 + nrm(ks[16], (D_MODEL,), 0.05),
    }

def second_block(x, p, norm_mix_g, w_in, w_sgu_spatial, b_sgu_spatial, ln_v_g, ln_v_b, rel_bias,
              w_out, norm_ffn_g, w_ff1, w_ff2, norm_ple_g, w_ple_gate, w_ple_proj, norm_final_g):
    B, S, _ = x.shape
    offsets = np.cumsum(SPLITS)[:-1].tolist()
    for i in range(DEPTH):
        h = rms_norm(x, norm_mix_g[i])
        proj = h @ w_in[i]
        za_u, za_v, q, k, v_att, g_a, g_b = jnp.split(proj, offsets, axis=-1)
        y_a = sgu_mixer(jax.nn.gelu(za_u), jax.nn.gelu(za_v), w_sgu_spatial[i], b_sgu_spatial[i],
                        ln_v_g[i], ln_v_b[i])
        heads = lambda t: t.reshape(B, S, ATT_HEADS, HEAD_DIM).transpose(0, 2, 1, 3)
        y_b = moba_attention(heads(q), heads(k), heads(v_att), rel_bias)
        y_b = y_b.transpose(0, 2, 1, 3).reshape(B, S, ATT_WIDTH)
        merged = jax.nn.sigmoid(g_a) * y_a + jax.nn.sigmoid(g_b) * y_b
        x = x + merged @ w_out[i]
        h = rms_norm(x, norm_ffn_g[i])
        x = x + jnp.square(jax.nn.relu(h @ w_ff1[i])) @ w_ff2[i]
        gate = jax.nn.sigmoid(rms_norm(x, norm_ple_g[i]) @ w_ple_gate[i])
        x = x + gate * (p[i] @ w_ple_proj[i])
    return rms_norm(x, norm_final_g)


def setup_inputs(seed=0):
    out = dict(first_inputs(seed))
    for name, value in second_inputs(seed + 1).items():
        if name != "x":
            out[name + "_2"] = value
    return out


def reference(
    x, c, ln1_g, ln2_g, w_ada, b_ada, w_in, b_f, fox_qk_g, diff_qk_g, diff_lam, diff_norm_g,
    w_out, w_gate, w_up, w_down, p_2, norm_mix_g_2, w_in_2, w_sgu_spatial_2, b_sgu_spatial_2,
    ln_v_g_2, ln_v_b_2, rel_bias_2, w_out_2, norm_ffn_g_2, w_ff1_2, w_ff2_2, norm_ple_g_2,
    w_ple_gate_2, w_ple_proj_2, norm_final_g_2,
):
    x = first_block(
        x, c, ln1_g, ln2_g, w_ada, b_ada, w_in, b_f, fox_qk_g, diff_qk_g, diff_lam, diff_norm_g,
        w_out, w_gate, w_up, w_down,
    )
    return second_block(
        x, p_2, norm_mix_g_2, w_in_2, w_sgu_spatial_2, b_sgu_spatial_2, ln_v_g_2, ln_v_b_2,
        rel_bias_2, w_out_2, norm_ffn_g_2, w_ff1_2, w_ff2_2, norm_ple_g_2, w_ple_gate_2,
        w_ple_proj_2, norm_final_g_2,
    )


_drawn_inputs = setup_inputs


def setup_inputs(seed=0):
    import zlib

    import numpy as np

    out = dict(_drawn_inputs(seed))
    spreads = {}
    factors = {'ln1_g': 8.0,
     'ln2_g': 8.0,
     'b_f': 8.0,
     'fox_qk_g': 8.0,
     'diff_qk_g': 8.0,
     'diff_lam': 3.128,
     'diff_norm_g': 25.732,
     'ln_v_g_2': 41.912,
     'ln_v_b_2': 64.0,
     'norm_ple_g_2': 200.0,
     'norm_mix_g_2': 8.0,
     'b_sgu_spatial_2': 8.0,
     'rel_bias_2': 27.093,
     'norm_ffn_g_2': 8.0,
     'p_2': 8.0,
     'w_ple_gate_2': 8.0,
     'w_ple_proj_2': 8.0}
    for name, (base, spread) in spreads.items():
        noise = np.random.default_rng([zlib.crc32(name.encode()), seed]).standard_normal(out[name].shape)
        drawn = base * np.exp(spread * noise) if base else spread * noise
        out[name] = __import__('jax').numpy.asarray(drawn.astype(out[name].dtype))
    for name, factor in factors.items():
        out[name] = (out[name] * factor).astype(out[name].dtype)
    return out
```

```python
from contextlib import ExitStack
from math import exp as _exp

import numpy as np

import concourse.bass as bass
from concourse import mybir

F32 = mybir.dt.float32
F32R = mybir.dt.float32r
ALU = mybir.AluOpType
ACT = mybir.ActivationFunctionType
AX = mybir.AxisListType.X

P = 128
D = 1024
S = 256
TB = S // P
KC = D // P
HD = 64
FOX, DIFF, MOBA = 8, 4, 16
W = 512
DFF = 2816
DFF2 = 4096
EPS = 1e-6
MASKED = -1e30
BUCKETS = 32
LAM_INIT = 0.8 - 0.6 * _exp(0.0)
SKEW = 384
RAW, SPL = 4, 3

C_ID, C_MASK, C_ALIBI, C_HOT = 0, 128, 384, 1408
C_ALL = C_HOT + SKEW

V_C, V_LN1, V_LN2, V_MIX, V_FFN, V_PLE, V_BS, V_QK, V_DN = 0, 8, 16, 24, 32, 40, 48, 56, 60
V_ALL = 61

PAIRS = FOX // 2 + DIFF + MOBA // 2
FOX_P, DIFF_P = FOX // 2, DIFF


def kind_of(u):
    return "fox" if u < FOX_P else "diff" if u < FOX_P + DIFF_P else "moba"


def plan():
    tiles, slabs, order = [], [], []

    def tile(name, n, chunks, operand, width=W):
        tiles.append(dict(name=name, n=n, K=chunks, operand=operand, width=width))
        return len(tiles) - 1

    def piece(T, k, slab, off):
        return dict(T=T, k=k, slab=slab, off=off, first=False, last=False)

    def narrow(T, weight, col, k0, width=W):
        s = len(slabs)
        ps = [piece(T, k0 + j, s, j * width) for j in range(4)]
        slabs.append(dict(weight=weight, row=k0 * P, chunks=4, col=col, cols=width))
        ps[0]["first"], ps[-1]["last"] = True, True
        return [("piece", p) for p in ps]

    def wide(Ts, weight, k0):
        s = len(slabs)
        ps = [piece(T, k0 + j, s, j * D + n * W) for j in range(2) for n, T in enumerate(Ts)]
        slabs.append(dict(weight=weight, row=k0 * P, chunks=2, col=0, cols=D))
        ps[0]["first"], ps[-1]["last"] = True, True
        return [("piece", p) for p in ps]

    def whole(name, n, weight, col, operand, width=W):
        T = tile(name, n, KC, operand, width)
        return narrow(T, weight, col, 0, width) + narrow(T, weight, col, 4, width) + [("evac", T)]

    def pair_gemm(name, weight, chunks, operand):
        Ts = [tile(name, n, chunks, operand) for n in range(2)]
        out = []
        for k0 in range(0, chunks, 2):
            out += wide(Ts, weight, k0)
        return out + [("evac", T) for T in Ts]

    def norm(i):
        return [("norm", i), ("turn", ("norm", i, 0)), ("turn", ("norm", i, 1))]

    def attention(us, filler, counts):
        filler = list(filler)

        def fill(n):
            out = []
            while n > 0 and filler:
                it = filler.pop(0)
                out.append(it)
                n -= it[0] in ("piece", "ada")
            while filler and filler[0][0] == "evac":
                out.append(filler.pop(0))
            return out

        out = [("heads", us[0]), ("scores", us[0])] + fill(counts[3])
        for u in us:
            diff = kind_of(u) == "diff"
            out += [("probsT", (u, 0))] + fill(counts[0])
            if not diff:
                out += [("probsT", (u, 1))] + fill(counts[1])
            out += [("values", u)]
            if u != us[-1]:
                out += [("heads", u + 1)]
            out += fill(counts[2])
            if kind_of(u) == "moba":
                out += [("back", u)]
            if u != us[-1]:
                out += [("scores", u + 1)] + fill(counts[3])
        return out + filler

    ada = [("ada", j) for j in range(3 * KC)]

    def with_ada(items, start):
        out = []
        for it in items:
            out.append(it)
            if it[0] == "piece" and it[1]["last"] and start < len(ada):
                out.append(ada[start])
                start += 1
        return out

    order += [("vectors", 0), ("relbias", 0)]
    order += ada[:KC] + [("mod", 0)] + norm(0) + [("fgate", 0)]
    fox_cols = [0, W, 2 * W]
    diff_cols = [3 * W + FOX + n * W for n in range(3)]
    head = []
    for n in range(3):
        head += whole("fox", n, "w_in", fox_cols[n], "h")
    order += with_ada(head, KC)
    tail = []
    for n in range(3):
        tail += whole("diff", n, "w_in", diff_cols[n], "h")
    tail = with_ada(tail, KC + 6)
    order += attention(list(range(FOX_P)), tail, (2, 2, 2, 2))
    wo = [tile("w_out", n, KC, "mix") for n in range(2)]
    fill = narrow(wo[0], "w_out", 0, 0) + narrow(wo[1], "w_out", W, 0)
    fill = fill[:4] + ada[20:22] + fill[4:] + ada[22:24]
    order += attention(list(range(FOX_P, FOX_P + DIFF_P)), fill, (1, 1, 1, 1))
    order += [("diffnorm", 0), ("mod", 1), ("turn", ("diff", 0, 0))]
    order += narrow(wo[0], "w_out", 0, 4) + [("evac", wo[0])]
    order += narrow(wo[1], "w_out", W, 4) + [("evac", wo[1])]
    order += norm(1)
    late = []
    for n in range((DFF + W - 1) // W):
        width = min(W, DFF - n * W)
        now = whole("gate", n, "w_gate", n * W, "h", width) + whole("up", n, "w_up", n * W, "h", width)
        order += now[:4] + late + now[4:]
        late = [("turn", ("hid", n, 0))]
    order += late
    down = pair_gemm("down", "w_down", DFF // P, "hid")
    order += down[:-2] + [("g2row", 0)] + down[-2:]
    order += norm(2) + [("spatial", 0)]
    for n in (0, 1):
        order += whole("v", n, "w_in_2", D + n * W, "h")
    order += [("layernorm", 0)]
    for n in (0, 1):
        order += whole("u", n, "w_in_2", n * W, "h")
    for j, name in enumerate(("q", "k", "vatt")):
        for n in (0, 1):
            order += whole(name, n, "w_in_2", 2 * D + j * D + n * W, "h")
            if (j, n) == (0, 1):
                order += [("sgu", 0), ("sgu", 1)]
    gates = []
    for j, name in enumerate(("ga", "gb")):
        for n in (0, 1):
            gates += whole(name, n, "w_in_2", 5 * D + j * D + n * W, "h")
    order += attention(list(range(FOX_P + DIFF_P, PAIRS)), gates, (1, 1, 1, 1))
    order += [("merge", 0), ("turn", ("merge", 0, 0)), ("merge", 1), ("turn", ("merge", 1, 0))]
    order += pair_gemm("w_out2", "w_out_2", KC, "h")
    order += norm(3)
    late = []
    for n in range(DFF2 // W):
        now = whole("ff1", n, "w_ff1_2", n * W, "h")
        order += now[:4] + late + now[4:]
        late = [("turn", ("hid2", n, 0))]
    order += late
    order += pair_gemm("ff2", "w_ff2_2", DFF2 // P, "hid")
    order += [("pT", 0)] + norm(4)[:1] + pair_gemm("ple_proj", "w_ple_proj_2", 2, "p") + norm(4)[1:]
    order += pair_gemm("ple", "w_ple_gate_2", KC, "h")
    order += [("final", 0)]

    out, split = [], 0
    for it in order:
        if it[0] == "piece" and it[1]["first"]:
            while split <= min(it[1]["slab"] + 2, len(slabs) - 1):
                out.append(("split", split))
                split += 1
        out.append(it)
    turn = 0
    turns = {}
    for it in out:
        if it[0] == "turn":
            turns[it[1]] = turn
            turn += 1
    return tiles, slabs, out, turns


TILES, SLABS, ORDER, TURNS = plan()
STREAM = [it for it in ORDER if it[0] in ("split", "ada")]
STREAM_AT = {it: n for n, it in enumerate(STREAM)}


def spread(ap, n):
    return bass.AP(tensor=ap.tensor, offset=ap.offset, ap=[list(d) for d in ap.ap] + [[0, n]])


def backwards(ap):
    d = [list(x) for x in ap.ap]
    step, n = d[-1]
    return bass.AP(tensor=ap.tensor, offset=ap.offset + step * (n - 1), ap=d[:-1] + [[-step, n]])


def twice(ap):
    d = [list(d) for d in ap.ap]
    return bass.AP(tensor=ap.tensor, offset=ap.offset, ap=[d[0], [0, TB], d[1]])


def slabs_before(step, operand):
    n = 0
    for it in ORDER:
        if it == step:
            return n
        if it[0] == "piece" and it[1]["last"] and TILES[it[1]["T"]]["operand"] == operand:
            n = it[1]["slab"] + 1
    raise ValueError(step)


def turned_head(u, i):
    k = kind_of(u)
    if k == "fox":
        return 2 * u + i
    if k == "diff":
        return FOX + u - FOX_P
    return FOX + DIFF + 2 * (u - FOX_P - DIFF_P) + i


def pair_of_turned(j):
    if j < FOX:
        return j // 2
    if j < FOX + DIFF:
        return FOX_P + j - FOX
    return FOX_P + DIFF_P + (j - FOX - DIFF) // 2


def build(nc, A, out):
    ctx = ExitStack()
    with ctx:
        def sem(name):
            return ctx.enter_context(nc.semaphore(name))

        def sb(name, shape, dt=F32, where=None):
            return (where or ctx).enter_context(nc.sbuf_tensor(name, shape, dt))

        PS = ctx.enter_context(nc.psum_tensor("PS", [P, 8, W], F32))
        skew = nc.dram_tensor("skew_dram", [MOBA, SKEW], F32, kind="Internal")

        raw = sb("raw", [P, RAW, 4 * W])
        whi = sb("whi", [P, SPL, 4 * W], F32R)
        wlo = sb("wlo", [P, SPL, 4 * W], F32R)
        hT = sb("hT", [P, 2, KC, S], F32R)
        qT = sb("qT", [P, 2, 2, 2, S], F32R)
        kT = sb("kT", [P, 2, 2, S], F32R)
        x = sb("x", [P, TB, D])
        con = sb("con", [P, C_ALIBI])
        identr = sb("identr", [P, P], F32R)
        col = sb("col", [P, V_ALL + 3])
        lam = sb("lam", [P, 6])
        expo = sb("expo", [P, 16])
        mod = sb("mod", [P, 3, W])
        nmax = sb("nmax", [P, 2 * PAIRS, TB])
        lsum = sb("lsum", [P, 2 * PAIRS, TB])
        rinv = sb("rinv", [P, 2 * PAIRS, TB])
        nss = sb("nss", [P, 6, TB])
        nrs = sb("nrs", [P, 6, TB])
        ident = con[:, C_ID:C_ID + P]
        mask = con[:, C_MASK:C_MASK + 2 * P]

        g = ExitStack()
        tok1 = sb("tok1", [P, 6, TB, W], F32, g)
        sq = sb("sq", [P, TB, W], F32, g)
        mixT = sb("mixT", [P, 2, KC, S], F32R, g)
        alibi = sb("alibi", [P, DIFF, 2 * P], F32, g)
        AB = sb("AB", [P, 4, KC], F32, g)
        wfg = sb("wfg", [P, KC, FOX], F32, g)
        wfgs = sb("wfgs", [P, 2, KC, FOX], F32R, g)
        bf = sb("bf", [FOX, 1], F32, g)
        fgt = sb("fgt", [FOX, 4, S], F32, g)
        ones = sb("ones", [FOX, S], F32, g)
        cumq = sb("cumq", [P, TB, FOX], F32, g)
        ncum = sb("ncum", [P, 2, S], F32R, g)
        hss = sb("hss", [P, 4, TB * 8], F32, g)
        hrs = sb("hrs", [P, 4, TB * 8], F32, g)
        dss = sb("dss", [P, TB * DIFF], F32, g)
        drs = sb("drs", [P, TB * DIFF], F32, g)
        g1row = tok1[:, 0].rearrange("p t w -> p (t w)")
        gg = ExitStack()
        vec = sb("vec", [V_ALL, P], F32, gg)
        lamb = sb("lamb", [P, 4, HD], F32, gg)
        lprod = sb("lprod", [P, 2, HD], F32, gg)
        cond = sb("cond", [P, 2, KC], F32, gg)
        cond32 = sb("cond32", [P, KC, 32], F32, gg)
        hot = sb("hot", [BUCKETS + 1, SKEW], F32, gg)
        table = sb("table", [BUCKETS + 1, MOBA], F32, gg)
        relrow = sb("relrow", [MOBA, SKEW], F32, gg)
        gg.close()
        gg = ExitStack()
        _ = sb("setup_space", [P, 2048], F32, gg)
        xn1 = sb("xn1", [P, TB, D], F32, gg)
        aff1 = sb("aff1", [P, 4, S], F32, gg)
        gg.close()
        gg = ExitStack()
        _2 = sb("cond_space", [P, 2048], F32, gg)
        sc1 = sb("sc1", [P, 2, 3 * P], F32, gg)
        pt1 = sb("pt1", [P, 2, 3 * P], F32, gg)
        od = sb("od", [P, TB, W], F32, gg)
        mcum = sb("mcum", [P, 2, 3 * P], F32, gg)
        gg.close()
        g.close()

        g = ExitStack()
        hidT1 = sb("hidT1", [P, 2, DFF // P, S], F32R, g)
        hid1 = sb("hid1", [P, 2, TB, W], F32, g)
        th1 = sb("th1", [P, TB, W], F32, g)
        xnb = sb("xnb", [P, TB, D], F32, g)
        affb = sb("affb", [P, 4, S], F32, g)
        g2row = sb("g2row", [P, D], F32, g)
        tmpb = affb[:, :, :].rearrange("p c s -> p (c s)").rearrange("p (t w) -> p t w", t=TB)
        g.close()

        g = ExitStack()
        tok2 = sb("tok2", [P, 3, TB, D], F32, g)
        ub = sb("ub", [P, TB, D], F32, g)
        vb = sb("vb", [P, TB, D], F32, g)
        toep = sb("toep", [P, MOBA, 2 * P], F32, g)
        sc2 = sb("sc2", [P, 2, 3 * P], F32, g)
        pt2 = sb("pt2", [P, 2, 3 * P], F32, g)
        wsT = sb("wsT", [P, 8, P], F32, g)
        ws = sb("ws", [P, 8, P], F32, g)
        th2 = ws[:, :, :].rearrange("p g s -> p (g s)").rearrange("p (t w) -> p t w", t=TB)
        ybT = sb("ybT", [P, S], F32, g)
        bn = sb("bn", [P, TB, 2, 6], F32, g)
        mv = sb("mv", [P, TB, 2], F32, g)
        vrs = sb("vrs", [P, TB], F32, g)
        xn2 = tok2[:, 0]
        lngb = toep[:, 0:8, :].rearrange("p h k -> p (h k)").rearrange("p (a d) -> p a d", a=2)
        g.close()

        g = ExitStack()
        hid2 = sb("hid2", [P, 2, TB, W], F32, g)
        xnc = sb("xnc", [P, TB, D], F32, g)
        gg = ExitStack()
        hidT2 = sb("hidT2", [P, 2, DFF2 // P, S], F32R, gg)
        gg.close()
        pp = sb("pp", [P, TB, D], F32, g)
        pin = sb("pin", [P, TB, 2 * P], F32, g)
        pT = sb("pT", [P, 2, 2, S], F32R, g)
        gfin = sb("gfin", [P, D], F32, g)
        fin = sb("fin", [P, TB, D], F32, g)
        thp = sb("thp", [P, 2, TB, W], F32, g)
        g.close()

        raw_in = [sem(f"raw_in{i}") for i in range(RAW)]
        hi_made, lo_made = sem("hi_made"), sem("lo_made")
        ada_used = sem("ada_used")
        gemm_done = sem("gemm_done")
        tile_done = sem("tile_done")
        tile_free = [sem("tile_free0"), sem("tile_free1")]
        vec_in, x_in, setup_in = sem("vec_in"), sem("x_in"), sem("setup_in")
        vec_ps, col_made, cond_th, cond_made = sem("vec_ps"), sem("col_made"), sem("cond_th"), sem("cond_made")
        zeroed, expo_made, ident_made = sem("zeroed"), sem("expo_made"), sem("ident_made")
        rel_ps, rel_row, rel_out, rel_in = sem("rel_ps"), sem("rel_row"), sem("rel_out"), sem("rel_in")
        table_set, lam_sum, lam_exp, lam_made = sem("table_set"), sem("lam_sum"), sem("lam_exp"), sem("lam_made")
        mod_in, mod_T, ab_made = sem("mod_in"), sem("mod_T"), sem("ab_made")
        g_ps, g1_row, g2_row = sem("g_ps"), sem("g1_row"), sem("g2_row")
        sum_act, sum_dve, norm_rs = sem("sum_act"), sem("sum_dve"), sem("norm_rs")
        xn_act, xn_dve = sem("xn_act"), sem("xn_dve")
        turned, turn_aff, turn_hi, turn_lo = sem("turned"), sem("turn_aff"), sem("turn_hi"), sem("turn_lo")
        wfg_hi, wfg_lo = sem("wfg_hi"), sem("wfg_lo")
        fg_ps, fg_abs, fg_log = sem("fg_ps"), sem("fg_abs"), sem("fg_log")
        cum_made, ncum_hi, ncum_lo, cumq_ps, cumq_in = (
            sem("cum_made"), sem("ncum_hi"), sem("ncum_lo"), sem("cumq_ps"), sem("cumq_in"))
        tok_in, sq_in, hss_in, qk_ready = sem("tok_in"), sem("sq_in"), sem("hss_in"), sem("qk_ready")
        heads_ps, heads_hi, heads_lo = sem("heads_ps"), sem("heads_hi"), sem("heads_lo")
        mcum_in, score_ps, smax, exp_done = sem("mcum_in"), sem("score_ps"), sem("smax"), sem("exp_done")
        fox_p, diff_p, inv_made = sem("fox_p"), sem("diff_p"), sem("inv_made")
        probs_ps, probs_sb, value_ps = sem("probs_ps"), sem("probs_sb"), sem("value_ps")
        mix_hi, mix_lo, od_in, dsq_in = sem("mix_hi"), sem("mix_lo"), sem("od_in"), sem("dsq_in")
        drs_made, od_made = sem("drs_made"), sem("od_made")
        ybT_in, back_ps, yb_in = sem("ybT_in"), sem("back_ps"), sem("yb_in")
        x_done, th_in, hid_in = sem("x_done"), sem("th_in"), sem("hid_in")
        tok2_in, v_in, u_in, r_in = sem("tok2_in"), sem("v_in"), sem("u_in"), sem("r_in")
        ws_in, ws_low, ws_ps, ws_T = sem("ws_in"), sem("ws_low"), sem("ws_ps"), sem("ws_T")
        ln_in, mv_made, vrs_made, vc_made, vn_made = (
            sem("ln_in"), sem("mv_made"), sem("vrs_made"), sem("vc_made"), sem("vn_made"))
        sgu_ps, ya_in, ga_in, gb_in, merged = sem("sgu_ps"), sem("ya_in"), sem("ga_in"), sem("gb_in"), sem("merged")
        p_in, p_ps, p_hi, p_lo, pp_in, gfin_in = (
            sem("p_in"), sem("p_ps"), sem("p_hi"), sem("p_lo"), sem("pp_in"), sem("gfin_in"))
        out_made, out_done = sem("out_made"), sem("out_done")
        act_step, dve_step, pool_step = sem("act_step"), sem("dve_step"), sem("pool_step")

        def slab_view(t, slot, s):
            m = SLABS[s]
            return t[:, slot, 0:m["chunks"] * m["cols"]]

        def landed(eng, it):
            n = STREAM_AT[it]
            eng.wait_ge(raw_in[n % RAW], 16 * (n // RAW + 1))
            return n % RAW

        def bank0(T):
            return 2 * (T % 2)

        def tile_ps(T):
            return PS[:, bank0(T):bank0(T) + TB, 0:TILES[T]["width"]]

        def turn_banks(q):
            return 4 + 2 * (q % 2)

        def turn_of(key):
            kind, n, h = key
            if kind == "norm":
                src = (xn1, xnb, xn2, xnc, xnc)[n]
                src = src[:, :, h * W:(h + 1) * W]
                return src, ((xn_act, n + 1), (xn_dve, n + 1)), hT, 4 * h, 4
            if kind == "diff":
                return od[:, :, :], ((od_made, 1),), mixT, 4, 4
            if kind == "merge":
                return tok2[:, 0, :, n * W:(n + 1) * W], ((merged, n + 1),), hT, 4 * n, 4
            if kind == "hid":
                chunks = min(4, DFF // P - 4 * n)
                return hid1[:, n % 2, :, 0:chunks * P], ((hid_in, n + 1),), hidT1, 4 * n, chunks
            return hid2[:, n % 2], ((hid_in, 6 + n + 1),), hidT2, 4 * n, 4

        def gain_of(key, c):
            kind, n, h = key
            if kind == "norm" and n >= 2:
                v = (V_MIX, V_FFN, V_PLE)[n - 2] + 4 * h + c
                return col[:, v:v + 1]
            if kind == "diff":
                return col[:, V_ALL + 2:V_ALL + 3]
            return 0.5 if kind == "merge" else None

        def heads_of(u):
            k = kind_of(u)
            if k == "moba":
                c = (u - FOX_P - DIFF_P) * P
                return tok2[:, 0, :, c:c + P], tok2[:, 1, :, c:c + P], 0.125, 1.0, (tok2_in, 6)
            j = 0 if k == "fox" else 3
            c = (u if k == "fox" else u - FOX_P) * P
            gq, gk = (V_ALL, V_QK + 1) if k == "fox" else (V_ALL + 1, V_QK + 3)
            return (tok1[:, j, :, c:c + P], tok1[:, j + 1, :, c:c + P],
                    col[:, gq:gq + 1], col[:, gk:gk + 1], (qk_ready, 2 if k == "fox" else 4))

        def scores_sb(u):
            return sc2 if kind_of(u) == "moba" else sc1

        def probs_T(u):
            return pt2 if kind_of(u) == "moba" else pt1

        NSETUP = 9
        QB = ((0, P), (P, 3 * P))

        block = ctx.enter_context(nc.Block())

        @block.sync
        def _(sp):
            for n, rows, v in (("c", 8, V_C), ("ln1_g", 8, V_LN1), ("ln2_g", 8, V_LN2),
                               ("norm_mix_g_2", 8, V_MIX), ("norm_ffn_g_2", 8, V_FFN),
                               ("norm_ple_g_2", 8, V_PLE), ("b_sgu_spatial_2", 8, V_BS)):
                src = A[n].rearrange("a b c -> (a b c)") if len(A[n].shape) == 3 else A[n].rearrange("a b -> (a b)")
                sp.dma_start(vec[v:v + rows, :], src.rearrange("(r q) -> r q", q=P)).then_inc(vec_in, 16)
            sp.dma_start(con[:, :], A["constants"][:, 0:C_ALIBI]).then_inc(vec_in, 16)
            for n, it in enumerate(STREAM):
                if n >= RAW:
                    kind, i = STREAM[n - RAW]
                    if kind == "ada":
                        sp.wait_ge(ada_used, i + 1)
                    else:
                        sp.wait_ge(lo_made, i + 1)
                if it[0] == "ada":
                    pack, k = divmod(it[1], KC)
                    src = A["w_ada"][0, k * P:(k + 1) * P, pack * 4 * W:(pack + 1) * 4 * W]
                    dst = raw[:, n % RAW, :]
                else:
                    m = SLABS[it[1]]
                    src = A[m["weight"]][0, m["row"]:m["row"] + m["chunks"] * P,
                                         m["col"]:m["col"] + m["cols"]].rearrange("(c p) n -> p c n", p=P)
                    dst = slab_view(raw, n % RAW, it[1]).rearrange("p (c n) -> p c n", c=m["chunks"])
                sp.dma_start(dst, src).then_inc(raw_in[n % RAW], 16)
            for t in range(TB):
                sp.wait_ge(out_made, t + 1)
                sp.dma_start(out[0, t * P:(t + 1) * P, :], fin[:, t, :]).then_inc(out_done, 16)
            sp.wait_ge(out_done, 16 * TB)

        @block.tensor
        def _(pe):
            reader = {}

            def take(*banks):
                for b in banks:
                    for s, v in reader.pop(b, ()):
                        pe.wait_ge(s, v)

            def products(out_ap, pairs):
                for n, (a, b) in enumerate(pairs):
                    last = pe.matmul(out_ap, a, b, start=(n == 0), stop=(n == len(pairs) - 1))
                return last

            def operand_ready(T, k):
                name = TILES[T]["operand"]
                if name == "mix":
                    if k < 4:
                        pe.wait_ge(mix_lo, k + 1)
                    else:
                        pe.wait_ge(turn_lo, TURNS[("diff", 0, 0)] + 1)
                elif name == "p":
                    pe.wait_ge(p_lo, 1)
                elif name == "hid":
                    kind = "hid" if TILES[T]["K"] == DFF // P else "hid2"
                    pe.wait_ge(turn_lo, TURNS[(kind, k // 4, 0)] + 1)
                else:
                    tn = TILES[T]["name"]
                    key = {"fox": ("norm", 0), "diff": ("norm", 0), "gate": ("norm", 1), "up": ("norm", 1),
                           "w_out2": ("merge",), "ff1": ("norm", 3), "ple": ("norm", 4)}.get(tn, ("norm", 2))
                    key = ("merge", k // 4, 0) if key == ("merge",) else (*key, k // 4)
                    pe.wait_ge(turn_lo, TURNS[key] + 1)

            def operand(T, k, t):
                name = TILES[T]["operand"]
                big = hidT1 if TILES[T]["K"] == DFF // P else hidT2
                src = {"h": hT, "mix": mixT, "p": pT, "hid": big}[name]
                return src[:, 0, k, t * P:(t + 1) * P], src[:, 1, k, t * P:(t + 1) * P]

            for it in ORDER:
                kind, i = it
                if kind == "piece":
                    T, k, s, off = i["T"], i["k"], i["slab"], i["off"]
                    width = TILES[T]["width"]
                    if i["first"]:
                        pe.wait_ge(hi_made, s + 1)
                        pe.wait_ge(lo_made, s + 1)
                    if k == 0 and T >= 2:
                        pe.wait_ge(tile_free[T % 2], T // 2)
                    operand_ready(T, k)
                    wh = whi[:, s % SPL, off:off + width]
                    wl = wlo[:, s % SPL, off:off + width]
                    for t in range(TB):
                        ah, al = operand(T, k, t)
                        o = PS[:, bank0(T) + t, 0:width]
                        end = k == TILES[T]["K"] - 1
                        pe.matmul(o, ah, wh, start=(k == 0), stop=False)
                        pe.matmul(o, ah, wl, start=False, stop=False)
                        last = pe.matmul(o, al, wh, start=False, stop=end)
                    if i["last"]:
                        last.then_inc(gemm_done, 1)
                    if end:
                        if i["last"]:
                            pe.wait_ge(gemm_done, s + 1)
                            pe.sem_inc(tile_done, 1)
                        else:
                            last.then_inc(tile_done, 1)

                elif kind == "vectors":
                    pe.wait_ge(vec_in, 16 * 8)
                    pe.wait_ge(setup_in, 16 * NSETUP)
                    pe.transpose(PS[:, 4, 0:V_ALL], vec[:, :], ident[0:V_ALL, 0:V_ALL]).then_inc(vec_ps, 1)

                elif kind == "relbias":
                    pe.wait_ge(table_set, 1)
                    pe.matmul(PS[0:MOBA, 5, 0:SKEW], table[:, :], hot[:, :], start=True, stop=True).then_inc(rel_ps, 1)
                    reader[4] = [(col_made, 1)]
                    reader[5] = [(rel_row, 1)]

                elif kind == "ada":
                    pack, k = divmod(i, KC)
                    if i == 0:
                        pe.wait_ge(cond_made, 1)
                    if k == 0 and pack >= 1:
                        pe.wait_ge(mod_in, pack)
                    slot = landed(pe, it)
                    for j in range(4):
                        last = pe.matmul(PS[32 * j:32 * j + 32, 7, :], cond32[:, k, :],
                                         raw[:, slot, j * W:(j + 1) * W], start=(k == 0), stop=(k == KC - 1))
                    last.then_inc(ada_used, 1)
                    if k == KC - 1:
                        reader[7] = [(mod_in, pack + 1)]

                elif kind == "mod":
                    packs = (0,) if i == 0 else (1, 2)
                    for n, pk in enumerate(packs):
                        pe.wait_ge(mod_in, pk + 1)
                        take(4 + n)
                        for c in range(4):
                            last = pe.transpose(PS[:, 4 + n, c * P:(c + 1) * P], mod[:, pk, c * P:(c + 1) * P], ident)
                    last.then_inc(mod_T, 1)
                    reader[4] = [(ab_made, 1 + i)]
                    reader[5] = reader.get(5, []) if i == 0 else [(ab_made, 2)]
                    if i == 1:
                        take(6, 7)
                        for j in range(2):
                            last = pe.matmul(PS[:, 6 + j, :], ident[:, 32 * j:32 * j + 1].to_broadcast([P, P]),
                                             mod[:, 1, :], start=True, stop=True)
                        last.then_inc(g_ps, 1)
                        reader[6] = reader[7] = [(g1_row, 1)]

                elif kind == "g2row":
                    take(4, 5)
                    for j in range(2):
                        last = pe.matmul(PS[:, 4 + j, :], ident[:, 32 * (2 + j):32 * (2 + j) + 1].to_broadcast([P, P]),
                                         mod[:, 2, :], start=True, stop=True)
                    last.then_inc(g_ps, 1)
                    reader[4] = reader[5] = [(g2_row, 1)]

                elif kind == "turn":
                    q = TURNS[i]
                    src, ready, _, _, chunks = turn_of(i)
                    b = turn_banks(q)
                    take(b, b + 1)
                    for s, v in ready:
                        pe.wait_ge(s, v)
                    for c in range(chunks):
                        for t in range(TB):
                            o = (c % 2) * S + t * P
                            last = pe.transpose(PS[:, b + c // 2, o:o + P], src[:, t, c * P:(c + 1) * P], ident)
                    last.then_inc(turned, 1)
                    reader[b] = reader[b + 1] = [(turn_lo, q + 1)]

                elif kind == "fgate":
                    pe.wait_ge(wfg_lo, 1)
                    pe.wait_ge(turn_lo, TURNS[("norm", 0, 1)] + 1)
                    take(4)
                    group = []
                    for k in range(KC):
                        wh, wl = wfgs[:, 0, k, :], wfgs[:, 1, k, :]
                        group += [(wh, hT[:, 0, k, :]), (wl, hT[:, 0, k, :]), (wh, hT[:, 1, k, :])]
                    products(PS[0:FOX, 4, 0:S], group).then_inc(fg_ps, 1)
                    take(5)
                    pe.wait_ge(cum_made, 1)
                    for t in range(TB):
                        last = pe.transpose(PS[:, 5, t * FOX:(t + 1) * FOX], fgt[:, 3, t * P:(t + 1) * P],
                                            ident[0:FOX, 0:FOX])
                    last.then_inc(cumq_ps, 1)
                    reader[4] = [(cum_made, 1)]
                    reader[5] = [(cumq_in, 1)]

                elif kind == "heads":
                    q, k, _, _, ready = heads_of(i)
                    take(4)
                    pe.wait_ge(*ready)
                    for n, src in enumerate((q, k)):
                        for t in range(TB):
                            last = pe.transpose(PS[:, 4, n * S + t * P:n * S + (t + 1) * P], src[:, t, :], ident)
                    last.then_inc(heads_ps, 1)
                    reader[4] = [(heads_lo, i + 1)]

                elif kind == "scores":
                    u, slot = i, i % 2
                    pe.wait_ge(heads_lo, u + 1)
                    if u == 0:
                        pe.wait_ge(zeroed, 2)
                        pe.wait_ge(ncum_lo, 1)
                    for n in range(2):
                        take(5 + n)
                        for t, (c0, c1) in enumerate(QB):
                            qh, ql = (qT[:, slot, part, n, t * P:(t + 1) * P] for part in range(2))
                            kh, kl = (kT[:, slot, part, 0:c1 - c0] for part in range(2))
                            group = [(qh, kh), (qh, kl), (ql, kh)]
                            if kind_of(u) == "fox":
                                pick = identr[:, 2 * u + n:2 * u + n + 1].to_broadcast([P, P])
                                group += [(pick, ncum[:, part, 0:c1 - c0]) for part in range(2)]
                            last = products(PS[:, 5 + n, c0:c1], group)
                        last.then_inc(score_ps, 1)
                        reader[5 + n] = [(smax, 2 * (2 * u + n) + 2)]

                elif kind == "probsT":
                    u, n = i
                    j = turned_head(u, n)
                    a = 2 * u + n
                    if kind_of(u) == "fox":
                        pe.wait_ge(fox_p, a + 1)
                    elif kind_of(u) == "diff":
                        pe.wait_ge(diff_p, u - FOX_P + 1)
                    else:
                        pe.wait_ge(exp_done, 2 * a + 2)
                    take(4)
                    src = scores_sb(u)
                    for m, c in enumerate((0, P, 2 * P)):
                        last = pe.transpose(PS[:, 4, m * P:(m + 1) * P], src[:, n, c:c + P], ident)
                    last.then_inc(probs_ps, 1)
                    reader[4] = [(probs_sb, j + 1)]

                elif kind == "values":
                    u, kd = i, kind_of(i)
                    pt = probs_T(u)
                    take(5)
                    if kd == "diff":
                        j = turned_head(u, 0)
                        pe.wait_ge(probs_sb, j + 1)
                        pe.wait_ge(tok_in, 6)
                        c = (u - FOX_P) * P
                        v = tok1[:, 5, :, c:c + P]
                        products(PS[:, 5, 0:P], [(pt[:, j % 2, 0:P], v[:, 0, :])])
                        last = products(PS[:, 5, P:2 * P], [(pt[:, j % 2, P:2 * P], v[:, 0, :]),
                                                            (pt[:, j % 2, 2 * P:3 * P], v[:, 1, :])])
                        reader[5] = [(dsq_in, u - FOX_P + 1)]
                    else:
                        for n in range(2):
                            j = turned_head(u, n)
                            pe.wait_ge(probs_sb, j + 1)
                            if kd == "fox":
                                pe.wait_ge(tok_in, 3)
                                v = tok1[:, 2, :, u * P + n * HD:u * P + (n + 1) * HD]
                            else:
                                pe.wait_ge(tok2_in, 6)
                                c = (u - FOX_P - DIFF_P) * P + n * HD
                                v = tok2[:, 2, :, c:c + HD]
                            o = PS[n * HD:(n + 1) * HD, 5, 0:S]
                            pe.matmul(o, v[:, 0, :], pt[:, j % 2, 0:S], start=True, stop=False)
                            last = pe.matmul(o[:, P:S], v[:, 1, :], pt[:, j % 2, S:S + P], start=False, stop=True)
                        reader[5] = [(mix_lo, u + 1)] if kd == "fox" else [(ybT_in, u - FOX_P - DIFF_P + 1)]
                    last.then_inc(value_ps, 1)

                elif kind == "back":
                    m = i - FOX_P - DIFF_P
                    take(4)
                    pe.wait_ge(ybT_in, m + 1)
                    for t in range(TB):
                        last = pe.transpose(PS[:, 4, t * P:(t + 1) * P], ybT[:, t * P:(t + 1) * P], ident)
                    last.then_inc(back_ps, 1)
                    reader[4] = [(yb_in, m + 1)]

                elif kind == "spatial":
                    pe.wait_ge(ws_low, 1)
                    take(4, 5)
                    for gr in range(8):
                        last = pe.transpose(PS[:, 4 + gr // 4, (gr % 4) * P:(gr % 4 + 1) * P], ws[:, gr, :], ident)
                    last.then_inc(ws_ps, 1)
                    reader[4] = reader[5] = [(ws_T, 1)]

                elif kind == "sgu":
                    b = 4 + 2 * i
                    take(b, b + 1)
                    pe.wait_ge(vn_made, TB)
                    pe.wait_ge(ws_T, 1)
                    for gr in range(4 * i, 4 * i + 4):
                        o = (gr % 2) * S
                        last = pe.matmul(PS[:, b + gr % 4 // 2, o:o + S].rearrange("p (t c) -> p t c", t=TB),
                                         wsT[:, gr, :], vb[:, :, gr * P:(gr + 1) * P], start=True, stop=True)
                    last.then_inc(sgu_ps, 1)
                    reader[b] = reader[b + 1] = [(ya_in, i + 1)]

                elif kind == "pT":
                    pe.wait_ge(p_in, 16)
                    take(4)
                    for c in range(2):
                        for t in range(TB):
                            last = pe.transpose(PS[:, 4, c * S + t * P:c * S + (t + 1) * P],
                                                pin[:, t, c * P:(c + 1) * P], ident)
                    last.then_inc(p_ps, 1)
                    reader[4] = [(p_lo, 1)]

        @block.scalar
        def _(act):
            own = 0
            act.dma_start(x[:, :, :], A["x"][0].rearrange("(t p) d -> p t d", p=P)).then_inc(x_in, 16)
            for n, r in (("fox_qk_g", V_QK), ("diff_qk_g", V_QK + 2)):
                for h in range(2):
                    act.dma_start(vec[r:r + 2, h * HD:(h + 1) * HD], A[n][0]).then_inc(setup_in, 16)
            act.dma_start(vec[V_DN:V_DN + 1, :], A["diff_norm_g"]).then_inc(setup_in, 16)
            act.dma_start(lamb[:, :, :], A["diff_lam"].to_broadcast([P, 4, HD])).then_inc(setup_in, 16)
            act.dma_start(hot[:, :], A["constants"][0:BUCKETS + 1, C_HOT:C_ALL]).then_inc(setup_in, 16)
            act.dma_start(table[0:BUCKETS, :], A["rel_bias_2"]).then_inc(setup_in, 16)
            act.dma_start(bf[:, :], A["b_f"].rearrange("a h -> h a")).then_inc(setup_in, 16)
            for j in range(4):
                bias = A["b_ada"]
                act.dma_start(mod[32 * j:32 * j + 32, :, :],
                              bass.AP(tensor=bias.tensor, offset=bias.offset + j * W, ap=[[0, 32], [4 * W, 3], [1, W]])
                              ).then_inc(lam_sum, 16)
            act.dma_start(wfg[:, :, :], A["w_in"][0, :, 3 * W:3 * W + FOX].rearrange("(c p) h -> p c h", p=P)
                          ).then_inc(wfg_hi, 16)
            act.dma_start(alibi[:, :, :], A["constants"][:, C_ALIBI:C_HOT].rearrange("p (h k) -> p h k", h=DIFF)
                          ).then_inc(wfg_hi, 16)

            for it in ORDER:
                kind, i = it
                if kind == "split":
                    slot = landed(act, it)
                    if i >= SPL:
                        act.wait_ge(gemm_done, i - SPL + 1)
                    act.activation(slab_view(whi, i % SPL, i), slab_view(raw, slot, i), ACT.Copy).then_inc(hi_made, 1)

                elif kind == "vectors":
                    act.wait_ge(ident_made, 1)
                    act.wait_ge(col_made, 1)
                    act.activation(cond[:, 0, :], col[:, V_C:V_C + KC], ACT.Tanh, scale=0.5).then_inc(cond_th, 1)
                    act.wait_ge(lam_exp, 1)
                    act.activation(lam[:, 2:4], lam[:, 0:2], ACT.Exp).then_inc(lam_exp, 1)
                    act.wait_ge(wfg_hi, 32)
                    act.activation(wfgs[:, 0], wfg[:, :, :], ACT.Copy).then_inc(wfg_lo, 1)

                elif kind == "mod" and i == 1:
                    act.wait_ge(g_ps, 1)
                    act.activation(g1row.rearrange("p (j w) -> p j w", j=2), PS[:, 6:8, :], ACT.Copy).then_inc(g1_row, 1)

                elif kind == "g2row":
                    act.wait_ge(g_ps, 2)
                    act.activation(g2row[:, :].rearrange("p (j w) -> p j w", j=2), PS[:, 4:6, :], ACT.Copy
                                   ).then_inc(g2_row, 1)

                elif kind in ("norm", "final"):
                    n = 5 if kind == "final" else i
                    xn = (xn1, xnb, xn2, xnc, xnc, fin)[n]
                    if n == 0:
                        act.wait_ge(x_in, 16)
                    else:
                        act.wait_ge(x_done, 2 * n)
                    if n == 1:
                        act.wait_ge(rel_out, 16)
                    act.activation(xn[:, 0, :], x[:, 0, :], ACT.Square, accum_out=nss[:, n, 0:1]).then_inc(sum_act, 1)
                    if kind == "norm":
                        act.wait_ge(norm_rs, n + 1)
                        act.activation(xn[:, 0, :], x[:, 0, :], ACT.Copy, scale=nrs[:, n, 0:1]).then_inc(xn_act, 1)

                elif kind == "turn":
                    q = TURNS[i]
                    _, _, dst, c0, chunks = turn_of(i)
                    b = turn_banks(q)
                    name = {"diff": "mix"}.get(i[0], "h" if i[0] in ("norm", "merge") else "hid")
                    if name == "h" and slabs_before(it, "h"):
                        act.wait_ge(gemm_done, slabs_before(it, "h"))
                    ps = PS[:, b:b + chunks // 2, :]
                    to = dst[:, 0, c0:c0 + chunks, :].rearrange("p (a c) s -> p a (c s)", c=2)
                    if i[0] == "norm" and i[1] < 2:
                        act.wait_ge(turn_aff, q_affine(i) + 1)
                        aff = aff1 if i[1] == 0 else affb
                        act.activation(dst[:, 0, c0:c0 + 4, :], aff[:, :, :], ACT.Copy).then_inc(turn_hi, 1)
                    else:
                        act.wait_ge(turned, q + 1)
                        gain = gain_of(i, 0)
                        if gain is None or isinstance(gain, float):
                            act.activation(to, ps, ACT.Copy, scale=1.0 if gain is None else gain).then_inc(turn_hi, 1)
                        else:
                            for c in range(chunks):
                                last = act.activation(dst[:, 0, c0 + c, :], PS[:, b + c // 2, c % 2 * S:(c % 2 + 1) * S],
                                                      ACT.Copy, scale=gain_of(i, c))
                            last.then_inc(turn_hi, 1)

                elif kind == "fgate":
                    act.wait_ge(fg_abs, 2)
                    act.activation(fgt[:, 1, :], fgt[:, 1, :], ACT.Exp).then_inc(act_step, 1)
                    own += 1
                    act.wait_ge(act_step, own)
                    act.activation(fgt[:, 1, :], fgt[:, 1, :], ACT.Ln, bias=1.0).then_inc(fg_log, 1)
                    act.wait_ge(cum_made, 1)
                    act.wait_ge(zeroed, 2)
                    act.activation(ncum[0:FOX, 0, :], fgt[:, 3, :], ACT.Copy, scale=-1.0).then_inc(ncum_hi, 1)

                elif kind == "heads":
                    u, slot = i, i % 2
                    _, _, gq, gk, _ = heads_of(u)
                    act.wait_ge(heads_ps, u + 1)
                    act.wait_ge(zeroed, 2)
                    if u >= 2:
                        act.wait_ge(score_ps, 2 * (u - 1))
                    for n in range(2):
                        r = slice(n * HD, (n + 1) * HD)
                        act.activation(qT[r, slot, 0, n, :], PS[r, 4, 0:S], ACT.Copy,
                                       scale=gq if isinstance(gq, float) else gq[r, :])
                    act.activation(kT[:, slot, 0, :], PS[:, 4, S:2 * S], ACT.Copy, scale=gk).then_inc(heads_hi, 1)

                elif kind == "scores":
                    sc = scores_sb(i)
                    for n in range(2):
                        a = 2 * i + n
                        for t, (c0, c1) in enumerate(QB):
                            act.wait_ge(smax, 2 * a + t + 1)
                            act.activation(sc[:, n, c0:c1], sc[:, n, c0:c1], ACT.Exp, bias=nmax[:, a, t:t + 1],
                                           scale=-1.0, accum_out=lsum[:, a, t:t + 1]).then_inc(exp_done, 1)

                elif kind == "probsT":
                    u, n = i
                    j = turned_head(u, n)
                    act.wait_ge(probs_ps, j + 1)
                    if j >= 2:
                        act.wait_ge(value_ps, pair_of_turned(j - 2) + 1)
                    act.activation(probs_T(u)[:, j % 2, :], PS[:, 4, 0:3 * P], ACT.Copy).then_inc(probs_sb, 1)

                elif kind == "values":
                    u, kd = i, kind_of(i)
                    act.wait_ge(value_ps, u + 1)
                    if kd == "fox":
                        act.activation(mixT[:, 0, u, :], PS[:, 5, 0:S], ACT.Copy).then_inc(mix_hi, 1)
                    elif kd == "moba":
                        m = u - FOX_P - DIFF_P
                        if m >= 1:
                            act.wait_ge(back_ps, m)
                        act.activation(ybT[:, :], PS[:, 5, 0:S], ACT.Copy).then_inc(ybT_in, 1)
                    else:
                        h = u - FOX_P
                        act.wait_ge(od_in, h + 1)
                        for t in range(TB):
                            c = t * DIFF + h
                            last = act.activation(sq[:, t, h * P:(h + 1) * P], PS[:, 5, t * P:(t + 1) * P], ACT.Square,
                                                  accum_out=dss[:, c:c + 1])
                        last.then_inc(dsq_in, 1)

                elif kind == "spatial":
                    act.wait_ge(ws_ps, 1)
                    act.activation(wsT[:, :, :].rearrange("p (b g) s -> p b (g s)", b=2), PS[:, 4:6, :], ACT.Copy
                                   ).then_inc(ws_T, 1)

                elif kind == "pT":
                    act.wait_ge(p_ps, 1)
                    act.activation(pT[:, 0].rearrange("p c s -> p (c s)"), PS[:, 4, :], ACT.Copy).then_inc(p_hi, 1)

                elif kind == "evac":
                    T = i
                    name, n, width = TILES[T]["name"], TILES[T]["n"], TILES[T]["width"]
                    ps, cols = tile_ps(T), slice(n * W, (n + 1) * W)
                    free = tile_free[T % 2]
                    if name in ("fox", "diff", "v", "u", "q", "k", "vatt", "ga", "gb", "gate", "ff1", "ple_proj", "ple"):
                        act.wait_ge(tile_done, T + 1)
                    if name in ("fox", "diff"):
                        j = n + (0 if name == "fox" else 3)
                        last = act.activation(tok1[:, j], ps, ACT.Copy)
                        last.then_inc(tok_in, 1)
                        if n < 2:
                            m = n + (0 if name == "fox" else 2)
                            if m:
                                act.wait_ge(hss_in, m)
                            act.activation(sq[:, :, :], ps, ACT.Square).then_inc(sq_in, 1)
                            act.wait_ge(sq_in, m + 1)
                        act.wait_ge(tok_in, j + 1)
                        act.sem_inc(free, 1)
                    elif name in ("v", "u"):
                        act.activation((vb if name == "v" else ub)[:, :, cols], ps, ACT.Gelu_apprx_tanh
                                       ).then_inc(v_in if name == "v" else u_in, 1)
                        act.wait_ge(v_in if name == "v" else u_in, n + 1)
                        act.sem_inc(free, 1)
                    elif name in ("q", "k", "vatt"):
                        j = ("q", "k", "vatt").index(name)
                        act.activation(tok2[:, j, :, cols], ps, ACT.Copy).then_inc(tok2_in, 1)
                        act.wait_ge(tok2_in, 2 * j + n + 1)
                        act.sem_inc(free, 1)
                    elif name == "ga":
                        if n == 0:
                            act.wait_ge(ws_T, 1)
                            act.wait_ge(ws_ps, 1)
                        else:
                            act.wait_ge(ga_in, 1)
                        act.activation(th2, ps, ACT.Tanh, scale=0.5).then_inc(th_in, 1)
                        act.wait_ge(th_in, 6 + n + 1)
                        act.sem_inc(free, 1)
                    elif name == "gb":
                        act.wait_ge(sgu_ps, 2)
                        act.activation(vb[:, :, cols], ps, ACT.Tanh, scale=0.5).then_inc(gb_in, 1)
                        act.wait_ge(gb_in, n + 1)
                        act.sem_inc(free, 1)
                    elif name == "gate":
                        if n:
                            act.wait_ge(r_in, n)
                        act.activation(th1[:, :, 0:width], ps, ACT.Tanh, scale=0.5).then_inc(th_in, 1)
                    elif name == "ff1":
                        act.activation(hid2[:, n % 2], ps, ACT.Relu).then_inc(u_in, 1)
                        act.wait_ge(u_in, 2 + n + 1)
                        act.sem_inc(free, 1)
                    elif name == "ple_proj":
                        act.activation(pp[:, :, cols], ps, ACT.Copy).then_inc(pp_in, 1)
                        act.wait_ge(pp_in, n + 1)
                        act.sem_inc(free, 1)
                    elif name == "ple":
                        act.activation(thp[:, n], ps, ACT.Tanh, scale=0.5).then_inc(th_in, 1)

        @block.vector
        def _(dve):
            own = [0]

            def then(ins):
                ins.then_inc(dve_step, 1)
                own[0] += 1
                dve.wait_ge(dve_step, own[0])

            def whole(t):
                return t.bitcast(F32)

            dve.memset(table[BUCKETS:BUCKETS + 1, :], MASKED).then_inc(table_set, 1)

            for it in ORDER:
                kind, i = it
                if kind == "split":
                    slot = landed(dve, it)
                    dve.wait_ge(hi_made, i + 1)
                    if i >= SPL:
                        dve.wait_ge(gemm_done, i - SPL + 1)
                    dve.tensor_tensor(slab_view(wlo, i % SPL, i), slab_view(raw, slot, i),
                                      whole(slab_view(whi, i % SPL, i)), ALU.subtract).then_inc(lo_made, 1)

                elif kind == "vectors":
                    dve.wait_ge(vec_in, 16 * 8)
                    dve.wait_ge(vec_ps, 1)
                    then(dve.tensor_copy(col[:, 0:V_ALL], PS[:, 4, 0:V_ALL]))
                    dve.tensor_scalar(col[:, V_ALL:V_ALL + 1], col[:, V_QK:V_QK + 1], HD ** -0.5, None, ALU.mult)
                    dve.tensor_scalar(col[:, V_ALL + 1:V_ALL + 2], col[:, V_QK + 2:V_QK + 3], HD ** -0.5, None, ALU.mult)
                    dve.tensor_scalar(col[:, V_ALL + 2:V_ALL + 3], col[:, V_DN:V_DN + 1], 1.0 - LAM_INIT, None,
                                      ALU.mult).then_inc(col_made, 1)
                    dve.tensor_copy(identr[:, :], ident).then_inc(ident_made, 1)
                    dve.wait_ge(cond_th, 1)
                    then(dve.scalar_tensor_tensor(out=cond[:, 1, :], in0=cond[:, 0, :], scalar=1.0,
                                                  in1=col[:, V_C:V_C + KC], op0=ALU.add, op1=ALU.mult))
                    dve.tensor_scalar(cond32[:, :, :], spread(cond[:, 1, :], 32), 0.5, None, ALU.mult
                                      ).then_inc(cond_made, 1)
                    dve.wait_ge(setup_in, 16 * NSETUP)
                    dve.memset(ones[:, :], 1.0)
                    for n in range(2):
                        last = dve.tensor_tensor_reduce(lprod[:, n, :], lamb[:, 2 * n, :], lamb[:, 2 * n + 1, :],
                                                        1.0, 0.0, ALU.mult, ALU.add, lam[:, n:n + 1])
                    last.then_inc(lam_exp, 1)
                    dve.wait_ge(lam_exp, 2)
                    dve.scalar_tensor_tensor(out=lam[:, 4:5], in0=lam[:, 2:3], scalar=LAM_INIT, in1=lam[:, 3:4],
                                             op0=ALU.add, op1=ALU.subtract).then_inc(lam_made, 1)
                    dve.wait_ge(wfg_lo, 1)
                    dve.tensor_tensor(wfgs[:, 1], wfg[:, :, :], whole(wfgs[:, 0]), ALU.subtract).then_inc(wfg_lo, 1)

                elif kind == "relbias":
                    dve.wait_ge(rel_ps, 1)
                    dve.tensor_copy(relrow[:, :], PS[0:MOBA, 5, 0:SKEW]).then_inc(rel_row, 1)

                elif kind == "ada" and i % KC == KC - 1:
                    pack = i // KC
                    if pack == 0:
                        dve.wait_ge(lam_sum, 16 * 4)
                    dve.wait_ge(ada_used, i + 1)
                    dve.tensor_tensor(mod[:, pack, :], PS[:, 7, :], mod[:, pack, :], ALU.add).then_inc(mod_in, 1)

                elif kind == "mod":
                    dve.wait_ge(mod_T, i + 1)
                    sh, sc, v = ((4, 0), (4, 2), V_LN1) if i == 0 else ((4, 2), (5, 0), V_LN2)

                    def columns(b, j0):
                        return PS[:, b, :].rearrange("p (c j r) -> p j c r", c=4, j=4)[:, j0:j0 + 2, :, 0]

                    dve.tensor_copy(AB[:, 2 * i + 1, :].rearrange("p (j c) -> p j c", j=2), columns(*sh))
                    dve.scalar_tensor_tensor(out=AB[:, 2 * i, :].rearrange("p (j c) -> p j c", j=2), in0=columns(*sc),
                                             scalar=1.0, in1=col[:, v:v + KC].rearrange("p (j c) -> p j c", j=2),
                                             op0=ALU.add, op1=ALU.mult).then_inc(ab_made, 1)

                elif kind in ("norm", "final"):
                    n = 5 if kind == "final" else i
                    xn = (xn1, xnb, xn2, xnc, xnc, fin)[n]
                    if n == 0:
                        dve.wait_ge(x_in, 16)
                    else:
                        dve.wait_ge(x_done, 2 * n)
                    if n == 1:
                        dve.wait_ge(rel_out, 16)
                    dve.tensor_tensor_reduce(xn[:, 1, :], x[:, 1, :], x[:, 1, :], 1.0, 0.0, ALU.mult, ALU.add,
                                             nss[:, n, 1:2]).then_inc(sum_dve, 1)
                    dve.wait_ge(norm_rs, n + 1)
                    if kind == "norm":
                        dve.tensor_scalar(xn[:, 1, :], x[:, 1, :], nrs[:, n, 1:2], None, ALU.mult).then_inc(xn_dve, 1)
                    else:
                        dve.wait_ge(gfin_in, 16)
                        for t in range(TB):
                            dve.scalar_tensor_tensor(out=fin[:, t, :], in0=x[:, t, :], scalar=nrs[:, n, t:t + 1],
                                                     in1=gfin[:, :], op0=ALU.mult, op1=ALU.mult).then_inc(out_made, 1)

                elif kind == "turn":
                    q = TURNS[i]
                    _, _, dst, c0, chunks = turn_of(i)
                    b = turn_banks(q)
                    name = "h" if i[0] in ("norm", "merge") else "other"
                    if name == "h" and slabs_before(it, "h"):
                        dve.wait_ge(gemm_done, slabs_before(it, "h"))
                    dve.wait_ge(turned, q + 1)
                    lo = dst[:, 1, c0:c0 + chunks, :]
                    hi = whole(dst[:, 0, c0:c0 + chunks, :])
                    if i[0] == "norm" and i[1] < 2:
                        aff = aff1 if i[1] == 0 else affb
                        if i[2] == 0:
                            dve.wait_ge(ab_made, i[1] + 1)
                        else:
                            dve.wait_ge(turn_lo, q)
                        for c in range(4):
                            k = c0 + c
                            last = dve.tensor_scalar(aff[:, c, :], PS[:, b + c // 2, c % 2 * S:(c % 2 + 1) * S],
                                                     AB[:, 2 * i[1], k:k + 1], AB[:, 2 * i[1] + 1, k:k + 1],
                                                     ALU.mult, ALU.add)
                        last.then_inc(turn_aff, 1)
                        dve.wait_ge(turn_hi, q + 1)
                        dve.wait_ge(turn_aff, q_affine(i) + 1)
                        dve.tensor_tensor(lo, aff[:, :, :], hi, ALU.subtract).then_inc(turn_lo, 1)
                    else:
                        dve.wait_ge(turn_hi, q + 1)
                        gain = gain_of(i, 0)
                        if gain is None or isinstance(gain, float):
                            ps = PS[:, b:b + chunks // 2, :]
                            dve.scalar_tensor_tensor(out=lo.rearrange("p (a c) s -> p a (c s)", c=2), in0=ps,
                                                     scalar=1.0 if gain is None else gain,
                                                     in1=hi.rearrange("p (a c) s -> p a (c s)", c=2),
                                                     op0=ALU.mult, op1=ALU.subtract).then_inc(turn_lo, 1)
                        else:
                            for c in range(chunks):
                                last = dve.scalar_tensor_tensor(out=lo[:, c, :], in0=PS[:, b + c // 2, c % 2 * S:(c % 2 + 1) * S],
                                                                scalar=gain_of(i, c), in1=hi[:, c, :],
                                                                op0=ALU.mult, op1=ALU.subtract)
                            last.then_inc(turn_lo, 1)

                elif kind == "fgate":
                    dve.wait_ge(fg_ps, 1)
                    dve.tensor_scalar(fgt[:, 0, :], PS[0:FOX, 4, 0:S], bf[:, :], None, ALU.add).then_inc(fg_abs, 1)
                    dve.wait_ge(fg_abs, 1)
                    dve.scalar_tensor_tensor(out=fgt[:, 1, :], in0=fgt[:, 0, :], scalar=-1.0, in1=fgt[:, 0, :],
                                             op0=ALU.mult, op1=ALU.min).then_inc(fg_abs, 1)
                    dve.wait_ge(fg_log, 1)
                    then(dve.scalar_tensor_tensor(out=fgt[:, 2, :], in0=fgt[:, 0, :], scalar=0.0, in1=fgt[:, 1, :],
                                                  op0=ALU.min, op1=ALU.subtract))
                    dve.tensor_tensor_scan(fgt[:, 3, :], ones[:, :], fgt[:, 2, :], 0.0, ALU.mult, ALU.add
                                           ).then_inc(cum_made, 1)
                    dve.wait_ge(ncum_hi, 1)
                    dve.wait_ge(cum_made, 1)
                    dve.scalar_tensor_tensor(out=ncum[0:FOX, 1, :], in0=fgt[:, 3, :], scalar=-1.0,
                                             in1=whole(ncum[0:FOX, 0, :]), op0=ALU.mult, op1=ALU.subtract
                                             ).then_inc(ncum_lo, 1)
                    dve.wait_ge(cumq_ps, 1)
                    dve.tensor_copy(cumq[:, :, :].rearrange("p t h -> p (t h)"), PS[:, 5, 0:TB * FOX]).then_inc(cumq_in, 1)

                elif kind == "heads":
                    u, slot = i, i % 2
                    _, _, gq, gk, _ = heads_of(u)
                    dve.wait_ge(heads_ps, u + 1)
                    dve.wait_ge(heads_hi, u + 1)
                    for n in range(2):
                        r = slice(n * HD, (n + 1) * HD)
                        dve.scalar_tensor_tensor(out=qT[r, slot, 1, n, :], in0=PS[r, 4, 0:S],
                                                 scalar=gq if isinstance(gq, float) else gq[r, :],
                                                 in1=whole(qT[r, slot, 0, n, :]), op0=ALU.mult, op1=ALU.subtract)
                    dve.scalar_tensor_tensor(out=kT[:, slot, 1, :], in0=PS[:, 4, S:2 * S], scalar=gk,
                                             in1=whole(kT[:, slot, 0, :]), op0=ALU.mult, op1=ALU.subtract
                                             ).then_inc(heads_lo, 1)

                elif kind == "scores":
                    u, kd, sc = i, kind_of(i), scores_sb(i)
                    for n in range(2):
                        a = 2 * u + n
                        dve.wait_ge(score_ps, a + 1)
                        if u and kd == kind_of(u - 1) or kd == "diff":
                            dve.wait_ge(probs_ps, turned_head(u - 1, n if kind_of(u - 1) != "diff" else 0) + 1)
                        if kd == "fox":
                            dve.wait_ge(mcum_in, a + 1)
                            bias = [mcum[:, a % 2, c0:c1] for c0, c1 in QB]
                        elif kd == "diff":
                            bias = [alibi[:, u - FOX_P, P:2 * P], alibi[:, u - FOX_P, :]]
                        else:
                            if u == FOX_P + DIFF_P:
                                dve.wait_ge(rel_in, 16)
                            h = a - 2 * (FOX_P + DIFF_P)
                            bias = [toep[:, h, 0:P], toep[:, h, :]]
                        for t, (c0, c1) in enumerate(QB):
                            made, score = sc[:, n, c0:c1], PS[:, 5 + n, c0:c1]
                            if kd == "moba":
                                made, score = backwards(made), backwards(score)
                            dve.tensor_tensor_reduce(made, score, bias[t], -1.0, 3e38,
                                                     ALU.add, ALU.min, nmax[:, a, t:t + 1]).then_inc(smax, 1)
                    for n in range(2):
                        a = 2 * u + n
                        dve.wait_ge(exp_done, 2 * a + 2)
                        then(dve.reciprocal(rinv[:, a, :], lsum[:, a, :]))
                        if kd == "fox":
                            for t, (c0, c1) in enumerate(QB):
                                last = dve.tensor_scalar(sc[:, n, c0:c1], sc[:, n, c0:c1], rinv[:, a, t:t + 1], None,
                                                         ALU.mult)
                            last.then_inc(fox_p, 1)
                    if kd == "diff":
                        a = 2 * u
                        if u == FOX_P:
                            dve.wait_ge(lam_made, 1)
                        then(dve.tensor_scalar(rinv[:, a + 1, :], rinv[:, a + 1, :], lam[:, 4:5], None, ALU.mult))
                        for t, (c0, c1) in enumerate(QB):
                            last = dve.tensor_scalar(sc[:, 1, c0:c1], sc[:, 1, c0:c1], rinv[:, a + 1, t:t + 1], None,
                                                     ALU.mult)
                        then(last)
                        for t, (c0, c1) in enumerate(QB):
                            last = dve.scalar_tensor_tensor(out=sc[:, 0, c0:c1], in0=sc[:, 0, c0:c1],
                                                            scalar=rinv[:, a, t:t + 1], in1=sc[:, 1, c0:c1],
                                                            op0=ALU.mult, op1=ALU.subtract)
                        last.then_inc(diff_p, 1)

                elif kind == "values":
                    u, kd = i, kind_of(i)
                    if kd == "fox":
                        dve.wait_ge(value_ps, u + 1)
                        dve.wait_ge(mix_hi, u + 1)
                        dve.tensor_tensor(mixT[:, 1, u, :], PS[:, 5, 0:S], whole(mixT[:, 0, u, :]), ALU.subtract
                                          ).then_inc(mix_lo, 1)
                    elif kd == "diff":
                        h = u - FOX_P
                        dve.wait_ge(value_ps, u + 1)
                        dve.tensor_copy(od[:, :, h * P:(h + 1) * P], PS[:, 5, 0:S].rearrange("p (t d) -> p t d", t=TB)
                                        ).then_inc(od_in, 1)

                elif kind == "diffnorm":
                    dve.wait_ge(drs_made, 1)
                    dve.wait_ge(od_in, DIFF)
                    o = od[:, :, :].rearrange("p t (h d) -> p (t h) d", h=DIFF)
                    dve.tensor_tensor(o, o, spread(drs[:, :], P), ALU.mult).then_inc(od_made, 1)

                elif kind == "back":
                    m = i - FOX_P - DIFF_P
                    dve.wait_ge(back_ps, m + 1)
                    inv = rinv[:, 2 * i:2 * i + 2, :].rearrange("p n t -> p t n")
                    dve.tensor_tensor(tok2[:, 0, :, m * P:(m + 1) * P].rearrange("p t (n d) -> p t n d", n=2),
                                      PS[:, 4, 0:S].rearrange("p (t n d) -> p t n d", t=TB, n=2), spread(inv, HD),
                                      ALU.mult).then_inc(yb_in, 1)

                elif kind == "layernorm":
                    dve.wait_ge(v_in, 2)
                    for t in range(TB):
                        for h in range(2):
                            last = dve.bn_stats(bn[:, t, h, :], vb[:, t, h * W:(h + 1) * W])
                    then(last)
                    for t in range(TB):
                        last = dve.bn_aggr(mv[:, t, :], bn[:, t].rearrange("p h s -> p (h s)"))
                    last.then_inc(mv_made, 1)
                    dve.wait_ge(mv_made, 1)
                    dve.wait_ge(vrs_made, 1)
                    for t in range(TB):
                        dve.tensor_scalar(vb[:, t, :], vb[:, t, :], mv[:, t, 0:1], vrs[:, t:t + 1],
                                          ALU.subtract, ALU.mult).then_inc(vc_made, 1)

                elif kind == "sgu":
                    dve.wait_ge(u_in, 2)
                    dve.wait_ge(sgu_ps, i + 1)
                    b = 4 + 2 * i
                    for gr in range(4 * i, 4 * i + 4):
                        c = (gr % 2) * S
                        uc = ub[:, :, gr * P:(gr + 1) * P]
                        last = dve.scalar_tensor_tensor(
                            out=uc, in0=PS[:, b + gr % 4 // 2, c:c + S].rearrange("p (t c) -> p t c", t=TB),
                            scalar=col[:, V_BS + gr:V_BS + gr + 1], in1=uc, op0=ALU.add, op1=ALU.mult)
                    last.then_inc(ya_in, 1)

                elif kind == "merge":
                    cols = slice(i * W, (i + 1) * W)
                    y = tok2[:, 0, :, cols]
                    dve.wait_ge(yb_in, 4 * (i + 1))
                    dve.wait_ge(gb_in, i + 1)
                    dve.wait_ge(ga_in, i + 1)
                    then(dve.scalar_tensor_tensor(out=y, in0=vb[:, :, cols], scalar=1.0, in1=y, op0=ALU.add,
                                                  op1=ALU.mult))
                    dve.tensor_tensor(y, y, ub[:, :, cols], ALU.add).then_inc(merged, 1)

                elif kind == "pT":
                    dve.wait_ge(p_ps, 1)
                    dve.wait_ge(p_hi, 1)
                    dve.tensor_tensor(pT[:, 1].rearrange("p c s -> p (c s)"), PS[:, 4, :],
                                      whole(pT[:, 0]).rearrange("p c s -> p (c s)"), ALU.subtract).then_inc(p_lo, 1)

                elif kind == "evac":
                    T = i
                    name, n, width = TILES[T]["name"], TILES[T]["n"], TILES[T]["width"]
                    ps, cols = tile_ps(T), slice(n * W, (n + 1) * W)
                    free = tile_free[T % 2]
                    if name in ("fox", "diff") and n < 2:
                        m = n + (0 if name == "fox" else 2)
                        dve.wait_ge(sq_in, m + 1)
                        dve.tensor_reduce(hss[:, m, :], sq[:, :, :].rearrange("p t (h d) -> p (t h) d", d=HD), AX,
                                          ALU.add).then_inc(hss_in, 1)
                    elif name in ("w_out", "down"):
                        row, tmp = (g1row, sq) if name == "w_out" else (g2row[:, :], tmpb)
                        dve.wait_ge(g1_row if name == "w_out" else g2_row, 1)
                        dve.wait_ge(tile_done, T + 1)
                        if name == "w_out":
                            dve.wait_ge(dsq_in, DIFF)
                        if n:
                            dve.wait_ge(x_done, (2 if name == "down" else 0) + n)
                        dve.tensor_tensor(tmp[:, :, :], ps, twice(row[:, cols]), ALU.mult).then_inc(free, 1)
                        dve.wait_ge(free, T // 2 + 1)
                        dve.tensor_tensor(x[:, :, cols], x[:, :, cols], tmp[:, :, :], ALU.add).then_inc(x_done, 1)
                    elif name in ("w_out2", "ff2"):
                        dve.wait_ge(tile_done, T + 1)
                        dve.tensor_tensor(x[:, :, cols], x[:, :, cols], ps, ALU.add).then_inc(x_done, 1)
                        done = {"w_out2": 4, "ff2": 6}[name] + n + 1
                        dve.wait_ge(x_done, done)
                        dve.sem_inc(free, 1)
                    elif name == "gate":
                        dve.wait_ge(th_in, n + 1)
                        th = th1[:, :, 0:width]
                        dve.scalar_tensor_tensor(out=hid1[:, n % 2, :, 0:width], in0=th, scalar=1.0, in1=ps,
                                                 op0=ALU.add, op1=ALU.mult).then_inc(r_in, 1)
                        dve.wait_ge(r_in, n + 1)
                        dve.sem_inc(free, 1)
                    elif name == "up":
                        dve.wait_ge(tile_done, T + 1)
                        o = hid1[:, n % 2, :, 0:width]
                        dve.scalar_tensor_tensor(out=o, in0=o, scalar=0.5, in1=ps, op0=ALU.mult, op1=ALU.mult
                                                 ).then_inc(hid_in, 1)
                        dve.wait_ge(hid_in, n + 1)
                        dve.sem_inc(free, 1)
                    elif name == "ga":
                        dve.wait_ge(th_in, 6 + n + 1)
                        dve.wait_ge(ya_in, 2)
                        uc = ub[:, :, cols]
                        dve.scalar_tensor_tensor(out=uc, in0=th2, scalar=1.0, in1=uc, op0=ALU.add, op1=ALU.mult
                                                 ).then_inc(ga_in, 1)
                    elif name == "ff1":
                        dve.wait_ge(u_in, 2 + n + 1)
                        h = hid2[:, n % 2]
                        dve.tensor_tensor(h, h, h, ALU.mult).then_inc(hid_in, 1)
                    elif name == "ple":
                        dve.wait_ge(th_in, 8 + n + 1)
                        dve.sem_inc(free, 1)
                        dve.wait_ge(pp_in, 2)
                        then(dve.scalar_tensor_tensor(out=thp[:, n], in0=thp[:, n], scalar=1.0, in1=pp[:, :, cols],
                                                      op0=ALU.add, op1=ALU.mult))
                        dve.scalar_tensor_tensor(out=x[:, :, cols], in0=thp[:, n], scalar=0.5, in1=x[:, :, cols],
                                                 op0=ALU.mult, op1=ALU.add).then_inc(x_done, 1)

        @block.gpsimd
        def _(pool):
            own = [0]

            def then(ins):
                ins.then_inc(pool_step, 1)
                own[0] += 1
                pool.wait_ge(pool_step, own[0])

            def inverse_root(dst, sums, width):
                then(pool.tensor_scalar(dst, sums, 1.0 / width, EPS, ALU.mult, ALU.add))
                n = dst.shape[-1]
                return pool.tensor_tensor(dst, dst, expo[:, 0:n], ALU.pow)

            then(pool.memset(expo[:, :], -0.5))
            then(pool.memset(qT[HD:P, :, :, 0, :].rearrange("p a b s -> p (a b) s").bitcast(F32), 0.0))
            pool.memset(qT[0:HD, :, :, 1, :].rearrange("p a b s -> p (a b) s").bitcast(F32), 0.0).then_inc(zeroed, 1)
            pool.wait_ge(zeroed, 1)
            pool.memset(ncum[:, :, :].bitcast(F32), 0.0).then_inc(zeroed, 1)

            for it in ORDER:
                kind, i = it
                if kind == "relbias":
                    pool.wait_ge(rel_row, 1)
                    pool.dma_start(skew.ap(), relrow[:, :]).then_inc(rel_out, 16)

                elif kind in ("norm", "final"):
                    n = 5 if kind == "final" else i
                    pool.wait_ge(sum_act, n + 1)
                    pool.wait_ge(sum_dve, n + 1)
                    inverse_root(nrs[:, n, :], nss[:, n, :], D).then_inc(norm_rs, 1)
                    if n == 2:
                        pool.wait_ge(gemm_done, slabs_before(("norm", 2), "hid"))
                        pool.wait_ge(x_done, 4)
                        pool.dma_start(ws[:, :, :], A["w_sgu_spatial_2"][0].rearrange("g t s -> t g s")
                                       ).then_inc(ws_in, 16)
                        for n, name in enumerate(("ln_v_g_2", "ln_v_b_2")):
                            pool.dma_start(lngb[:, n, :], A[name].to_broadcast([P, D])).then_inc(ln_in, 16)

                elif kind == "evac" and TILES[i]["name"] in ("fox", "diff") and TILES[i]["n"] < 2:
                    n, name = TILES[i]["n"], TILES[i]["name"]
                    m, j = (n, n) if name == "fox" else (n + 2, n + 3)
                    pool.wait_ge(hss_in, m + 1)
                    then(inverse_root(hrs[:, m, :], hss[:, m, :], HD))
                    pool.wait_ge(tok_in, j + 1)
                    t = tok1[:, j].rearrange("p t (h d) -> p (t h) d", d=HD)
                    pool.tensor_tensor(t, t, spread(hrs[:, m, :], HD), ALU.mult).then_inc(qk_ready, 1)

                elif kind == "scores" and kind_of(i) == "fox":
                    for n in range(2):
                        a = 2 * i + n
                        if a == 0:
                            pool.wait_ge(cumq_in, 1)
                        if a >= 2:
                            pool.wait_ge(smax, 2 * (a - 2) + 2)
                        pool.tensor_scalar(mcum[:, a % 2, 0:P], mask[:, P:2 * P], cumq[:, 0, a:a + 1], None, ALU.add)
                        pool.tensor_scalar(mcum[:, a % 2, P:3 * P], mask, cumq[:, 1, a:a + 1], None, ALU.add
                                           ).then_inc(mcum_in, 1)

                elif kind == "diffnorm":
                    pool.wait_ge(dsq_in, DIFF)
                    inverse_root(drs[:, :], dss[:, :], 2 * HD).then_inc(drs_made, 1)

                elif kind == "spatial":
                    pool.wait_ge(ws_in, 16)
                    pool.affine_select(out=ws[:, :, :], in_=ws[:, :, :], compare_op=ALU.is_ge, fill=0.0, base=0,
                                       pattern=[[0, 8], [-1, P]], channel_multiplier=1).then_inc(ws_low, 1)

                elif kind == "layernorm":
                    pool.wait_ge(mv_made, 1)
                    then(pool.tensor_scalar(vrs[:, :], mv[:, :, 1], 1.0, EPS, ALU.mult, ALU.add))
                    pool.tensor_tensor(vrs[:, :], vrs[:, :], expo[:, 0:TB], ALU.pow).then_inc(vrs_made, 1)
                    pool.wait_ge(ln_in, 32)
                    for t in range(TB):
                        pool.wait_ge(vc_made, t + 1)
                        then(pool.tensor_tensor(vb[:, t, :], vb[:, t, :], lngb[:, 0, :], ALU.mult))
                        pool.tensor_tensor(vb[:, t, :], vb[:, t, :], lngb[:, 1, :], ALU.add).then_inc(vn_made, 1)
                    pool.wait_ge(vn_made, TB)
                    pool.wait_ge(rel_out, 16)
                    pool.dma_start(toep[:, :, :], bass.AP(tensor=skew, offset=0,
                                                          ap=[[1, P], [SKEW, MOBA], [1, 2 * P]])).then_inc(rel_in, 16)

                elif kind == "pT":
                    pool.wait_ge(gemm_done, slabs_before(("pT", 0), "hid"))
                    pool.dma_start(pin[:, :, :], A["p_2"][0, 0].rearrange("(t p) f -> p t f", p=P)).then_inc(p_in, 16)
                    pool.dma_start(gfin[:, :], A["norm_final_g_2"].rearrange("(a d) -> a d", a=1).to_broadcast([P, D])
                                   ).then_inc(gfin_in, 16)


def q_affine(key):
    return 2 * key[1] + key[2]


def constants():
    c = np.zeros((P, C_ALL), np.float32)
    c[:, C_ID:C_ID + P] = np.eye(P)
    dist = P + np.arange(P)[:, None] - np.arange(2 * P)[None, :]
    c[:, C_MASK:C_MASK + 2 * P] = np.where(dist >= 0, 0.0, MASKED)
    for h in range(DIFF):
        slope = 2.0 ** (-8.0 * (h + 1) / DIFF)
        c[:, C_ALIBI + h * 2 * P:C_ALIBI + (h + 1) * 2 * P] = np.where(dist >= 0, -slope * dist, MASKED)
    far = np.arange(SKEW) - (P - 1)
    exact = BUCKETS // 2
    n = np.maximum(far, exact).astype(np.float32)
    large = exact + (np.log(n / np.float32(exact)) / np.float32(np.log(1024 / exact)) * np.float32(BUCKETS - exact)
                     ).astype(np.int32)
    bucket = np.where(far < 0, BUCKETS, np.where(far < exact, np.maximum(far, 0), np.minimum(large, BUCKETS - 1)))
    c[bucket, C_HOT + np.arange(SKEW)] = 1.0
    return c


_INS = ["x", "c", "ln1_g", "ln2_g", "w_ada", "b_ada", "w_in", "b_f", "fox_qk_g", "diff_qk_g", "diff_lam",
        "diff_norm_g", "w_out", "w_gate", "w_up", "w_down", "p_2", "norm_mix_g_2", "w_in_2", "w_sgu_spatial_2",
        "b_sgu_spatial_2", "ln_v_g_2", "ln_v_b_2", "rel_bias_2", "w_out_2", "norm_ffn_g_2", "w_ff1_2", "w_ff2_2",
        "norm_ple_g_2", "w_ple_gate_2", "w_ple_proj_2", "norm_final_g_2"]


def kernel(**inputs):
    import concourse.bacc as bacc
    from concourse.bass_utils import run_bass_kernel_spmd

    nc = bacc.Bacc("TRN2", target_bir_lowering=False, num_devices=1)
    arrays, args = {}, {}
    for name in _INS + ["constants"]:
        a = constants() if name == "constants" else np.ascontiguousarray(inputs[name])
        arrays[f"in_{name}"] = a
        args[name] = nc.dram_tensor(f"in_{name}", a.shape, mybir.dt.from_np(a.dtype), kind="ExternalInput").ap()
    result = nc.dram_tensor("out_x", (1, S, D), F32, kind="ExternalOutput").ap()
    build(nc, args, result)
    r = run_bass_kernel_spmd(nc, [arrays], core_ids=[0])
    return r.results[0]["out_x"]
```

```python
from contextlib import ExitStack
from math import exp as _exp

import numpy as np

import concourse.bass as bass
from concourse import mybir

F32 = mybir.dt.float32
F32R = mybir.dt.float32r
ALU = mybir.AluOpType
ACT = mybir.ActivationFunctionType
AX = mybir.AxisListType.X

P = 128
D = 1024
S = 256
TB = S // P
KC = D // P
HD = 64
FOX, DIFF, MOBA = 8, 4, 16
W = 512
DFF = 2816
DFF2 = 4096
EPS = 1e-6
MASKED = -1e30
BUCKETS = 32
LAM_INIT = 0.8 - 0.6 * _exp(0.0)
SKEW = 384
RAW, SPL = 4, 3

C_ID, C_MASK, C_ALIBI, C_HOT = 0, 128, 384, 1408
C_ALL = C_HOT + SKEW

V_C, V_LN1, V_LN2, V_MIX, V_FFN, V_PLE, V_BS, V_QK, V_DN = 0, 8, 16, 24, 32, 40, 48, 56, 60
V_ALL = 61

PAIRS = FOX // 2 + DIFF + MOBA // 2
FOX_P, DIFF_P = FOX // 2, DIFF


def kind_of(u):
    return "fox" if u < FOX_P else "diff" if u < FOX_P + DIFF_P else "moba"


def plan():
    tiles, slabs, order = [], [], []

    def tile(name, n, chunks, operand, width=W):
        tiles.append(dict(name=name, n=n, K=chunks, operand=operand, width=width))
        return len(tiles) - 1

    def slab(T, weight, col, k0, chunks=4, width=W):
        s = len(slabs)
        slabs.append(dict(weight=weight, row=k0 * P, chunks=chunks, col=col, cols=width))
        return [("piece", dict(T=T, k=k0 + j, slab=s, off=j * width, first=j == 0, last=j == chunks - 1))
                for j in range(chunks)]

    def whole(name, n, weight, col, operand, width=W):
        T = tile(name, n, KC, operand, width)
        return slab(T, weight, col, 0, 4, width) + slab(T, weight, col, 4, 4, width) + [("evac", T)]

    def long(name, n, weight, operand, chunks):
        T = tile(name, n, chunks, operand)
        out = []
        for k0 in range(0, chunks, 4):
            out += slab(T, weight, n * W, k0, min(4, chunks - k0))
        return out + [("evac", T)]

    def halves(name, weight, col, operand, ahead, between, after=()):
        Ts = [tile(name, n, KC, operand) for n in range(2)]
        out = slab(Ts[0], weight, col, 0) + ahead + slab(Ts[1], weight, col + W, 0) + between
        for n, T in enumerate(Ts):
            out += slab(T, weight, col + n * W, 4) + [("evac", T)] + (after[n] if after else [])
        return out

    def insert(items, *at):
        out = list(items)
        for pos, steps in sorted(at, reverse=True, key=lambda x: x[0]):
            out[pos:pos] = steps
        return out

    def attention(us, filler, counts, late=()):
        filler = list(filler)

        def fill(n):
            out = []
            while n > 0 and filler:
                it = filler.pop(0)
                out.append(it)
                n -= it[0] in ("piece", "ada")
            while filler and filler[0][0] not in ("piece", "ada"):
                out.append(filler.pop(0))
            return out

        moba = kind_of(us[0]) == "moba"
        out = [("heads", us[0])] + fill(counts[3]) + [("scores", us[0])] + fill(counts[2])
        for u in us:
            more = u != us[-1]
            out += [("probsT", (u, 0))]
            if more:
                out += [("heads", u + 1)]
            out += fill(counts[0])
            if kind_of(u) != "diff":
                out += [("probsT", (u, 1))] + fill(counts[1])
            out += [("values", u)] + fill(counts[3])
            if more:
                out += [("scores", u + 1)]
                if moba:
                    out += [("back", u)]
                out += fill(counts[2])
        late = filler + list(late)
        if moba:
            out += late[:3] + [("back", us[-1])]
            late = late[3:]
        return out + late

    ada = [("ada", j) for j in range(3 * KC)]

    order += [("cond", 0), ("sums", (0, 0)), ("sums", (0, 1)), ("norm", 0)]
    order += ada[:2] + [("vectors", 0)] + ada[2:4] + [("mod", 0), ("turn", ("norm", 0, 0))]
    fox = [tile("fox", n, KC, "h") for n in range(2)]
    order += slab(fox[0], "w_in", 0, 0) + ada[4:6] + slab(fox[1], "w_in", W, 0) + ada[6:8]
    order += [("mod", 1), ("turn", ("norm", 0, 1)), ("setup", 0), ("relbias", 0)]
    order += slab(fox[0], "w_in", 0, 4) + [("evac", fox[0])]
    order += slab(fox[1], "w_in", W, 4) + [("evac", fox[1]), ("fgate", 0)]
    order += insert(whole("fox", 2, "w_in", 2 * W, "h"), (4, [("cum", 0)]))
    tail = []
    for n in range(3):
        tail += whole("diff", n, "w_in", 3 * W + FOX + n * W, "h")
    tail = insert(tail, (8, ada[8:9]), (18, ada[9:10]))
    order += attention(list(range(FOX_P)), tail, (1, 1, 3, 1))
    wo = [tile("w_out", n, KC, "mix") for n in range(2)]
    fill = slab(wo[0], "w_out", 0, 0) + slab(wo[1], "w_out", W, 0)
    fill = insert(fill, *[(j, [ada[10 + j]]) for j in range(8)])
    order += attention(list(range(FOX_P, FOX_P + DIFF_P)), fill, (1, 1, 2, 1), ada[18:20] + [("grow", 0)])
    order += [("diffnorm", 0)] + ada[20:21] + [("turn", ("diff", 0, 0))] + ada[21:22]
    order += slab(wo[0], "w_out", 0, 4) + [("evac", wo[0]), ("sums", (1, 0))]
    order += slab(wo[1], "w_out", W, 4) + [("evac", wo[1]), ("sums", (1, 1))] + ada[22:24]
    order += [("mod", 2), ("norm", 1)]
    order += [("turn", ("norm", 1, 0)), ("turn", ("norm", 1, 1))]
    late = []
    for n in range((DFF + W - 1) // W):
        width = min(W, DFF - n * W)
        now = whole("gate", n, "w_gate", n * W, "h", width) + whole("up", n, "w_up", n * W, "h", width)
        order += insert(now, (4, late))
        late = [("turn", ("hid", n, 0))]
    order += insert(long("down", 0, "w_down", "hid", DFF // P), (4, late), (8, [("grow", 1)]))
    order += insert(long("down", 1, "w_down", "hid", DFF // P), (6, [("sums", (2, 0)), ("turn", ("norm", 2, 0))]))
    order += [("sums", (2, 1)), ("norm", 2)]
    order += halves("v", "w_in_2", D, "h", [("turn", ("norm", 2, 1))], [], [[("spatial", 0)], []])
    order += [("layernorm", 0)]
    for n in (0, 1):
        order += whole("u", n, "w_in_2", n * W, "h")
    for j, name in enumerate(("q", "k", "vatt")):
        for n in (0, 1):
            order += whole(name, n, "w_in_2", 2 * D + j * D + n * W, "h")
            if (j, n) == (0, 1):
                order += [("sgu", 0), ("sgu", 1)]
    gates = []
    for n in (0, 1):
        for j, name in enumerate(("ga", "gb")):
            gates += whole(name, n, "w_in_2", 5 * D + j * D + n * W, "h")
    wo = [tile("w_out2", n, KC, "h") for n in range(2)]
    gates = insert(gates, (len(gates) - 5, [("merge", 0), ("turn", ("merge", 0, 0))]))
    most = slab(wo[0], "w_out_2", 0, 0) + slab(wo[1], "w_out_2", W, 0)
    order += attention(list(range(FOX_P + DIFF_P, PAIRS)), gates, (1, 1, 3, 0), most[:3])
    order += [("merge", 1)] + most[3:6] + [("turn", ("merge", 1, 0))] + most[6:]
    order += slab(wo[0], "w_out_2", 0, 4) + [("evac", wo[0])]
    order += insert(slab(wo[1], "w_out_2", W, 4), (2, [("sums", (3, 0)), ("turn", ("norm", 3, 0))]))
    order += [("evac", wo[1]), ("sums", (3, 1)), ("norm", 3)]
    order += halves("ff1", "w_ff1_2", 0, "h", [("turn", ("norm", 3, 1))], [])
    turns2 = [[("turn", ("hid2", n, 0))] for n in range(DFF2 // W)]
    for n in range(2, DFF2 // W):
        now = whole("ff1", n, "w_ff1_2", n * W, "h")
        order += insert(now, (4, turns2[n - 1] if n > 2 else turns2[0] + turns2[1]))
    order += insert(long("ff2", 0, "w_ff2_2", "hid", DFF2 // P), (4, turns2[-1]), (10, [("pT", 0)]))
    order += insert(long("ff2", 1, "w_ff2_2", "hid", DFF2 // P), (6, [("sums", (4, 0)), ("turn", ("norm", 4, 0))]))
    for n in (0, 1):
        order += long("ple_proj", n, "w_ple_proj_2", "p", 2) + [[("sums", (4, 1)), ("norm", 4)], []][n]
    order += halves("ple", "w_ple_gate_2", 0, "h", [("turn", ("norm", 4, 1))], [],
                    [[("sums", (5, 0))], [("sums", (5, 1))]])
    order += [("final", 0)]

    out, split = [], 0
    for it in order:
        if it[0] == "piece" and it[1]["first"]:
            while split <= min(it[1]["slab"] + 2, len(slabs) - 1):
                out.append(("split", split))
                split += 1
        out.append(it)
    turn = 0
    turns = {}
    for it in out:
        if it[0] == "turn":
            turns[it[1]] = turn
            turn += 1
    return tiles, slabs, out, turns


TILES, SLABS, ORDER, TURNS = plan()
assert [p["slab"] for kind, p in ORDER if kind == "piece" and p["first"]] == list(range(len(SLABS)))
LAST_SLAB = {p["T"]: p["slab"] for kind, p in ORDER if kind == "piece"}
STREAM = [it for it in ORDER if it[0] in ("split", "ada")]
STREAM_AT = {it: n for n, it in enumerate(STREAM)}


def transfers(it):
    return 2 if it[0] == "ada" and it[1] < KC else 1


def spread(ap, n):
    return bass.AP(tensor=ap.tensor, offset=ap.offset, ap=[list(d) for d in ap.ap] + [[0, n]])


def backwards(ap):
    d = [list(x) for x in ap.ap]
    step, n = d[-1]
    return bass.AP(tensor=ap.tensor, offset=ap.offset + step * (n - 1), ap=d[:-1] + [[-step, n]])


def twice(ap):
    d = [list(d) for d in ap.ap]
    return bass.AP(tensor=ap.tensor, offset=ap.offset, ap=[d[0], [0, TB], d[1]])


def slabs_before(step, operand):
    n = 0
    for it in ORDER:
        if it == step:
            return n
        if it[0] == "piece" and it[1]["last"] and TILES[it[1]["T"]]["operand"] == operand:
            n = it[1]["slab"] + 1
    raise ValueError(step)


def turned_head(u, i):
    k = kind_of(u)
    if k == "fox":
        return 2 * u + i
    if k == "diff":
        return FOX + u - FOX_P
    return FOX + DIFF + 2 * (u - FOX_P - DIFF_P) + i


def pair_of_turned(j):
    if j < FOX:
        return j // 2
    if j < FOX + DIFF:
        return FOX_P + j - FOX
    return FOX_P + DIFF_P + (j - FOX - DIFF) // 2


def build(nc, A, out):
    ctx = ExitStack()
    with ctx:
        def sem(name):
            return ctx.enter_context(nc.semaphore(name))

        def sb(name, shape, dt=F32, where=None):
            return (where or ctx).enter_context(nc.sbuf_tensor(name, shape, dt))

        PS = ctx.enter_context(nc.psum_tensor("PS", [P, 8, W], F32))
        skew = nc.dram_tensor("skew_dram", [MOBA, SKEW], F32, kind="Internal")

        raw = sb("raw", [P, RAW, 4 * W])
        whi = sb("whi", [P, SPL, 4 * W], F32R)
        wlo = sb("wlo", [P, SPL, 4 * W], F32R)
        hT = sb("hT", [P, 2, KC, S], F32R)
        qT = sb("qT", [P, 2, 2, 2, S], F32R)
        gk = ExitStack()
        kT = sb("kT", [P, 2, 2, S], F32R, gk)
        gk.close()
        pin = sb("pin", [P, TB, W])[:, :, 0:2 * P]
        x = sb("x", [P, TB, D])
        con = sb("con", [P, C_ALIBI])
        identr = sb("identr", [P, P], F32R)
        col = sb("col", [P, V_ALL + 3])
        cond32 = sb("cond32", [P, KC, 32])
        lam = sb("lam", [P, 6])
        expo = sb("expo", [P, 16])
        mod = sb("mod", [P, 3, W])
        nmax = sb("nmax", [P, 2 * PAIRS, TB])
        lsum = sb("lsum", [P, 2 * PAIRS, TB])
        rinv = sb("rinv", [P, 2 * PAIRS, TB])
        nss = sb("nss", [P, 6, TB, 2])
        nrs = sb("nrs", [P, 6, TB])
        nrs2 = sb("nrs2", [P, 6, TB])
        ident = con[:, C_ID:C_ID + P]
        mask = con[:, C_MASK:C_MASK + 2 * P]

        g = ExitStack()
        tok1 = sb("tok1", [P, 6, TB, W], F32, g)
        sq = sb("sq", [P, TB, W], F32, g)
        mixT = sb("mixT", [P, 2, KC, S], F32R, g)
        alibi = sb("alibi", [P, DIFF, 2 * P], F32, g)
        AB = sb("AB", [P, 4, KC], F32, g)
        wfg = sb("wfg", [P, KC, FOX], F32, g)
        wfgs = sb("wfgs", [P, 2, KC, FOX], F32R, g)
        bf = sb("bf", [FOX, 1], F32, g)
        fgt = sb("fgt", [FOX, 4, S], F32, g)
        ones = sb("ones", [FOX, S], F32, g)
        cumq = sb("cumq", [P, TB, FOX], F32, g)
        ncum = sb("ncum", [P, 2, S], F32R, g)
        hss = sb("hss", [P, 4, TB * 8], F32, g)
        hrs = sb("hrs", [P, 4, TB * 8], F32, g)
        dss = sb("dss", [P, TB * DIFF], F32, g)
        drs = sb("drs", [P, TB * DIFF], F32, g)
        g1row = tok1[:, 0].rearrange("p t w -> p (t w)")
        gg = ExitStack()
        vec = sb("vec", [V_ALL, P], F32, gg)
        lamb = sb("lamb", [P, 4, HD], F32, gg)
        lprod = sb("lprod", [P, 2, HD], F32, gg)
        cond = sb("cond", [P, 2, KC], F32, gg)
        hot = sb("hot", [BUCKETS + 1, SKEW], F32, gg)
        table = sb("table", [BUCKETS + 1, MOBA], F32, gg)
        relrow = sb("relrow", [MOBA, SKEW], F32, gg)
        gg.close()
        gg = ExitStack()
        _ = sb("setup_space", [P, 2048], F32, gg)
        xn1 = sb("xn1", [P, TB, D], F32, gg)
        aff1 = sb("aff1", [P, 4, S], F32, gg)
        gg.close()
        gg = ExitStack()
        _2 = sb("cond_space", [P, 2048], F32, gg)
        sc1 = sb("sc1", [P, 2, 3 * P], F32, gg)
        pt1 = sb("pt1", [P, 2, 3 * P], F32, gg)
        od = sb("od", [P, TB, W], F32, gg)
        mcum = sb("mcum", [P, 2, 3 * P], F32, gg)
        gg.close()
        g.close()

        g = ExitStack()
        hidT1 = sb("hidT1", [P, 2, DFF // P, S], F32R, g)
        hid1 = sb("hid1", [P, 2, TB, W], F32, g)
        th1 = sb("th1", [P, TB, W], F32, g)
        xnb = sb("xnb", [P, TB, D], F32, g)
        affb = sb("affb", [P, 4, S], F32, g)
        g2row = sb("g2row", [P, D], F32, g)
        tmpb = affb[:, :, :].rearrange("p c s -> p (c s)").rearrange("p (t w) -> p t w", t=TB)
        g.close()

        g = ExitStack()
        tok2 = sb("tok2", [P, 3, TB, D], F32, g)
        ub = sb("ub", [P, TB, D], F32, g)
        vb = sb("vb", [P, TB, D], F32, g)
        toep = sb("toep", [P, MOBA, 2 * P], F32, g)
        sc2 = sb("sc2", [P, 2, 3 * P], F32, g)
        pt2 = sb("pt2", [P, 2, 3 * P], F32, g)
        wsT = sb("wsT", [P, 8, P], F32, g)
        ws = sb("ws", [P, 8, P], F32, g)
        th2 = ws[:, :, :].rearrange("p g s -> p (g s)").rearrange("p (t w) -> p t w", t=TB)
        ybT = sb("ybT", [P, S], F32, g)
        bn = sb("bn", [P, TB, 2, 6], F32, g)
        mv = sb("mv", [P, TB, 2], F32, g)
        vrs = sb("vrs", [P, TB], F32, g)
        lngb = toep[:, 0:8, :].rearrange("p h k -> p (h k)").rearrange("p (a d) -> p a d", a=2)
        g.close()

        g = ExitStack()
        hid2 = sb("hid2", [P, 2, TB, W], F32, g)
        xnc = sb("xnc", [P, TB, D], F32, g)
        gg = ExitStack()
        hidT2 = sb("hidT2", [P, 2, DFF2 // P, S], F32R, gg)
        gg.close()
        pp = sb("pp", [P, TB, D], F32, g)
        gfin = sb("gfin", [P, D], F32, g)
        fin = sb("fin", [P, TB, D], F32, g)
        thp = sb("thp", [P, 2, TB, W], F32, g)
        pT = qT[:, 0]
        g.close()

        raw_in = [sem(f"raw_in{i}") for i in range(RAW)]
        hi_made, lo_made = sem("hi_made"), sem("lo_made")
        ada_used = sem("ada_used")
        gemm_done = sem("gemm_done")
        cond_in, vec_in, x_in, setup_in = sem("cond_in"), sem("vec_in"), sem("x_in"), sem("setup_in")
        bias_in, gate_w_in, alibi_in = sem("bias_in"), sem("gate_w_in"), sem("alibi_in")
        c_ps, c_col, vec_ps, col_made, cond_th, cond_made = sem("c_ps"), sem("c_col"), sem("vec_ps"), sem("col_made"), sem("cond_th"), sem("cond_made")
        zeroed, expo_made, ident_made = sem("zeroed"), sem("expo_made"), sem("ident_made")
        rel_ps, rel_row, rel_out, rel_in = sem("rel_ps"), sem("rel_row"), sem("rel_out"), sem("rel_in")
        table_set, lam_dot, lam_exp, lam_made = sem("table_set"), sem("lam_dot"), sem("lam_exp"), sem("lam_made")
        mod_in, mod_T, ab_made = sem("mod_in"), sem("mod_T"), sem("ab_made")
        g_ps, g1_row, g2_row = sem("g_ps"), sem("g1_row"), sem("g2_row")
        sums_made, norm_rs = sem("sums_made"), sem("norm_rs")
        xn_act, xn_dve = sem("xn_act"), sem("xn_dve")
        turned, turn_aff, turn_hi, turn_lo = sem("turned"), sem("turn_aff"), sem("turn_hi"), sem("turn_lo")
        wfg_hi, wfg_lo = sem("wfg_hi"), sem("wfg_lo")
        fg_ps, fg_abs, fg_log = sem("fg_ps"), sem("fg_abs"), sem("fg_log")
        cum_made, ncum_hi, ncum_lo, cumq_ps, cumq_in = (
            sem("cum_made"), sem("ncum_hi"), sem("ncum_lo"), sem("cumq_ps"), sem("cumq_in"))
        tok_in, sq_in, hss_in, qk_ready = sem("tok_in"), sem("sq_in"), sem("hss_in"), sem("qk_ready")
        heads_ps, heads_hi, heads_lo = sem("heads_ps"), sem("heads_hi"), sem("heads_lo")
        mcum_in, score_ps, smax, exp_done = sem("mcum_in"), sem("score_ps"), sem("smax"), sem("exp_done")
        fox_p, diff_p, inv_made = sem("fox_p"), sem("diff_p"), sem("inv_made")
        probs_ps, probs_sb, value_ps = sem("probs_ps"), sem("probs_sb"), sem("value_ps")
        mix_hi, mix_lo, od_in, dsq_in = sem("mix_hi"), sem("mix_lo"), sem("od_in"), sem("dsq_in")
        drs_made, od_made = sem("drs_made"), sem("od_made")
        ybT_in, back_ps, yb_in = sem("ybT_in"), sem("back_ps"), sem("yb_in")
        scaled, x_done, hid_in, hid2_in = sem("scaled"), sem("x_done"), sem("hid_in"), sem("hid2_in")
        relu_in, gate_th, ga_th, ple_th = sem("relu_in"), sem("gate_th"), sem("ga_th"), sem("ple_th")
        tok2_in, v_in, u_in, r_in = sem("tok2_in"), sem("v_in"), sem("u_in"), sem("r_in")
        ws_in, ws_low, ws_ps, ws_T = sem("ws_in"), sem("ws_low"), sem("ws_ps"), sem("ws_T")
        ln_in, mv_made, vrs_made, vc_made, vn_made = (
            sem("ln_in"), sem("mv_made"), sem("vrs_made"), sem("vc_made"), sem("vn_made"))
        sgu_ps, ya_in, ga_in, gb_in, merged = sem("sgu_ps"), sem("ya_in"), sem("ga_in"), sem("gb_in"), sem("merged")
        p_in, p_ps, p_hi, p_lo, pp_in, gfin_in = (
            sem("p_in"), sem("p_ps"), sem("p_hi"), sem("p_lo"), sem("pp_in"), sem("gfin_in"))
        out_made, out_done = sem("out_made"), sem("out_done")
        act_step, dve_step, pool_step = sem("act_step"), sem("dve_step"), sem("pool_step")

        def slab_view(t, slot, s):
            m = SLABS[s]
            return t[:, slot, 0:m["chunks"] * m["cols"]]

        def landed(eng, it):
            n = STREAM_AT[it]
            eng.wait_ge(raw_in[n % RAW], 16 * sum(transfers(STREAM[m]) for m in range(n % RAW, n + 1, RAW)))
            return n % RAW

        def bank0(T):
            return 2 * (T % 2)

        def tile_ps(T):
            return PS[:, bank0(T):bank0(T) + TB, 0:TILES[T]["width"]]

        def complete(eng, T):
            eng.wait_ge(gemm_done, LAST_SLAB[T] + 1)

        def tile_readers(T):
            name, n = TILES[T]["name"], TILES[T]["n"]
            if name in ("fox", "diff"):
                j = n + (0 if name == "fox" else 3)
                return [(tok_in, j + 1)] + ([(sq_in, n + 1 + (0 if name == "fox" else 2))] if n < 2 else [])
            if name in ("q", "k", "vatt"):
                return [(tok2_in, 2 * ("q", "k", "vatt").index(name) + n + 1)]
            s, before = {"w_out": (scaled, 0), "down": (scaled, 2), "w_out2": (x_done, 4), "ff2": (x_done, 6),
                         "gate": (r_in, 0), "up": (hid_in, 0), "v": (v_in, 0), "u": (u_in, 0), "ga": (ga_th, 0),
                         "gb": (gb_in, 0), "ff1": (relu_in, 0), "ple_proj": (pp_in, 0), "ple": (ple_th, 0)}[name]
            return [(s, before + n + 1)]

        def turn_banks(q):
            return 4 + 2 * (q % 2 if q >= 2 else 0)

        def turn_of(key):
            kind, n, h = key
            if kind == "norm":
                if n >= 2:
                    return x[:, :, h * W:(h + 1) * W], ((x_done, 2 * n - 1 + h),), hT, 4 * h, 4
                return (xn1, xnb)[n][:, :, h * W:(h + 1) * W], ((xn_act, n + 1), (xn_dve, n + 1)), hT, 4 * h, 4
            if kind == "diff":
                return od[:, :, :], ((od_made, 1),), mixT, 4, 4
            if kind == "merge":
                return tok2[:, 0, :, n * W:(n + 1) * W], ((merged, n + 1),), hT, 4 * n, 4
            if kind == "hid":
                chunks = min(4, DFF // P - 4 * n)
                return hid1[:, n % 2, :, 0:chunks * P], ((hid_in, n + 1),), hidT1, 4 * n, chunks
            return hid2[:, n % 2], ((hid2_in, n + 1),), hidT2, 4 * n, 4

        def gain_of(key, c):
            kind, n, h = key
            if kind == "norm" and n >= 2:
                v = (V_MIX, V_FFN, V_PLE)[n - 2] + 4 * h + c
                return col[:, v:v + 1]
            if kind == "diff":
                return col[:, V_ALL + 2:V_ALL + 3]
            return 0.5 if kind == "merge" else None

        def heads_of(u):
            k = kind_of(u)
            if k == "moba":
                c = (u - FOX_P - DIFF_P) * P
                return tok2[:, 0, :, c:c + P], tok2[:, 1, :, c:c + P], 0.125, 1.0, (tok2_in, 6)
            j = 0 if k == "fox" else 3
            c = (u if k == "fox" else u - FOX_P) * P
            gq, gk = (V_ALL, V_QK + 1) if k == "fox" else (V_ALL + 1, V_QK + 3)
            return (tok1[:, j, :, c:c + P], tok1[:, j + 1, :, c:c + P],
                    col[:, gq:gq + 1], col[:, gk:gk + 1], (qk_ready, 2 if k == "fox" else 4))

        def scores_sb(u):
            return sc2 if kind_of(u) == "moba" else sc1

        def probs_T(u):
            return pt2 if kind_of(u) == "moba" else pt1

        def grow_bank(i):
            return (5, 6)[i]

        def scratch_of(n):
            return (xn1, xnb, xnb, xnc, xnc, fin)[n]

        NSETUP = 4
        NROWS = 11
        QB = ((0, P), (P, 3 * P))

        block = ctx.enter_context(nc.Block())

        @block.sync
        def _(sp):
            sp.dma_start(vec[V_C:V_C + KC, :], A["c"].rearrange("a (r q) -> (a r) q", q=P)).then_inc(cond_in, 16)
            sp.dma_start(con[:, :], A["constants"][:, 0:C_ALIBI]).then_inc(cond_in, 16)
            for n, it in enumerate(STREAM):
                if n >= RAW:
                    kind, i = STREAM[n - RAW]
                    if kind == "ada":
                        sp.wait_ge(ada_used, i + 1)
                    else:
                        sp.wait_ge(lo_made, i + 1)
                if it[0] == "ada":
                    pack, k = divmod(it[1], KC)
                    w, dst = A["w_ada"], raw[:, n % RAW, :]
                    if pack == 0:
                        half, k = divmod(k, 4)
                        for c in range(2):
                            r = (2 * k + c) * P
                            src = w[0, r:r + P, 0:2 * D].rearrange("p (j w) -> p j w", j=2)[:, :, half * W:(half + 1) * W]
                            sp.dma_start(dst[:, 2 * c * W:2 * (c + 1) * W].rearrange("p (j w) -> p j w", j=2), src
                                         ).then_inc(raw_in[n % RAW], 16)
                        continue
                    src = w[0, k * P:(k + 1) * P, pack * 4 * W:(pack + 1) * 4 * W]
                else:
                    m = SLABS[it[1]]
                    src = A[m["weight"]][0, m["row"]:m["row"] + m["chunks"] * P,
                                         m["col"]:m["col"] + m["cols"]].rearrange("(c p) n -> p c n", p=P)
                    dst = slab_view(raw, n % RAW, it[1]).rearrange("p (c n) -> p c n", c=m["chunks"])
                sp.dma_start(dst, src).then_inc(raw_in[n % RAW], 16)
            for t in range(TB):
                sp.wait_ge(out_made, t + 1)
                sp.dma_start(out[0, t * P:(t + 1) * P, :], fin[:, t, :]).then_inc(out_done, 16)
            sp.wait_ge(out_done, 16 * TB)

        @block.tensor
        def _(pe):
            reader = {}

            def take(*banks):
                for b in banks:
                    for s, v in reader.pop(b, ()):
                        pe.wait_ge(s, v)

            def products(out_ap, pairs):
                for n, (a, b) in enumerate(pairs):
                    last = pe.matmul(out_ap, a, b, start=(n == 0), stop=(n == len(pairs) - 1))
                return last

            def operand_ready(T, k):
                name = TILES[T]["operand"]
                if name == "mix":
                    if k < 4:
                        pe.wait_ge(mix_lo, k + 1)
                    else:
                        pe.wait_ge(turn_lo, TURNS[("diff", 0, 0)] + 1)
                elif name == "p":
                    pe.wait_ge(p_lo, 1)
                elif name == "hid":
                    kind = "hid" if TILES[T]["K"] == DFF // P else "hid2"
                    pe.wait_ge(turn_lo, TURNS[(kind, k // 4, 0)] + 1)
                else:
                    tn = TILES[T]["name"]
                    key = {"fox": ("norm", 0), "diff": ("norm", 0), "gate": ("norm", 1), "up": ("norm", 1),
                           "w_out2": ("merge",), "ff1": ("norm", 3), "ple": ("norm", 4)}.get(tn, ("norm", 2))
                    key = ("merge", k // 4, 0) if key == ("merge",) else (*key, k // 4)
                    pe.wait_ge(turn_lo, TURNS[key] + 1)

            def operand(T, k, t):
                name = TILES[T]["operand"]
                big = hidT1 if TILES[T]["K"] == DFF // P else hidT2
                src = {"h": hT, "mix": mixT, "p": pT, "hid": big}[name]
                return src[:, 0, k, t * P:(t + 1) * P], src[:, 1, k, t * P:(t + 1) * P]

            for it in ORDER:
                kind, i = it
                if kind == "piece":
                    T, k, s, off = i["T"], i["k"], i["slab"], i["off"]
                    width = TILES[T]["width"]
                    if i["first"]:
                        pe.wait_ge(hi_made, s + 1)
                        pe.wait_ge(lo_made, s + 1)
                    if k == 0 and T >= 2:
                        for ready in tile_readers(T - 2):
                            pe.wait_ge(*ready)
                    operand_ready(T, k)
                    wh = whi[:, s % SPL, off:off + width]
                    wl = wlo[:, s % SPL, off:off + width]
                    for t in range(TB):
                        ah, al = operand(T, k, t)
                        o = PS[:, bank0(T) + t, 0:width]
                        end = k == TILES[T]["K"] - 1
                        pe.matmul(o, ah, wh, start=(k == 0), stop=False)
                        pe.matmul(o, ah, wl, start=False, stop=False)
                        last = pe.matmul(o, al, wh, start=False, stop=end)
                    if i["last"]:
                        last.then_inc(gemm_done, 1)

                elif kind == "cond":
                    pe.wait_ge(cond_in, 32)
                    pe.transpose(PS[:, 5, 0:KC], vec[0:KC, :], ident[0:KC, 0:KC]).then_inc(c_ps, 1)
                    reader[5] = [(c_col, 1)]

                elif kind == "vectors":
                    pe.wait_ge(vec_in, 16 * NROWS)
                    pe.transpose(PS[:, 4, 0:V_ALL], vec[:, :], ident[0:V_ALL, 0:V_ALL]).then_inc(vec_ps, 1)
                    reader[4] = [(col_made, 1)]

                elif kind == "relbias":
                    pe.wait_ge(table_set, 1)
                    pe.wait_ge(setup_in, 16 * NSETUP)
                    take(5)
                    pe.matmul(PS[0:MOBA, 5, 0:SKEW], table[:, :], hot[:, :], start=True, stop=True).then_inc(rel_ps, 1)
                    reader[5] = [(rel_row, 1)]

                elif kind == "ada":
                    pack, k = divmod(i, KC)
                    if i == 0:
                        pe.wait_ge(cond_made, 1)
                    slot = landed(pe, it)
                    if pack == 0:
                        half, k = divmod(k, 4)
                        if k == 0:
                            take(7 - half)
                        for c in range(2):
                            for j in range(2):
                                r = 64 * half + 32 * j
                                last = pe.matmul(PS[r:r + 32, 7 - half, :], cond32[:, 2 * k + c, :],
                                                 raw[:, slot, (2 * c + j) * W:(2 * c + j + 1) * W],
                                                 start=(k + c == 0), stop=(k == 3 and c == 1))
                        if k == 3:
                            reader[7 - half] = [(mod_in, half + 1)]
                    else:
                        if k == 0:
                            take(7)
                        for j in range(4):
                            last = pe.matmul(PS[32 * j:32 * j + 32, 7, :], cond32[:, k, :],
                                             raw[:, slot, j * W:(j + 1) * W], start=(k == 0), stop=(k == KC - 1))
                        if k == KC - 1:
                            reader[7] = [(mod_in, pack + 2)]
                    last.then_inc(ada_used, 1)

                elif kind == "mod" and i < 2:
                    pe.wait_ge(mod_in, i + 1)
                    take(7 - i)
                    r = slice(64 * i, 64 * i + 64)
                    for c in range(4):
                        last = pe.transpose(PS[:, 7 - i, c * 64:(c + 1) * 64], mod[r, 0, c * P:(c + 1) * P], ident[r, r])
                    last.then_inc(mod_T, 1)
                    reader[7 - i] = [(ab_made, 1 + i)]

                elif kind == "mod":
                    for n, pk in enumerate((1, 2)):
                        pe.wait_ge(mod_in, pk + 2)
                        take(4 + n)
                        for c in range(4):
                            last = pe.transpose(PS[:, 4 + n, c * P:(c + 1) * P], mod[:, pk, c * P:(c + 1) * P], ident)
                    last.then_inc(mod_T, 1)
                    reader[4] = reader[5] = [(ab_made, 3)]

                elif kind == "grow":
                    pe.wait_ge(mod_in, 3 + i)
                    b = grow_bank(i)
                    take(b, b + 1)
                    for j in range(2):
                        r = 32 * (2 * i + j)
                        last = pe.matmul(PS[:, b + j, :], ident[:, r:r + 1].to_broadcast([P, P]), mod[:, 1 + i, :],
                                         start=True, stop=True)
                    last.then_inc(g_ps, 1)
                    reader[b] = reader[b + 1] = [((g1_row, g2_row)[i], 1)]

                elif kind == "turn":
                    q = TURNS[i]
                    src, ready, _, _, chunks = turn_of(i)
                    b = turn_banks(q)
                    take(b, b + 1)
                    for s, v in ready:
                        pe.wait_ge(s, v)
                    for c in range(chunks):
                        for t in range(TB):
                            o = (c % 2) * S + t * P
                            last = pe.transpose(PS[:, b + c // 2, o:o + P], src[:, t, c * P:(c + 1) * P], ident)
                    last.then_inc(turned, 1)
                    reader[b] = reader[b + 1] = [(turn_lo, q + 1)]

                elif kind == "fgate":
                    pe.wait_ge(wfg_lo, 1)
                    pe.wait_ge(turn_lo, TURNS[("norm", 0, 1)] + 1)
                    pe.wait_ge(wfg_hi, 1)
                    take(4)
                    group = []
                    for k in range(KC):
                        wh, wl = wfgs[:, 0, k, :], wfgs[:, 1, k, :]
                        group += [(wh, hT[:, 0, k, :]), (wl, hT[:, 0, k, :]), (wh, hT[:, 1, k, :])]
                    products(PS[0:FOX, 4, 0:S], group).then_inc(fg_ps, 1)
                    reader[4] = [(cum_made, 1)]

                elif kind == "cum":
                    take(5)
                    pe.wait_ge(cum_made, 1)
                    for t in range(TB):
                        last = pe.transpose(PS[:, 5, t * FOX:(t + 1) * FOX], fgt[:, 3, t * P:(t + 1) * P],
                                            ident[0:FOX, 0:FOX])
                    last.then_inc(cumq_ps, 1)
                    reader[5] = [(cumq_in, 1)]

                elif kind == "heads":
                    q, k, _, _, ready = heads_of(i)
                    take(4)
                    pe.wait_ge(*ready)
                    for n, src in enumerate((q, k)):
                        for t in range(TB):
                            last = pe.transpose(PS[:, 4, n * S + t * P:n * S + (t + 1) * P], src[:, t, :], ident)
                    last.then_inc(heads_ps, 1)
                    reader[4] = [(heads_lo, i + 1)]

                elif kind == "scores":
                    u, slot = i, i % 2
                    pe.wait_ge(heads_lo, u + 1)
                    if u == 0:
                        pe.wait_ge(zeroed, 2)
                        pe.wait_ge(ncum_lo, 1)
                    for n in range(2):
                        take(5 + n)
                        for t, (c0, c1) in enumerate(QB):
                            qh, ql = (qT[:, slot, part, n, t * P:(t + 1) * P] for part in range(2))
                            kh, kl = (kT[:, slot, part, 0:c1 - c0] for part in range(2))
                            group = [(qh, kh), (qh, kl), (ql, kh)]
                            if kind_of(u) == "fox":
                                pick = identr[:, 2 * u + n:2 * u + n + 1].to_broadcast([P, P])
                                group += [(pick, ncum[:, part, 0:c1 - c0]) for part in range(2)]
                            last = products(PS[:, 5 + n, c0:c1], group)
                        last.then_inc(score_ps, 1)
                        reader[5 + n] = [(smax, 2 * (2 * u + n) + 2)]

                elif kind == "probsT":
                    u, n = i
                    j = turned_head(u, n)
                    a = 2 * u + n
                    if kind_of(u) == "fox":
                        pe.wait_ge(fox_p, a + 1)
                    elif kind_of(u) == "diff":
                        pe.wait_ge(diff_p, u - FOX_P + 1)
                    else:
                        pe.wait_ge(exp_done, 2 * a + 2)
                    take(4)
                    src = scores_sb(u)
                    for m, c in enumerate((0, P, 2 * P)):
                        last = pe.transpose(PS[:, 4, m * P:(m + 1) * P], src[:, n, c:c + P], ident)
                    last.then_inc(probs_ps, 1)
                    reader[4] = [(probs_sb, j + 1)]

                elif kind == "values":
                    u, kd = i, kind_of(i)
                    pt = probs_T(u)
                    take(5)
                    if kd == "diff":
                        j = turned_head(u, 0)
                        pe.wait_ge(probs_sb, j + 1)
                        pe.wait_ge(tok_in, 6)
                        c = (u - FOX_P) * P
                        v = tok1[:, 5, :, c:c + P]
                        products(PS[:, 5, 0:P], [(pt[:, j % 2, 0:P], v[:, 0, :])])
                        last = products(PS[:, 5, P:2 * P], [(pt[:, j % 2, P:2 * P], v[:, 0, :]),
                                                            (pt[:, j % 2, 2 * P:3 * P], v[:, 1, :])])
                        reader[5] = [(dsq_in, u - FOX_P + 1)]
                    else:
                        for n in range(2):
                            j = turned_head(u, n)
                            pe.wait_ge(probs_sb, j + 1)
                            if kd == "fox":
                                pe.wait_ge(tok_in, 3)
                                v = tok1[:, 2, :, u * P + n * HD:u * P + (n + 1) * HD]
                            else:
                                pe.wait_ge(tok2_in, 6)
                                c = (u - FOX_P - DIFF_P) * P + n * HD
                                v = tok2[:, 2, :, c:c + HD]
                            o = PS[n * HD:(n + 1) * HD, 5, 0:S]
                            pe.matmul(o, v[:, 0, :], pt[:, j % 2, 0:S], start=True, stop=False)
                            last = pe.matmul(o[:, P:S], v[:, 1, :], pt[:, j % 2, S:S + P], start=False, stop=True)
                        reader[5] = [(mix_lo, u + 1)] if kd == "fox" else [(ybT_in, u - FOX_P - DIFF_P + 1)]
                    last.then_inc(value_ps, 1)

                elif kind == "back":
                    m = i - FOX_P - DIFF_P
                    take(4)
                    pe.wait_ge(ybT_in, m + 1)
                    for t in range(TB):
                        last = pe.transpose(PS[:, 4, t * P:(t + 1) * P], ybT[:, t * P:(t + 1) * P], ident)
                    last.then_inc(back_ps, 1)
                    reader[4] = [(yb_in, m + 1)]

                elif kind == "spatial":
                    pe.wait_ge(ws_low, 1)
                    take(4, 5)
                    for gr in range(8):
                        last = pe.transpose(PS[:, 4 + gr // 4, (gr % 4) * P:(gr % 4 + 1) * P], ws[:, gr, :], ident)
                    last.then_inc(ws_ps, 1)
                    reader[4] = reader[5] = [(ws_T, 1)]

                elif kind == "sgu":
                    b = 4 + 2 * i
                    take(b, b + 1)
                    pe.wait_ge(vn_made, TB)
                    pe.wait_ge(ws_T, 1)
                    for gr in range(4 * i, 4 * i + 4):
                        o = (gr % 2) * S
                        last = pe.matmul(PS[:, b + gr % 4 // 2, o:o + S].rearrange("p (t c) -> p t c", t=TB),
                                         wsT[:, gr, :], vb[:, :, gr * P:(gr + 1) * P], start=True, stop=True)
                    last.then_inc(sgu_ps, 1)
                    reader[b] = reader[b + 1] = [(ya_in, i + 1)]

                elif kind == "pT":
                    pe.wait_ge(p_in, 16)
                    take(4)
                    for c in range(2):
                        for t in range(TB):
                            last = pe.transpose(PS[:, 4, c * S + t * P:c * S + (t + 1) * P],
                                                pin[:, t, c * P:(c + 1) * P], ident)
                    last.then_inc(p_ps, 1)
                    reader[4] = [(p_lo, 1)]

        @block.scalar
        def _(act):
            own = 0
            act.dma_start(x[:, :, :], A["x"][0].rearrange("(t p) d -> p t d", p=P)).then_inc(x_in, 16)
            for n, v in (("ln1_g", V_LN1), ("ln2_g", V_LN2), ("norm_mix_g_2", V_MIX), ("norm_ffn_g_2", V_FFN),
                         ("norm_ple_g_2", V_PLE), ("b_sgu_spatial_2", V_BS)):
                src = A[n].rearrange("a b c -> (a b c)") if len(A[n].shape) == 3 else A[n].rearrange("a b -> (a b)")
                act.dma_start(vec[v:v + KC, :], src.rearrange("(r q) -> r q", q=P)).then_inc(vec_in, 16)
            for n, r in (("fox_qk_g", V_QK), ("diff_qk_g", V_QK + 2)):
                for h in range(2):
                    act.dma_start(vec[r:r + 2, h * HD:(h + 1) * HD], A[n][0]).then_inc(vec_in, 16)
            act.dma_start(vec[V_DN:V_DN + 1, :], A["diff_norm_g"]).then_inc(vec_in, 16)
            for it in ORDER:
                kind, i = it
                if kind == "split":
                    slot = landed(act, it)
                    if i >= SPL:
                        act.wait_ge(gemm_done, i - SPL + 1)
                    act.activation(slab_view(whi, i % SPL, i), slab_view(raw, slot, i), ACT.Copy).then_inc(hi_made, 1)

                elif kind == "cond":
                    act.wait_ge(c_col, 1)
                    act.activation(cond[:, 0, :], col[:, V_C:V_C + KC], ACT.Tanh, scale=0.5).then_inc(cond_th, 1)

                    act.dma_start(wfg[:, :, :], A["w_in"][0, :, 3 * W:3 * W + FOX].rearrange("(c p) h -> p c h", p=P)
                                  ).then_inc(gate_w_in, 16)
                    act.dma_start(alibi[:, :, :], A["constants"][:, C_ALIBI:C_HOT].rearrange("p (h k) -> p h k", h=DIFF)
                                  ).then_inc(alibi_in, 16)

                elif kind == "setup":
                    act.wait_ge(lam_dot, 1)
                    act.activation(lam[:, 2:4], lam[:, 0:2], ACT.Exp).then_inc(lam_exp, 1)
                    act.wait_ge(gate_w_in, 16)
                    act.activation(wfgs[:, 0], wfg[:, :, :], ACT.Copy).then_inc(wfg_hi, 1)

                elif kind == "grow":
                    act.wait_ge(g_ps, i + 1)
                    row = g1row if i == 0 else g2row[:, :]
                    act.activation(row.rearrange("p (j w) -> p j w", j=2), PS[:, grow_bank(i):grow_bank(i) + 2, :], ACT.Copy
                                   ).then_inc((g1_row, g2_row)[i], 1)

                elif kind == "sums":
                    n, h = i
                    if n == 0:
                        act.wait_ge(x_in, 16)
                    else:
                        act.wait_ge(x_done, 2 * n - 1 + h)
                    if n == 1:
                        act.wait_ge(rel_out, 16)
                    for t in range(TB):
                        last = act.activation(scratch_of(n)[:, t, h * W:(h + 1) * W], x[:, t, h * W:(h + 1) * W],
                                              ACT.Square, accum_out=nss[:, n, t, h:h + 1])
                    last.then_inc(sums_made, 1)

                elif kind == "norm" and i < 2:
                    act.wait_ge(norm_rs, i + 1)
                    act.activation((xn1, xnb)[i][:, 0, :], x[:, 0, :], ACT.Copy, scale=nrs[:, i, 0:1]).then_inc(xn_act, 1)

                elif kind == "turn":
                    q = TURNS[i]
                    _, _, dst, c0, chunks = turn_of(i)
                    b = turn_banks(q)
                    name = {"diff": "mix"}.get(i[0], "h" if i[0] in ("norm", "merge") else "hid")
                    if name == "h" and slabs_before(it, "h"):
                        act.wait_ge(gemm_done, slabs_before(it, "h"))
                    ps = PS[:, b:b + chunks // 2, :]
                    to = dst[:, 0, c0:c0 + chunks, :].rearrange("p (a c) s -> p a (c s)", c=2)
                    if i[0] == "norm" and i[1] < 2:
                        act.wait_ge(turn_aff, q_affine(i) + 1)
                        aff = aff1 if i[1] == 0 else affb
                        act.activation(dst[:, 0, c0:c0 + 4, :], aff[:, :, :], ACT.Copy).then_inc(turn_hi, 1)
                    else:
                        act.wait_ge(turned, q + 1)
                        gain = gain_of(i, 0)
                        if gain is None or isinstance(gain, float):
                            act.activation(to, ps, ACT.Copy, scale=1.0 if gain is None else gain).then_inc(turn_hi, 1)
                        else:
                            for c in range(chunks):
                                last = act.activation(dst[:, 0, c0 + c, :], PS[:, b + c // 2, c % 2 * S:(c % 2 + 1) * S],
                                                      ACT.Copy, scale=gain_of(i, c))
                            last.then_inc(turn_hi, 1)

                elif kind == "fgate":
                    act.wait_ge(fg_abs, 2)
                    act.activation(fgt[:, 1, :], fgt[:, 1, :], ACT.Exp).then_inc(act_step, 1)
                    own += 1
                    act.wait_ge(act_step, own)
                    act.activation(fgt[:, 1, :], fgt[:, 1, :], ACT.Ln, bias=1.0).then_inc(fg_log, 1)
                    act.wait_ge(cum_made, 1)
                    act.wait_ge(zeroed, 2)
                    act.activation(ncum[0:FOX, 0, :], fgt[:, 3, :], ACT.Copy, scale=-1.0).then_inc(ncum_hi, 1)

                elif kind == "heads":
                    u, slot = i, i % 2
                    _, _, gq, gk, _ = heads_of(u)
                    act.wait_ge(heads_ps, u + 1)
                    act.wait_ge(zeroed, 2)
                    if u >= 2:
                        act.wait_ge(score_ps, 2 * (u - 1))
                    for n in range(2):
                        r = slice(n * HD, (n + 1) * HD)
                        act.activation(qT[r, slot, 0, n, :], PS[r, 4, 0:S], ACT.Copy,
                                       scale=gq if isinstance(gq, float) else gq[r, :])
                    act.activation(kT[:, slot, 0, :], PS[:, 4, S:2 * S], ACT.Copy, scale=gk).then_inc(heads_hi, 1)

                elif kind == "scores":
                    sc = scores_sb(i)
                    for n in range(2):
                        a = 2 * i + n
                        for t, (c0, c1) in enumerate(QB):
                            act.wait_ge(smax, 2 * a + t + 1)
                            act.activation(sc[:, n, c0:c1], sc[:, n, c0:c1], ACT.Exp, bias=nmax[:, a, t:t + 1],
                                           scale=-1.0, accum_out=lsum[:, a, t:t + 1]).then_inc(exp_done, 1)

                elif kind == "probsT":
                    u, n = i
                    j = turned_head(u, n)
                    act.wait_ge(probs_ps, j + 1)
                    if j >= 2:
                        act.wait_ge(value_ps, pair_of_turned(j - 2) + 1)
                    act.activation(probs_T(u)[:, j % 2, :], PS[:, 4, 0:3 * P], ACT.Copy).then_inc(probs_sb, 1)

                elif kind == "values":
                    u, kd = i, kind_of(i)
                    act.wait_ge(value_ps, u + 1)
                    if kd == "fox":
                        act.activation(mixT[:, 0, u, :], PS[:, 5, 0:S], ACT.Copy).then_inc(mix_hi, 1)
                    elif kd == "moba":
                        m = u - FOX_P - DIFF_P
                        if m >= 1:
                            act.wait_ge(back_ps, m)
                        act.activation(ybT[:, :], PS[:, 5, 0:S], ACT.Copy).then_inc(ybT_in, 1)
                    else:
                        h = u - FOX_P
                        act.wait_ge(od_in, h + 1)
                        for t in range(TB):
                            c = t * DIFF + h
                            last = act.activation(sq[:, t, h * P:(h + 1) * P], PS[:, 5, t * P:(t + 1) * P], ACT.Square,
                                                  accum_out=dss[:, c:c + 1])
                        last.then_inc(dsq_in, 1)

                elif kind == "spatial":
                    act.wait_ge(ws_ps, 1)
                    act.activation(wsT[:, :, :].rearrange("p (b g) s -> p b (g s)", b=2), PS[:, 4:6, :], ACT.Copy
                                   ).then_inc(ws_T, 1)

                elif kind == "pT":
                    act.wait_ge(p_ps, 1)
                    act.activation(pT[:, 0].rearrange("p c s -> p (c s)"), PS[:, 4, :], ACT.Copy).then_inc(p_hi, 1)

                elif kind == "evac":
                    T = i
                    name, n, width = TILES[T]["name"], TILES[T]["n"], TILES[T]["width"]
                    ps, cols = tile_ps(T), slice(n * W, (n + 1) * W)
                    rs, half_rs = nrs, nrs2

                    def rows(out, func, factor, n):
                        act.wait_ge(norm_rs, n + 1)
                        for t in range(TB):
                            last = act.activation(out[:, t, :], PS[:, bank0(T) + t, :], func, scale=factor[:, n, t:t + 1])
                        return last

                    if name in ("fox", "diff", "v", "u", "q", "k", "vatt", "ga", "gb", "gate", "ff1", "ple_proj", "ple"):
                        complete(act, T)
                    if name in ("fox", "diff"):
                        j = n + (0 if name == "fox" else 3)
                        act.activation(tok1[:, j], ps, ACT.Copy).then_inc(tok_in, 1)
                        if n < 2:
                            m = n + (0 if name == "fox" else 2)
                            if m:
                                act.wait_ge(hss_in, m)
                            act.activation(sq[:, :, :], ps, ACT.Square).then_inc(sq_in, 1)
                    elif name == "v":
                        rows(vb[:, :, cols], ACT.Gelu_apprx_tanh, rs, 2).then_inc(v_in, 1)
                    elif name == "u":
                        rows(ub[:, :, cols], ACT.Gelu_apprx_tanh, rs, 2).then_inc(u_in, 1)
                    elif name in ("q", "k", "vatt"):
                        j = ("q", "k", "vatt").index(name)
                        rows(tok2[:, j, :, cols], ACT.Copy, rs, 2).then_inc(tok2_in, 1)
                    elif name == "ga":
                        if n == 0:
                            act.wait_ge(ws_T, 1)
                            act.wait_ge(ws_ps, 1)
                        else:
                            act.wait_ge(ga_in, 1)
                        rows(th2, ACT.Tanh, half_rs, 2).then_inc(ga_th, 1)
                    elif name == "gb":
                        act.wait_ge(sgu_ps, 2)
                        rows(vb[:, :, cols], ACT.Tanh, half_rs, 2).then_inc(gb_in, 1)
                    elif name == "gate":
                        if n:
                            act.wait_ge(r_in, n)
                        act.activation(th1[:, :, 0:width], ps, ACT.Tanh, scale=0.5).then_inc(gate_th, 1)
                    elif name == "ff1":
                        if n >= 2:
                            act.wait_ge(turned, TURNS[("hid2", n - 2, 0)] + 1)
                        act.activation(hid2[:, n % 2], ps, ACT.Relu).then_inc(relu_in, 1)
                    elif name == "ple_proj":
                        act.activation(pp[:, :, cols], ps, ACT.Copy).then_inc(pp_in, 1)
                    elif name == "ple":
                        rows(thp[:, n], ACT.Tanh, half_rs, 4).then_inc(ple_th, 1)

        @block.vector
        def _(dve):
            own = [0]

            def then(ins):
                ins.then_inc(dve_step, 1)
                own[0] += 1
                dve.wait_ge(dve_step, own[0])

            def whole(t):
                return t.bitcast(F32)

            dve.memset(table[BUCKETS:BUCKETS + 1, :], MASKED).then_inc(table_set, 1)

            for it in ORDER:
                kind, i = it
                if kind == "split":
                    slot = landed(dve, it)
                    dve.wait_ge(hi_made, i + 1)
                    if i >= SPL:
                        dve.wait_ge(gemm_done, i - SPL + 1)
                    dve.tensor_tensor(slab_view(wlo, i % SPL, i), slab_view(raw, slot, i),
                                      whole(slab_view(whi, i % SPL, i)), ALU.subtract).then_inc(lo_made, 1)

                elif kind == "cond":
                    dve.wait_ge(c_ps, 1)
                    dve.tensor_copy(col[:, V_C:V_C + KC], PS[:, 5, 0:KC]).then_inc(c_col, 1)
                    dve.wait_ge(c_col, 1)
                    dve.wait_ge(cond_th, 1)
                    then(dve.scalar_tensor_tensor(out=cond[:, 1, :], in0=cond[:, 0, :], scalar=1.0,
                                                  in1=col[:, V_C:V_C + KC], op0=ALU.add, op1=ALU.mult))
                    dve.tensor_scalar(cond32[:, :, :], spread(cond[:, 1, :], 32), 0.5, None, ALU.mult
                                      ).then_inc(cond_made, 1)

                elif kind == "vectors":
                    dve.wait_ge(vec_ps, 1)
                    then(dve.tensor_copy(col[:, V_LN1:V_ALL], PS[:, 4, V_LN1:V_ALL]))
                    dve.tensor_scalar(col[:, V_ALL:V_ALL + 1], col[:, V_QK:V_QK + 1], HD ** -0.5, None, ALU.mult)
                    dve.tensor_scalar(col[:, V_ALL + 1:V_ALL + 2], col[:, V_QK + 2:V_QK + 3], HD ** -0.5, None, ALU.mult)
                    dve.tensor_scalar(col[:, V_ALL + 2:V_ALL + 3], col[:, V_DN:V_DN + 1], 1.0 - LAM_INIT, None,
                                      ALU.mult).then_inc(col_made, 1)

                elif kind == "setup":
                    dve.wait_ge(cond_in, 32)
                    dve.tensor_copy(identr[:, :], ident).then_inc(ident_made, 1)
                    dve.wait_ge(setup_in, 16 * NSETUP)
                    dve.memset(ones[:, :], 1.0)
                    for n in range(2):
                        last = dve.tensor_tensor_reduce(lprod[:, n, :], lamb[:, 2 * n, :], lamb[:, 2 * n + 1, :],
                                                        1.0, 0.0, ALU.mult, ALU.add, lam[:, n:n + 1])
                    last.then_inc(lam_dot, 1)
                    dve.wait_ge(lam_exp, 1)
                    dve.scalar_tensor_tensor(out=lam[:, 4:5], in0=lam[:, 2:3], scalar=LAM_INIT, in1=lam[:, 3:4],
                                             op0=ALU.add, op1=ALU.subtract).then_inc(lam_made, 1)
                    dve.wait_ge(gate_w_in, 16)
                    dve.wait_ge(wfg_hi, 1)
                    dve.tensor_tensor(wfgs[:, 1], wfg[:, :, :], whole(wfgs[:, 0]), ALU.subtract).then_inc(wfg_lo, 1)

                elif kind == "relbias":
                    dve.wait_ge(rel_ps, 1)
                    dve.tensor_copy(relrow[:, :], PS[0:MOBA, 5, 0:SKEW]).then_inc(rel_row, 1)

                elif kind == "ada" and (i % KC == KC - 1 or i == 3):
                    if i == 3:
                        dve.wait_ge(bias_in, 16 * 8)
                    dve.wait_ge(ada_used, i + 1)
                    if i < KC:
                        half = i // 4
                        r = slice(64 * half, 64 * half + 64)
                        dve.tensor_tensor(mod[r, 0, :], PS[r, 7 - half, :], mod[r, 0, :], ALU.add).then_inc(mod_in, 1)
                    else:
                        pack = i // KC
                        dve.tensor_tensor(mod[:, pack, :], PS[:, 7, :], mod[:, pack, :], ALU.add).then_inc(mod_in, 1)

                elif kind == "mod":
                    dve.wait_ge(mod_T, i + 1)
                    if i < 2:
                        k = slice(4 * i, 4 * i + 4)
                        both = PS[:, 7 - i, 0:S].rearrange("p (c j r) -> p c j r", c=4, j=2)
                        if i == 0:
                            dve.wait_ge(col_made, 1)
                        dve.tensor_copy(AB[:, 1, k], both[:, :, 0, 0])
                        dve.scalar_tensor_tensor(out=AB[:, 0, k], in0=both[:, :, 1, 0], scalar=1.0,
                                                 in1=col[:, V_LN1 + 4 * i:V_LN1 + 4 * i + 4], op0=ALU.add, op1=ALU.mult
                                                 ).then_inc(ab_made, 1)
                    else:
                        def columns(b, j0):
                            return PS[:, b, :].rearrange("p (c j r) -> p j c r", c=4, j=4)[:, j0:j0 + 2, :, 0]

                        dve.tensor_copy(AB[:, 3, :].rearrange("p (j c) -> p j c", j=2), columns(4, 2))
                        dve.scalar_tensor_tensor(out=AB[:, 2, :].rearrange("p (j c) -> p j c", j=2), in0=columns(5, 0),
                                                 scalar=1.0,
                                                 in1=col[:, V_LN2:V_LN2 + KC].rearrange("p (j c) -> p j c", j=2),
                                                 op0=ALU.add, op1=ALU.mult).then_inc(ab_made, 1)

                elif kind == "norm" and i < 2:
                    dve.wait_ge(norm_rs, i + 1)
                    dve.tensor_scalar((xn1, xnb)[i][:, 1, :], x[:, 1, :], nrs[:, i, 1:2], None, ALU.mult
                                      ).then_inc(xn_dve, 1)

                elif kind == "final":
                    dve.wait_ge(norm_rs, 6)
                    dve.wait_ge(gfin_in, 16)
                    for t in range(TB):
                        dve.scalar_tensor_tensor(out=fin[:, t, :], in0=x[:, t, :], scalar=nrs[:, 5, t:t + 1],
                                                 in1=gfin[:, :], op0=ALU.mult, op1=ALU.mult).then_inc(out_made, 1)

                elif kind == "turn":
                    q = TURNS[i]
                    _, _, dst, c0, chunks = turn_of(i)
                    b = turn_banks(q)
                    name = "h" if i[0] in ("norm", "merge") else "other"
                    if name == "h" and slabs_before(it, "h"):
                        dve.wait_ge(gemm_done, slabs_before(it, "h"))
                    dve.wait_ge(turned, q + 1)
                    lo = dst[:, 1, c0:c0 + chunks, :]
                    hi = whole(dst[:, 0, c0:c0 + chunks, :])
                    if i[0] == "norm" and i[1] < 2:
                        aff = aff1 if i[1] == 0 else affb
                        dve.wait_ge(ab_made, 1 + i[2] if i[1] == 0 else 3)
                        if i[2]:
                            dve.wait_ge(turn_lo, q)
                        for c in range(4):
                            k = c0 + c
                            last = dve.tensor_scalar(aff[:, c, :], PS[:, b + c // 2, c % 2 * S:(c % 2 + 1) * S],
                                                     AB[:, 2 * i[1], k:k + 1], AB[:, 2 * i[1] + 1, k:k + 1],
                                                     ALU.mult, ALU.add)
                        last.then_inc(turn_aff, 1)
                        dve.wait_ge(turn_hi, q + 1)
                        dve.wait_ge(turn_aff, q_affine(i) + 1)
                        dve.tensor_tensor(lo, aff[:, :, :], hi, ALU.subtract).then_inc(turn_lo, 1)
                    else:
                        dve.wait_ge(turn_hi, q + 1)
                        gain = gain_of(i, 0)
                        if gain is None or isinstance(gain, float):
                            ps = PS[:, b:b + chunks // 2, :]
                            dve.scalar_tensor_tensor(out=lo.rearrange("p (a c) s -> p a (c s)", c=2), in0=ps,
                                                     scalar=1.0 if gain is None else gain,
                                                     in1=hi.rearrange("p (a c) s -> p a (c s)", c=2),
                                                     op0=ALU.mult, op1=ALU.subtract).then_inc(turn_lo, 1)
                        else:
                            for c in range(chunks):
                                last = dve.scalar_tensor_tensor(out=lo[:, c, :], in0=PS[:, b + c // 2, c % 2 * S:(c % 2 + 1) * S],
                                                                scalar=gain_of(i, c), in1=hi[:, c, :],
                                                                op0=ALU.mult, op1=ALU.subtract)
                            last.then_inc(turn_lo, 1)

                elif kind == "fgate":
                    dve.wait_ge(fg_ps, 1)
                    dve.tensor_scalar(fgt[:, 0, :], PS[0:FOX, 4, 0:S], bf[:, :], None, ALU.add).then_inc(fg_abs, 1)
                    dve.wait_ge(fg_abs, 1)
                    dve.scalar_tensor_tensor(out=fgt[:, 1, :], in0=fgt[:, 0, :], scalar=-1.0, in1=fgt[:, 0, :],
                                             op0=ALU.mult, op1=ALU.min).then_inc(fg_abs, 1)
                    dve.wait_ge(fg_log, 1)
                    then(dve.scalar_tensor_tensor(out=fgt[:, 2, :], in0=fgt[:, 0, :], scalar=0.0, in1=fgt[:, 1, :],
                                                  op0=ALU.min, op1=ALU.subtract))
                    dve.tensor_tensor_scan(fgt[:, 3, :], ones[:, :], fgt[:, 2, :], 0.0, ALU.mult, ALU.add
                                           ).then_inc(cum_made, 1)
                    dve.wait_ge(ncum_hi, 1)
                    dve.wait_ge(cum_made, 1)
                    dve.scalar_tensor_tensor(out=ncum[0:FOX, 1, :], in0=fgt[:, 3, :], scalar=-1.0,
                                             in1=whole(ncum[0:FOX, 0, :]), op0=ALU.mult, op1=ALU.subtract
                                             ).then_inc(ncum_lo, 1)

                elif kind == "cum":
                    dve.wait_ge(cumq_ps, 1)
                    dve.tensor_copy(cumq[:, :, :].rearrange("p t h -> p (t h)"), PS[:, 5, 0:TB * FOX]).then_inc(cumq_in, 1)

                elif kind == "heads":
                    u, slot = i, i % 2
                    _, _, gq, gk, _ = heads_of(u)
                    dve.wait_ge(heads_ps, u + 1)
                    dve.wait_ge(heads_hi, u + 1)
                    for n in range(2):
                        r = slice(n * HD, (n + 1) * HD)
                        dve.scalar_tensor_tensor(out=qT[r, slot, 1, n, :], in0=PS[r, 4, 0:S],
                                                 scalar=gq if isinstance(gq, float) else gq[r, :],
                                                 in1=whole(qT[r, slot, 0, n, :]), op0=ALU.mult, op1=ALU.subtract)
                    dve.scalar_tensor_tensor(out=kT[:, slot, 1, :], in0=PS[:, 4, S:2 * S], scalar=gk,
                                             in1=whole(kT[:, slot, 0, :]), op0=ALU.mult, op1=ALU.subtract
                                             ).then_inc(heads_lo, 1)

                elif kind == "scores":
                    u, kd, sc = i, kind_of(i), scores_sb(i)
                    for n in range(2):
                        a = 2 * u + n
                        dve.wait_ge(score_ps, a + 1)
                        if u and kd == kind_of(u - 1) or kd == "diff":
                            dve.wait_ge(probs_ps, turned_head(u - 1, n if kind_of(u - 1) != "diff" else 0) + 1)
                        if kd == "fox":
                            dve.wait_ge(mcum_in, a + 1)
                            bias = [mcum[:, a % 2, c0:c1] for c0, c1 in QB]
                        elif kd == "diff":
                            dve.wait_ge(alibi_in, 16)
                            bias = [alibi[:, u - FOX_P, P:2 * P], alibi[:, u - FOX_P, :]]
                        else:
                            if u == FOX_P + DIFF_P:
                                dve.wait_ge(rel_in, 16)
                            h = a - 2 * (FOX_P + DIFF_P)
                            bias = [toep[:, h, 0:P], toep[:, h, :]]
                        for t, (c0, c1) in enumerate(QB):
                            made, score = sc[:, n, c0:c1], PS[:, 5 + n, c0:c1]
                            if kd == "moba":
                                made, score = backwards(made), backwards(score)
                            dve.tensor_tensor_reduce(made, score, bias[t], -1.0, 3e38,
                                                     ALU.add, ALU.min, nmax[:, a, t:t + 1]).then_inc(smax, 1)
                    for n in range(2):
                        a = 2 * u + n
                        dve.wait_ge(exp_done, 2 * a + 2)
                        then(dve.reciprocal(rinv[:, a, :], lsum[:, a, :]))
                        if kd == "fox":
                            for t, (c0, c1) in enumerate(QB):
                                last = dve.tensor_scalar(sc[:, n, c0:c1], sc[:, n, c0:c1], rinv[:, a, t:t + 1], None,
                                                         ALU.mult)
                            last.then_inc(fox_p, 1)
                    if kd == "diff":
                        a = 2 * u
                        if u == FOX_P:
                            dve.wait_ge(lam_made, 1)
                        then(dve.tensor_scalar(rinv[:, a + 1, :], rinv[:, a + 1, :], lam[:, 4:5], None, ALU.mult))
                        for t, (c0, c1) in enumerate(QB):
                            last = dve.tensor_scalar(sc[:, 1, c0:c1], sc[:, 1, c0:c1], rinv[:, a + 1, t:t + 1], None,
                                                     ALU.mult)
                        then(last)
                        for t, (c0, c1) in enumerate(QB):
                            last = dve.scalar_tensor_tensor(out=sc[:, 0, c0:c1], in0=sc[:, 0, c0:c1],
                                                            scalar=rinv[:, a, t:t + 1], in1=sc[:, 1, c0:c1],
                                                            op0=ALU.mult, op1=ALU.subtract)
                        last.then_inc(diff_p, 1)

                elif kind == "values":
                    u, kd = i, kind_of(i)
                    if kd == "fox":
                        dve.wait_ge(value_ps, u + 1)
                        dve.wait_ge(mix_hi, u + 1)
                        dve.tensor_tensor(mixT[:, 1, u, :], PS[:, 5, 0:S], whole(mixT[:, 0, u, :]), ALU.subtract
                                          ).then_inc(mix_lo, 1)
                    elif kd == "diff":
                        h = u - FOX_P
                        dve.wait_ge(value_ps, u + 1)
                        dve.tensor_copy(od[:, :, h * P:(h + 1) * P], PS[:, 5, 0:S].rearrange("p (t d) -> p t d", t=TB)
                                        ).then_inc(od_in, 1)

                elif kind == "diffnorm":
                    dve.wait_ge(drs_made, 1)
                    dve.wait_ge(od_in, DIFF)
                    o = od[:, :, :].rearrange("p t (h d) -> p (t h) d", h=DIFF)
                    dve.tensor_tensor(o, o, spread(drs[:, :], P), ALU.mult).then_inc(od_made, 1)

                elif kind == "back":
                    m = i - FOX_P - DIFF_P
                    dve.wait_ge(back_ps, m + 1)
                    inv = rinv[:, 2 * i:2 * i + 2, :].rearrange("p n t -> p t n")
                    dve.tensor_tensor(tok2[:, 0, :, m * P:(m + 1) * P].rearrange("p t (n d) -> p t n d", n=2),
                                      PS[:, 4, 0:S].rearrange("p (t n d) -> p t n d", t=TB, n=2), spread(inv, HD),
                                      ALU.mult).then_inc(yb_in, 1)

                elif kind == "layernorm":
                    dve.wait_ge(v_in, 2)
                    for t in range(TB):
                        for h in range(2):
                            last = dve.bn_stats(bn[:, t, h, :], vb[:, t, h * W:(h + 1) * W])
                    then(last)
                    for t in range(TB):
                        last = dve.bn_aggr(mv[:, t, :], bn[:, t].rearrange("p h s -> p (h s)"))
                    last.then_inc(mv_made, 1)
                    dve.wait_ge(mv_made, 1)
                    dve.wait_ge(vrs_made, 1)
                    for t in range(TB):
                        dve.tensor_scalar(vb[:, t, :], vb[:, t, :], mv[:, t, 0:1], vrs[:, t:t + 1],
                                          ALU.subtract, ALU.mult).then_inc(vc_made, 1)

                elif kind == "sgu":
                    dve.wait_ge(u_in, 2)
                    dve.wait_ge(sgu_ps, i + 1)
                    b = 4 + 2 * i
                    for gr in range(4 * i, 4 * i + 4):
                        c = (gr % 2) * S
                        uc = ub[:, :, gr * P:(gr + 1) * P]
                        last = dve.scalar_tensor_tensor(
                            out=uc, in0=PS[:, b + gr % 4 // 2, c:c + S].rearrange("p (t c) -> p t c", t=TB),
                            scalar=col[:, V_BS + gr:V_BS + gr + 1], in1=uc, op0=ALU.add, op1=ALU.mult)
                    last.then_inc(ya_in, 1)

                elif kind == "merge":
                    cols = slice(i * W, (i + 1) * W)
                    y = tok2[:, 0, :, cols]
                    dve.wait_ge(yb_in, 4 * (i + 1))
                    dve.wait_ge(gb_in, i + 1)
                    dve.wait_ge(ga_in, i + 1)
                    then(dve.scalar_tensor_tensor(out=y, in0=vb[:, :, cols], scalar=1.0, in1=y, op0=ALU.add,
                                                  op1=ALU.mult))
                    dve.tensor_tensor(y, y, ub[:, :, cols], ALU.add).then_inc(merged, 1)

                elif kind == "pT":
                    dve.wait_ge(p_ps, 1)
                    dve.wait_ge(p_hi, 1)
                    dve.tensor_tensor(pT[:, 1].rearrange("p c s -> p (c s)"), PS[:, 4, :],
                                      whole(pT[:, 0]).rearrange("p c s -> p (c s)"), ALU.subtract).then_inc(p_lo, 1)

                elif kind == "evac":
                    T = i
                    name, n, width = TILES[T]["name"], TILES[T]["n"], TILES[T]["width"]
                    ps, cols = tile_ps(T), slice(n * W, (n + 1) * W)
                    if name in ("fox", "diff") and n < 2:
                        m = n + (0 if name == "fox" else 2)
                        dve.wait_ge(sq_in, m + 1)
                        dve.tensor_reduce(hss[:, m, :], sq[:, :, :].rearrange("p t (h d) -> p (t h) d", d=HD), AX,
                                          ALU.add).then_inc(hss_in, 1)
                    elif name in ("w_out", "down"):
                        row, tmp, m = (g1row, sq, n) if name == "w_out" else (g2row[:, :], tmpb, 2 + n)
                        dve.wait_ge(g1_row if name == "w_out" else g2_row, 1)
                        complete(dve, T)
                        if name == "w_out":
                            dve.wait_ge(dsq_in, DIFF)
                        if n:
                            dve.wait_ge(x_done, m)
                        dve.tensor_tensor(tmp[:, :, :], ps, twice(row[:, cols]), ALU.mult).then_inc(scaled, 1)
                        dve.wait_ge(scaled, m + 1)
                        dve.tensor_tensor(x[:, :, cols], x[:, :, cols], tmp[:, :, :], ALU.add).then_inc(x_done, 1)
                    elif name == "w_out2":
                        complete(dve, T)
                        dve.tensor_tensor(x[:, :, cols], x[:, :, cols], ps, ALU.add).then_inc(x_done, 1)
                    elif name == "ff2":
                        complete(dve, T)
                        dve.wait_ge(norm_rs, 4)
                        for t in range(TB):
                            last = dve.scalar_tensor_tensor(out=x[:, t, cols], in0=PS[:, bank0(T) + t, :],
                                                            scalar=nrs2[:, 3, t:t + 1], in1=x[:, t, cols],
                                                            op0=ALU.mult, op1=ALU.add)
                        last.then_inc(x_done, 1)
                    elif name == "gate":
                        dve.wait_ge(gate_th, n + 1)
                        th = th1[:, :, 0:width]
                        dve.scalar_tensor_tensor(out=hid1[:, n % 2, :, 0:width], in0=th, scalar=1.0, in1=ps,
                                                 op0=ALU.add, op1=ALU.mult).then_inc(r_in, 1)
                    elif name == "up":
                        complete(dve, T)
                        dve.wait_ge(r_in, n + 1)
                        o = hid1[:, n % 2, :, 0:width]
                        dve.scalar_tensor_tensor(out=o, in0=o, scalar=0.5, in1=ps, op0=ALU.mult, op1=ALU.mult
                                                 ).then_inc(hid_in, 1)
                    elif name == "ga":
                        dve.wait_ge(ga_th, n + 1)
                        dve.wait_ge(ya_in, 2)
                        uc = ub[:, :, cols]
                        dve.scalar_tensor_tensor(out=uc, in0=th2, scalar=1.0, in1=uc, op0=ALU.add, op1=ALU.mult
                                                 ).then_inc(ga_in, 1)
                    elif name == "ff1":
                        dve.wait_ge(relu_in, n + 1)
                        h = hid2[:, n % 2]
                        dve.tensor_tensor(h, h, h, ALU.mult).then_inc(hid2_in, 1)
                    elif name == "ple":
                        dve.wait_ge(ple_th, n + 1)
                        dve.wait_ge(pp_in, 2)
                        then(dve.scalar_tensor_tensor(out=thp[:, n], in0=thp[:, n], scalar=1.0, in1=pp[:, :, cols],
                                                      op0=ALU.add, op1=ALU.mult))
                        dve.scalar_tensor_tensor(out=x[:, :, cols], in0=thp[:, n], scalar=0.5, in1=x[:, :, cols],
                                                 op0=ALU.mult, op1=ALU.add).then_inc(x_done, 1)

        @block.gpsimd
        def _(pool):
            own = [0]

            def then(ins):
                ins.then_inc(pool_step, 1)
                own[0] += 1
                pool.wait_ge(pool_step, own[0])

            def inverse_root(dst, sums, width):
                then(pool.tensor_scalar(dst, sums, 1.0 / width, EPS, ALU.mult, ALU.add))
                n = dst.shape[-1]
                return pool.tensor_tensor(dst, dst, expo[:, 0:n], ALU.pow)

            bias = A["b_ada"]
            for j in range(4):
                r = slice(32 * j, 32 * j + 32)
                half, scale = divmod(j, 2)
                pool.dma_start(mod[r, 0, :], bass.AP(tensor=bias.tensor, offset=bias.offset + scale * D + half * W,
                                                    ap=[[0, 32], [1, W]])).then_inc(bias_in, 16)
                pool.dma_start(mod[r, 1:3, :], bass.AP(tensor=bias.tensor, offset=bias.offset + (4 + j) * W,
                                                      ap=[[0, 32], [4 * W, 2], [1, W]])).then_inc(bias_in, 16)
            pool.dma_start(lamb[:, :, :], A["diff_lam"].to_broadcast([P, 4, HD])).then_inc(setup_in, 16)
            pool.dma_start(hot[:, :], A["constants"][0:BUCKETS + 1, C_HOT:C_ALL]).then_inc(setup_in, 16)
            pool.dma_start(table[0:BUCKETS, :], A["rel_bias_2"]).then_inc(setup_in, 16)
            pool.dma_start(bf[:, :], A["b_f"].rearrange("a h -> h a")).then_inc(setup_in, 16)
            then(pool.memset(expo[:, :], -0.5))
            then(pool.memset(qT[HD:P, :, :, 0, :].rearrange("p a b s -> p (a b) s").bitcast(F32), 0.0))
            pool.memset(qT[0:HD, :, :, 1, :].rearrange("p a b s -> p (a b) s").bitcast(F32), 0.0).then_inc(zeroed, 1)
            pool.wait_ge(zeroed, 1)
            pool.memset(ncum[:, :, :].bitcast(F32), 0.0).then_inc(zeroed, 1)

            for it in ORDER:
                kind, i = it
                if kind == "relbias":
                    pool.wait_ge(rel_row, 1)
                    pool.dma_start(skew.ap(), relrow[:, :]).then_inc(rel_out, 16)

                elif kind in ("norm", "final"):
                    n = 5 if kind == "final" else i
                    pool.wait_ge(sums_made, 2 * n + 2)
                    then(pool.tensor_tensor(nss[:, n, :, 0], nss[:, n, :, 0], nss[:, n, :, 1], ALU.add))
                    last = inverse_root(nrs[:, n, :], nss[:, n, :, 0], D)
                    if n in (2, 3, 4):
                        then(last)
                        if n == 3:
                            last = pool.tensor_tensor(nrs2[:, n, :], nrs[:, n, :], nrs[:, n, :], ALU.mult)
                        else:
                            last = pool.tensor_scalar(nrs2[:, n, :], nrs[:, n, :], 0.5, None, ALU.mult)
                    last.then_inc(norm_rs, 1)
                    if n == 2:
                        pool.wait_ge(gemm_done, slabs_before(("norm", 2), "hid"))
                        pool.wait_ge(x_done, 4)
                        pool.dma_start(ws[:, :, :], A["w_sgu_spatial_2"][0].rearrange("g t s -> t g s")
                                       ).then_inc(ws_in, 16)
                        for n, name in enumerate(("ln_v_g_2", "ln_v_b_2")):
                            pool.dma_start(lngb[:, n, :], A[name].to_broadcast([P, D])).then_inc(ln_in, 16)
                    elif n == 3:
                        pool.wait_ge(score_ps, 2 * PAIRS)
                        pool.dma_start(pin[:, :, :], A["p_2"][0, 0].rearrange("(t p) f -> p t f", p=P)).then_inc(p_in, 16)
                    elif n == 4:
                        pool.wait_ge(gemm_done, slabs_before(("norm", 4), "hid"))
                        pool.dma_start(gfin[:, :], A["norm_final_g_2"].rearrange("(a d) -> a d", a=1).to_broadcast([P, D])
                                       ).then_inc(gfin_in, 16)

                elif kind == "evac" and TILES[i]["name"] in ("fox", "diff") and TILES[i]["n"] < 2:
                    n, name = TILES[i]["n"], TILES[i]["name"]
                    m, j = (n, n) if name == "fox" else (n + 2, n + 3)
                    pool.wait_ge(hss_in, m + 1)
                    then(inverse_root(hrs[:, m, :], hss[:, m, :], HD))
                    pool.wait_ge(tok_in, j + 1)
                    t = tok1[:, j].rearrange("p t (h d) -> p (t h) d", d=HD)
                    pool.tensor_tensor(t, t, spread(hrs[:, m, :], HD), ALU.mult).then_inc(qk_ready, 1)

                elif kind == "scores" and kind_of(i) == "fox":
                    for n in range(2):
                        a = 2 * i + n
                        if a == 0:
                            pool.wait_ge(cumq_in, 1)
                        if a >= 2:
                            pool.wait_ge(smax, 2 * (a - 2) + 2)
                        pool.tensor_scalar(mcum[:, a % 2, 0:P], mask[:, P:2 * P], cumq[:, 0, a:a + 1], None, ALU.add)
                        pool.tensor_scalar(mcum[:, a % 2, P:3 * P], mask, cumq[:, 1, a:a + 1], None, ALU.add
                                           ).then_inc(mcum_in, 1)

                elif kind == "diffnorm":
                    pool.wait_ge(dsq_in, DIFF)
                    inverse_root(drs[:, :], dss[:, :], 2 * HD).then_inc(drs_made, 1)

                elif kind == "spatial":
                    pool.wait_ge(ws_in, 16)
                    pool.affine_select(out=ws[:, :, :], in_=ws[:, :, :], compare_op=ALU.is_ge, fill=0.0, base=0,
                                       pattern=[[0, 8], [-1, P]], channel_multiplier=1).then_inc(ws_low, 1)

                elif kind == "layernorm":
                    pool.wait_ge(mv_made, 1)
                    then(pool.tensor_scalar(vrs[:, :], mv[:, :, 1], 1.0, EPS, ALU.mult, ALU.add))
                    pool.tensor_tensor(vrs[:, :], vrs[:, :], expo[:, 0:TB], ALU.pow).then_inc(vrs_made, 1)
                    pool.wait_ge(ln_in, 32)
                    for t in range(TB):
                        pool.wait_ge(vc_made, t + 1)
                        then(pool.tensor_tensor(vb[:, t, :], vb[:, t, :], lngb[:, 0, :], ALU.mult))
                        pool.tensor_tensor(vb[:, t, :], vb[:, t, :], lngb[:, 1, :], ALU.add).then_inc(vn_made, 1)
                    pool.wait_ge(vn_made, TB)
                    pool.wait_ge(rel_out, 16)
                    pool.dma_start(toep[:, :, :], bass.AP(tensor=skew, offset=0,
                                                          ap=[[1, P], [SKEW, MOBA], [1, 2 * P]])).then_inc(rel_in, 16)


def q_affine(key):
    return 2 * key[1] + key[2]


def constants():
    c = np.zeros((P, C_ALL), np.float32)
    c[:, C_ID:C_ID + P] = np.eye(P)
    dist = P + np.arange(P)[:, None] - np.arange(2 * P)[None, :]
    c[:, C_MASK:C_MASK + 2 * P] = np.where(dist >= 0, 0.0, MASKED)
    for h in range(DIFF):
        slope = 2.0 ** (-8.0 * (h + 1) / DIFF)
        c[:, C_ALIBI + h * 2 * P:C_ALIBI + (h + 1) * 2 * P] = np.where(dist >= 0, -slope * dist, MASKED)
    far = np.arange(SKEW) - (P - 1)
    exact = BUCKETS // 2
    n = np.maximum(far, exact).astype(np.float32)
    large = exact + (np.log(n / np.float32(exact)) / np.float32(np.log(1024 / exact)) * np.float32(BUCKETS - exact)
                     ).astype(np.int32)
    bucket = np.where(far < 0, BUCKETS, np.where(far < exact, np.maximum(far, 0), np.minimum(large, BUCKETS - 1)))
    c[bucket, C_HOT + np.arange(SKEW)] = 1.0
    return c


_INS = ["x", "c", "ln1_g", "ln2_g", "w_ada", "b_ada", "w_in", "b_f", "fox_qk_g", "diff_qk_g", "diff_lam",
        "diff_norm_g", "w_out", "w_gate", "w_up", "w_down", "p_2", "norm_mix_g_2", "w_in_2", "w_sgu_spatial_2",
        "b_sgu_spatial_2", "ln_v_g_2", "ln_v_b_2", "rel_bias_2", "w_out_2", "norm_ffn_g_2", "w_ff1_2", "w_ff2_2",
        "norm_ple_g_2", "w_ple_gate_2", "w_ple_proj_2", "norm_final_g_2"]


def kernel(**inputs):
    import concourse.bacc as bacc
    from concourse.bass_utils import run_bass_kernel_spmd

    nc = bacc.Bacc("TRN2", target_bir_lowering=False, num_devices=1)
    arrays, args = {}, {}
    for name in _INS + ["constants"]:
        a = constants() if name == "constants" else np.ascontiguousarray(inputs[name])
        arrays[f"in_{name}"] = a
        args[name] = nc.dram_tensor(f"in_{name}", a.shape, mybir.dt.from_np(a.dtype), kind="ExternalInput").ap()
    result = nc.dram_tensor("out_x", (1, S, D), F32, kind="ExternalOutput").ap()
    build(nc, args, result)
    r = run_bass_kernel_spmd(nc, [arrays], core_ids=[0])
    return r.results[0]["out_x"]
```

```python
from contextlib import ExitStack
from math import exp as _exp

import numpy as np

import concourse.bass as bass
from concourse import mybir

F32 = mybir.dt.float32
F32R = mybir.dt.float32r
ALU = mybir.AluOpType
ACT = mybir.ActivationFunctionType
AX = mybir.AxisListType.X

P = 128
D = 1024
S = 256
TB = S // P
KC = D // P
HD = 64
FOX, DIFF, MOBA = 8, 4, 16
W = 512
DFF = 2816
DFF2 = 4096
EPS = 1e-6
MASKED = -1e30
BUCKETS = 32
LAM_INIT = 0.8 - 0.6 * _exp(0.0)
SKEW = 384
RAW, SPL = 5, 3

C_ID, C_MASK, C_ALIBI, C_HOT = 0, 128, 384, 1408
C_ALL = C_HOT + SKEW

V_C, V_LN1, V_LN2, V_MIX, V_FFN, V_PLE, V_BS, V_QK, V_DN = 0, 8, 16, 24, 32, 40, 48, 56, 60
V_ALL = 61

PAIRS = FOX // 2 + DIFF + MOBA // 2
FOX_P, DIFF_P = FOX // 2, DIFF


BETWEEN = {"fox": (3, 1, 2, 1, 2), 1: (3, 1, 2, 1, 1), 2: (3, 2, 1, 0, 2), 3: (2, 0, 3, 0, 1),
           "diff": (1, 0, 1, 2, 2), 7: (1, 0, 1, 0, 2),
           "moba": (2, 0, 1, 0, 1), 8: (2, 0, 1, 0, 0), 15: (2, 1, 1, 1, 1)}


def kind_of(u):
    return "fox" if u < FOX_P else "diff" if u < FOX_P + DIFF_P else "moba"


def plan():
    tiles, slabs, order = [], [], []

    def tile(name, n, chunks, operand, width=W):
        tiles.append(dict(name=name, n=n, K=chunks, operand=operand, width=width))
        return len(tiles) - 1

    def slab(T, weight, col, k0, chunks=4, width=W):
        s = len(slabs)
        slabs.append(dict(weight=weight, row=k0 * P, chunks=chunks, col=col, cols=width))
        return [("piece", dict(T=T, k=k0 + j, slab=s, off=j * width, first=j == 0, last=j == chunks - 1))
                for j in range(chunks)]

    def whole(name, n, weight, col, operand, width=W):
        T = tile(name, n, KC, operand, width)
        return slab(T, weight, col, 0, 4, width) + slab(T, weight, col, 4, 4, width) + [("evac", T)]

    def long(name, n, weight, operand, chunks):
        T = tile(name, n, chunks, operand)
        out = []
        for k0 in range(0, chunks, 4):
            out += slab(T, weight, n * W, k0, min(4, chunks - k0))
        return out + [("evac", T)]

    def halves(name, weight, col, operand, ahead, between, after=()):
        Ts = [tile(name, n, KC, operand) for n in range(2)]
        out = slab(Ts[0], weight, col, 0) + ahead + slab(Ts[1], weight, col + W, 0) + between
        for n, T in enumerate(Ts):
            out += slab(T, weight, col + n * W, 4) + [("evac", T)] + (after[n] if after else [])
        return out

    def insert(items, *at):
        out = list(items)
        for pos, steps in sorted(at, reverse=True, key=lambda x: x[0]):
            out[pos:pos] = steps
        return out

    def attention(us, filler, late=()):
        filler = list(filler)

        def fill(n):
            out = []
            while n > 0 and filler:
                it = filler.pop(0)
                out.append(it)
                n -= it[0] in ("piece", "ada")
            while filler and filler[0][0] not in ("piece", "ada"):
                out.append(filler.pop(0))
            return out

        out = []
        for u in us:
            moba, c = kind_of(u) == "moba", BETWEEN.get(u, BETWEEN[kind_of(u)])
            if u != us[-1]:
                out += [("scores", u + 1)]
            if moba and u != us[0]:
                out += [("back", u - 1)]
            out += fill(c[0]) + [("probsT", (u, 0))] + fill(c[1])
            if u + 2 <= us[-1]:
                out += [("heads", u + 2)]
            out += fill(c[2])
            if kind_of(u) != "diff":
                out += [("probsT", (u, 1))] + fill(c[3])
            out += [("values", u)] + fill(c[4])
        late = filler + list(late)
        if moba:
            out += late[:3] + [("back", us[-1])]
            late = late[3:]
        return out + late

    def turns(kind, n, pairs):
        return [("turn", (kind, n, h)) for h in pairs]

    def parts(kind, n, pairs):
        return [("part", (kind, n, h)) for h in pairs]

    ada = [("ada", j) for j in range(3 * KC)]

    order += [("cond", 0), ("sums", (0, 0)), ("sums", (0, 1)), ("norm", 0)]
    order += ada[:4] + [("mod", 0), *turns("norm", 0, (0, 1)), ("split", None), *parts("norm", 0, (0, 1))]
    fox = [tile("fox", n, KC, "h") for n in range(2)]
    order += insert(slab(fox[0], "w_in", 0, 0), *[(1 + j, [ada[4 + j]]) for j in range(4)])
    order += [("mod", 1), *turns("norm", 0, (2, 3)), ("split", None), *parts("norm", 0, (2, 3))]
    order += slab(fox[1], "w_in", W, 0) + [("vectors", 0), ("setup", 0), ("relbias", 0)]
    order += slab(fox[0], "w_in", 0, 4) + [("evac", fox[0])]
    now = slab(fox[1], "w_in", W, 4) + [("evac", fox[1])] + whole("fox", 2, "w_in", 2 * W, "h")
    order += insert(now, (2, [("unit", 0)]), (2, [("fgate", 0)]), (4, [("logf", 0)]), (6, [("unit", 1)]),
                    (7, [("cum", 0)]), (9, [("heads", 0)]), (10, [("scores", 0), ("heads", 1)]))
    tail = []
    for n in range(3):
        tail += whole("diff", n, "w_in", 3 * W + FOX + n * W, "h")
    tail = insert(tail, (11, [("unit", 2)]), (20, [("unit", 3)]), (23, ada[8:10]))
    wo = [tile("w_out", n, KC, "mix") for n in range(2)]
    fill = slab(wo[0], "w_out", 0, 0) + slab(wo[1], "w_out", W, 0)
    tail += insert(fill, *[(j, [ada[10 + j]]) for j in range(8)])
    order += attention(list(range(FOX_P + DIFF_P)), tail, ada[18:20] + [("grow", 0)])
    order += [("diffnorm", 0)] + ada[20:21] + turns("diff", 0, (0, 1)) + ada[21:22]
    order += slab(wo[0], "w_out", 0, 4) + [("evac", wo[0])]
    order += insert(slab(wo[1], "w_out", W, 4), (1, [("sums", (1, 0))])) + [("evac", wo[1]), ("sums", (1, 1))] + ada[22:24]
    order += [("mod", 2), ("norm", 1)]
    order += turns("norm", 1, (0, 1)) + parts("norm", 1, (0, 1)) + turns("norm", 1, (2, 3)) + parts("norm", 1, (2, 3))
    late = []
    for n in range((DFF + W - 1) // W):
        width = min(W, DFF - n * W)
        now = whole("gate", n, "w_gate", n * W, "h", width) + whole("up", n, "w_up", n * W, "h", width)
        order += insert(now, (4, late))
        late = turns("hid", n, range(width // 256))
    order += insert(long("down", 0, "w_down", "hid", DFF // P), (4, late), (8, [("grow", 1)]))
    order += insert(long("down", 1, "w_down", "hid", DFF // P), (6, [("sums", (2, 0)), *turns("norm", 2, (0, 1))]))
    order += [("sums", (2, 1)), ("norm", 2)]
    order += halves("v", "w_in_2", D, "h", turns("norm", 2, (2, 3)), [], [[("spatial", 0)], []])
    order += [("layernorm", 0)]
    for n in (0, 1):
        order += whole("u", n, "w_in_2", n * W, "h")
    for j, name in enumerate(("q", "k", "vatt")):
        for n in (0, 1):
            now = whole(name, n, "w_in_2", 2 * D + j * D + n * W, "h")
            if (j, n) == (2, 1):
                m = FOX_P + DIFF_P
                now = insert(now, (0, [("heads", m)]), (3, [("scores", m), ("heads", m + 1)]))
            order += now
            if (j, n) == (0, 1):
                order += [("sgu", 0), ("sgu", 1)]
    gates = []
    for n in (0, 1):
        for j, name in enumerate(("ga", "gb")):
            gates += whole(name, n, "w_in_2", 5 * D + j * D + n * W, "h")
    wo = [tile("w_out2", n, KC, "h") for n in range(2)]
    gates = insert(gates, (len(gates) - 7, [("merge", 0)]), (len(gates) - 5, turns("merge", 0, (0, 1))))
    most = slab(wo[0], "w_out_2", 0, 0) + slab(wo[1], "w_out_2", W, 0)
    order += attention(list(range(FOX_P + DIFF_P, PAIRS)), gates, most[:3])
    order += [("merge", 1)] + most[3:6] + turns("merge", 1, (0, 1)) + most[6:]
    order += slab(wo[0], "w_out_2", 0, 4) + [("evac", wo[0])]
    order += insert(slab(wo[1], "w_out_2", W, 4), (2, [("sums", (3, 0)), *turns("norm", 3, (0, 1))]))
    order += [("evac", wo[1]), ("sums", (3, 1)), ("norm", 3)]
    order += halves("ff1", "w_ff1_2", 0, "h", turns("norm", 3, (2, 3)), [])
    turns2 = [turns("hid2", n, (0, 1)) for n in range(DFF2 // W)]
    for n in range(2, DFF2 // W):
        now = whole("ff1", n, "w_ff1_2", n * W, "h")
        order += insert(now, (4, turns2[n - 1] if n > 2 else turns2[0] + turns2[1]))
    order += insert(long("ff2", 0, "w_ff2_2", "hid", DFF2 // P), (4, turns2[-1]), (10, [("pT", 0)]))
    order += insert(long("ff2", 1, "w_ff2_2", "hid", DFF2 // P), (6, [("sums", (4, 0)), *turns("norm", 4, (0, 1))]))
    for n in (0, 1):
        order += long("ple_proj", n, "w_ple_proj_2", "p", 2) + [[("sums", (4, 1)), ("norm", 4)], []][n]
    order += halves("ple", "w_ple_gate_2", 0, "h", turns("norm", 4, (2, 3)), [],
                    [[("sums", (5, 0))], [("sums", (5, 1))]])
    order += [("final", 0)]

    out, split = [], 0
    for it in order:
        if it == ("split", None):
            out.append(("split", split))
            split += 1
            continue
        if it[0] == "piece" and it[1]["first"]:
            while split <= min(it[1]["slab"] + min(2, it[1]["slab"] + 1), len(slabs) - 1):
                out.append(("split", split))
                split += 1
        out.append(it)
    turn = 0
    turns = {}
    for it in out:
        if it[0] == "turn":
            turns[it[1]] = turn
            turn += 1
    return tiles, slabs, out, turns


TILES, SLABS, ORDER, TURNS = plan()
assert [p["slab"] for kind, p in ORDER if kind == "piece" and p["first"]] == list(range(len(SLABS)))
LAST_SLAB = {p["T"]: p["slab"] for kind, p in ORDER if kind == "piece"}
STREAM = [it for it in ORDER if it[0] in ("split", "ada")]
STREAM_AT = {it: n for n, it in enumerate(STREAM)}


def transfers(it):
    return 2 if it[0] == "ada" and it[1] < KC else 1


def spread(ap, n):
    return bass.AP(tensor=ap.tensor, offset=ap.offset, ap=[list(d) for d in ap.ap] + [[0, n]])


def backwards(ap):
    d = [list(x) for x in ap.ap]
    step, n = d[-1]
    return bass.AP(tensor=ap.tensor, offset=ap.offset + step * (n - 1), ap=d[:-1] + [[-step, n]])


def twice(ap):
    d = [list(d) for d in ap.ap]
    return bass.AP(tensor=ap.tensor, offset=ap.offset, ap=[d[0], [0, TB], d[1]])


def slabs_before(step, operand):
    n = 0
    for it in ORDER:
        if it == step:
            return n
        if it[0] == "piece" and it[1]["last"] and TILES[it[1]["T"]]["operand"] == operand:
            n = it[1]["slab"] + 1
    raise ValueError(step)


def turned_head(u, i):
    k = kind_of(u)
    if k == "fox":
        return 2 * u + i
    if k == "diff":
        return FOX + u - FOX_P
    return FOX + DIFF + 2 * (u - FOX_P - DIFF_P) + i


def pair_of_turned(j):
    if j < FOX:
        return j // 2
    if j < FOX + DIFF:
        return FOX_P + j - FOX
    return FOX_P + DIFF_P + (j - FOX - DIFF) // 2


def build(nc, A, out):
    ctx = ExitStack()
    with ctx:
        def sem(name):
            return ctx.enter_context(nc.semaphore(name))

        def sb(name, shape, dt=F32, where=None):
            return (where or ctx).enter_context(nc.sbuf_tensor(name, shape, dt))

        PS = ctx.enter_context(nc.psum_tensor("PS", [P, 8, W], F32))
        skew = nc.dram_tensor("skew_dram", [MOBA, SKEW], F32, kind="Internal")

        raw = sb("raw", [P, RAW, 4 * W])
        whi = sb("whi", [P, SPL, 4 * W], F32R)
        wlo = sb("wlo", [P, SPL, 4 * W], F32R)
        hT = sb("hT", [P, 2, KC, S], F32R)
        qT = sb("qT", [P, 2, 2, 2, S], F32R)
        gk = ExitStack()
        kT = sb("kT", [P, 2, 2, S], F32R, gk)
        gk.close()
        pin = sb("pin", [P, TB, W])[:, :, 0:2 * P]
        x = sb("x", [P, TB, D])
        con = sb("con", [P, C_ALIBI])
        identr = sb("identr", [P, P], F32R)
        col = sb("col", [P, V_ALL + 3])
        cond32 = sb("cond32", [P, KC, 32])
        lam = sb("lam", [P, 6])
        expo = sb("expo", [P, 16])
        mod = sb("mod", [P, 3, W])
        nmax = sb("nmax", [P, 2 * PAIRS, TB])
        lsum = sb("lsum", [P, 2 * PAIRS, TB])
        rinv = sb("rinv", [P, 2 * PAIRS, TB])
        nss = sb("nss", [P, 6, TB, 2])
        nrs = sb("nrs", [P, 6, TB])
        nrs2 = sb("nrs2", [P, 6, TB])
        ident = con[:, C_ID:C_ID + P]
        mask = con[:, C_MASK:C_MASK + 2 * P]

        g = ExitStack()
        tok1 = sb("tok1", [P, 6, TB, W], F32, g)
        sq = sb("sq", [P, TB, W], F32, g)
        gg = ExitStack()
        aff1 = sb("aff1", [P, 4, S], F32, gg)
        gg.close()
        mixT = sb("mixT", [P, 2, KC, S], F32R, g)
        alibi = sb("alibi", [P, DIFF, 2 * P], F32, g)
        AB = sb("AB", [P, 4, KC], F32, g)
        wfg = sb("wfg", [P, KC, FOX], F32, g)
        wfgs = sb("wfgs", [P, 2, KC, FOX], F32R, g)
        bf = sb("bf", [FOX, 1], F32, g)
        fgt = sb("fgt", [FOX, 4, S], F32, g)
        ones = sb("ones", [FOX, S], F32, g)
        cumq = sb("cumq", [P, TB, FOX], F32, g)
        ncum = sb("ncum", [P, 2, S], F32R, g)
        hss = sb("hss", [P, 4, TB * 8], F32, g)
        hrs = sb("hrs", [P, 4, TB * 8], F32, g)
        dss = sb("dss", [P, TB * DIFF], F32, g)
        drs = sb("drs", [P, TB * DIFF], F32, g)
        od = tok1[:, 1]
        g1row = tok1[:, 0].rearrange("p t w -> p (t w)")
        gg = ExitStack()
        vec = sb("vec", [V_ALL, P], F32, gg)
        lamb = sb("lamb", [P, 4, HD], F32, gg)
        lprod = sb("lprod", [P, 2, HD], F32, gg)
        cond = sb("cond", [P, 2, KC], F32, gg)
        hot = sb("hot", [BUCKETS + 1, SKEW], F32, gg)
        table = sb("table", [BUCKETS + 1, MOBA], F32, gg)
        relrow = sb("relrow", [MOBA, SKEW], F32, gg)
        gg.close()
        gg = ExitStack()
        _ = sb("setup_space", [P, 2048], F32, gg)
        xn1 = sb("xn1", [P, TB, D], F32, gg)
        gg.close()
        gg = ExitStack()
        _ = sb("relrow_space", [P, 1024], F32, gg)
        sc1 = sb("sc1", [P, 2, 2, 3 * P], F32, gg)
        pt1 = sb("pt1", [P, 2, 3 * P], F32, gg)
        mcum = sb("mcum", [P, 2, 3 * P], F32, gg)
        gg.close()
        g.close()

        g = ExitStack()
        hidT1 = sb("hidT1", [P, 2, DFF // P, S], F32R, g)
        hid1 = sb("hid1", [P, 2, TB, W], F32, g)
        th1 = sb("th1", [P, TB, W], F32, g)
        xnb = sb("xnb", [P, TB, D], F32, g)
        affb = sb("affb", [P, 4, S], F32, g)
        g2row = sb("g2row", [P, D], F32, g)
        tmpb = affb[:, :, :].rearrange("p c s -> p (c s)").rearrange("p (t w) -> p t w", t=TB)
        g.close()

        g = ExitStack()
        tok2 = sb("tok2", [P, 3, TB, D], F32, g)
        ub = sb("ub", [P, TB, D], F32, g)
        vb = sb("vb", [P, TB, D], F32, g)
        toep = sb("toep", [P, MOBA, 2 * P], F32, g)
        sc2 = sb("sc2", [P, 2, 2, 3 * P], F32, g)
        pt2 = sb("pt2", [P, 2, 3 * P], F32, g)
        wsT = sb("wsT", [P, 8, P], F32, g)
        ws = sb("ws", [P, 8, P], F32, g)
        th2 = ws[:, :, :].rearrange("p g s -> p (g s)").rearrange("p (t w) -> p t w", t=TB)
        ybT = wsT[:, 0:2, :].rearrange("p g s -> p (g s)")
        bn = sb("bn", [P, TB, 2, 6], F32, g)
        mv = sb("mv", [P, TB, 2], F32, g)
        vrs = sb("vrs", [P, TB], F32, g)
        lngb = toep[:, 0:8, :].rearrange("p h k -> p (h k)").rearrange("p (a d) -> p a d", a=2)
        g.close()

        g = ExitStack()
        hid2 = sb("hid2", [P, 2, TB, W], F32, g)
        gg = ExitStack()
        hidT2 = sb("hidT2", [P, 2, DFF2 // P, S], F32R, gg)
        gg.close()
        pp = sb("pp", [P, TB, D], F32, g)
        gfin = sb("gfin", [P, D], F32, g)
        fin = sb("fin", [P, TB, D], F32, g)
        thp = sb("thp", [P, 2, TB, W], F32, g)
        pT = qT[:, 0]
        g.close()

        raw_in = [sem(f"raw_in{i}") for i in range(RAW)]
        hi_made = sem("hi_made")
        lo_made = sem("lo_made")
        rows_done = sem("rows_done")
        ada_used = sem("ada_used")
        gemm_done = sem("gemm_done")
        cond_in = sem("cond_in")
        vec_in = sem("vec_in")
        x_in = sem("x_in")
        setup_in = sem("setup_in")
        late_bias_in = sem("late_bias_in")
        bias_in = sem("bias_in")
        gate_w_in = sem("gate_w_in")
        alibi_in = sem("alibi_in")
        c_ps = sem("c_ps")
        c_col = sem("c_col")
        vec_ps = sem("vec_ps")
        col_made = sem("col_made")
        cond_th = sem("cond_th")
        cond_made = sem("cond_made")
        zeroed = sem("zeroed")
        rel_ps = sem("rel_ps")
        rel_row = sem("rel_row")
        rel_out = sem("rel_out")
        rel_in = sem("rel_in")
        table_set = sem("table_set")
        lam_dot = sem("lam_dot")
        lam_exp = sem("lam_exp")
        lam_made = sem("lam_made")
        mod_in = sem("mod_in")
        mod_T = sem("mod_T")
        ab_made = sem("ab_made")
        g_ps = sem("g_ps")
        g1_row = sem("g1_row")
        g2_row = sem("g2_row")
        sums_made = sem("sums_made")
        norm_rs = sem("norm_rs")
        xn_act = sem("xn_act")
        xn_dve = sem("xn_dve")
        turned = sem("turned")
        turn_aff = sem("turn_aff")
        turn_hi = sem("turn_hi")
        turn_lo = sem("turn_lo")
        wfg_hi = sem("wfg_hi")
        wfg_lo = sem("wfg_lo")
        fg_ps = sem("fg_ps")
        fg_abs = sem("fg_abs")
        fg_log = sem("fg_log")
        cum_made = sem("cum_made")
        ncum_hi = sem("ncum_hi")
        ncum_lo = sem("ncum_lo")
        cumq_ps = sem("cumq_ps")
        cumq_in = sem("cumq_in")
        tok_in = sem("tok_in")
        sq_in = sem("sq_in")
        hss_in = sem("hss_in")
        hrs_made = sem("hrs_made")
        qk_ready = sem("qk_ready")
        heads_ps = sem("heads_ps")
        heads_hi = sem("heads_hi")
        heads_lo = sem("heads_lo")
        mcum_in = sem("mcum_in")
        score_ps = sem("score_ps")
        smax = sem("smax")
        exp_done = sem("exp_done")
        fox_p = sem("fox_p")
        diff_p = sem("diff_p")
        probs_ps = sem("probs_ps")
        probs_sb = sem("probs_sb")
        value_ps = sem("value_ps")
        mix_hi = sem("mix_hi")
        mix_lo = sem("mix_lo")
        od_in = sem("od_in")
        dsq_in = sem("dsq_in")
        drs_made = sem("drs_made")
        od_made = sem("od_made")
        ybT_in = sem("ybT_in")
        back_ps = sem("back_ps")
        yb_in = sem("yb_in")
        scaled = sem("scaled")
        x_done = sem("x_done")
        hid_in = sem("hid_in")
        hid2_in = sem("hid2_in")
        relu_in = sem("relu_in")
        gate_th = sem("gate_th")
        ga_th = sem("ga_th")
        ple_th = sem("ple_th")
        tok2_in = sem("tok2_in")
        v_in = sem("v_in")
        u_in = sem("u_in")
        r_in = sem("r_in")
        ws_in = sem("ws_in")
        ws_low = sem("ws_low")
        ws_ps = sem("ws_ps")
        ws_T = sem("ws_T")
        ln_in = sem("ln_in")
        mv_made = sem("mv_made")
        vrs_made = sem("vrs_made")
        vc_made = sem("vc_made")
        vn_made = sem("vn_made")
        sgu_ps = sem("sgu_ps")
        ya_in = sem("ya_in")
        ga_in = sem("ga_in")
        gb_in = sem("gb_in")
        merged = sem("merged")
        p_in = sem("p_in")
        p_ps = sem("p_ps")
        p_hi = sem("p_hi")
        p_lo = sem("p_lo")
        pp_in = sem("pp_in")
        gfin_in = sem("gfin_in")
        out_made = sem("out_made")
        out_done = sem("out_done")
        act_step = sem("act_step")
        dve_step = sem("dve_step")
        pool_step = sem("pool_step")

        def slab_view(t, slot, s):
            m = SLABS[s]
            return t[:, slot, 0:m["chunks"] * m["cols"]]

        def landed(eng, it):
            n = STREAM_AT[it]
            eng.wait_ge(raw_in[n % RAW], 16 * sum(transfers(STREAM[m]) for m in range(n % RAW, n + 1, RAW)))
            return n % RAW

        def bank0(T):
            return 2 * (T % 2)

        def tile_ps(T):
            return PS[:, bank0(T):bank0(T) + TB, 0:TILES[T]["width"]]

        def complete(eng, T):
            eng.wait_ge(gemm_done, LAST_SLAB[T] + 1)

        def by_rows(T):
            return TILES[T]["name"] in ("w_out", "ple") and TILES[T]["n"] == 1

        def rows_complete(eng, T, t):
            if by_rows(T) and t == 0:
                eng.wait_ge(rows_done, 1 if TILES[T]["name"] == "w_out" else 2)
            else:
                complete(eng, T)

        def tile_readers(T):
            name, n = TILES[T]["name"], TILES[T]["n"]
            if name in ("fox", "diff"):
                j = n + (0 if name == "fox" else 3)
                return [(tok_in, j + 1)] + ([(sq_in, n + 1 + (0 if name == "fox" else 2))] if n < 2 else [])
            if name in ("q", "k", "vatt"):
                return [(tok2_in, 2 * ("q", "k", "vatt").index(name) + n + 1)]
            if name in ("w_out2", "ff2"):
                return [(x_done, 2 * ((4 if name == "w_out2" else 6) + n + 1))]
            if name in ("w_out", "down"):
                return [(scaled, 2 * ((0 if name == "w_out" else 2) + n + 1))]
            s, before = {"gate": (r_in, 0), "up": (hid_in, 0), "v": (v_in, 0), "u": (u_in, 0), "ga": (ga_th, 0),
                         "gb": (gb_in, 0), "ff1": (relu_in, 0), "ple_proj": (pp_in, 0), "ple": (ple_th, 0)}[name]
            return [(s, before + n + 1)]

        def turn_bank(q):
            return 4 + (q % 4 if q >= 4 else q % 2)

        def turn_of(key):
            kind, n, h = key
            c = slice(h * 2 * P, (h + 1) * 2 * P)
            if kind == "norm":
                if n >= 2:
                    return x[:, :, c], ((x_done, 2 * (2 * n - 1 + h // 2)),), hT, 2 * h
                return (xn1, xnb)[n][:, :, c], ((xn_act, n + 1), (xn_dve, n + 1)), hT, 2 * h
            if kind == "diff":
                return od[:, :, c], ((od_made, 1),), mixT, 4 + 2 * h
            if kind == "merge":
                return tok2[:, 0, :, n * W + h * 2 * P:n * W + (h + 1) * 2 * P], ((merged, n + 1),), hT, 4 * n + 2 * h
            if kind == "hid":
                return hid1[:, n % 2, :, c], ((hid_in, n + 1),), hidT1, 4 * n + 2 * h
            return hid2[:, n % 2, :, c], ((hid2_in, n + 1),), hidT2, 4 * n + 2 * h

        def is_affine(key):
            return key[0] == "norm" and key[1] < 2

        def affine(key):
            h = 2 * (key[2] % 2)
            return (aff1, affb)[key[1]][:, h:h + 2, :]

        def gain_of(key, c):
            kind, n, h = key
            if kind == "norm" and n >= 2:
                v = (V_MIX, V_FFN, V_PLE)[n - 2] + 2 * h + c
                return col[:, v:v + 1]
            if kind == "diff":
                return col[:, V_ALL + 2:V_ALL + 3]
            return 0.5 if kind == "merge" else None

        def heads_of(u):
            k = kind_of(u)
            if k == "moba":
                c = (u - FOX_P - DIFF_P) * P
                return tok2[:, 0, :, c:c + P], tok2[:, 1, :, c:c + P], 0.125, 1.0, (tok2_in, 4)
            j = 0 if k == "fox" else 3
            c = (u if k == "fox" else u - FOX_P) * P
            gq, gk = (V_ALL, V_QK + 1) if k == "fox" else (V_ALL + 1, V_QK + 3)
            return (tok1[:, j, :, c:c + P], tok1[:, j + 1, :, c:c + P],
                    col[:, gq:gq + 1], col[:, gk:gk + 1], (qk_ready, 2 if k == "fox" else 4))

        def scores_sb(u):
            return (sc2 if kind_of(u) == "moba" else sc1)[:, u % 2]

        def probs_T(u):
            return pt2 if kind_of(u) == "moba" else pt1

        def heads_bank(u):
            return 7 if kind_of(u) == "moba" else 4

        def probs_bank(n):
            return (4, 6)[n]

        def grow_bank(i):
            return (5, 6)[i]

        def squares_of(n, t, h):
            if n in (3, 4):
                return mod[:, t, :]
            return (xn1, xnb, xnb, None, None, fin)[n][:, t, h * W:(h + 1) * W]

        NSETUP = 5
        NROWS = 10
        QB = ((0, P), (P, 3 * P))

        block = ctx.enter_context(nc.Block())

        @block.sync
        def _(sp):
            sp.dma_start(vec[V_C:V_C + KC, :], A["c"].rearrange("a (r q) -> (a r) q", q=P)).then_inc(cond_in, 16)
            sp.dma_start(vec[V_LN1:V_LN1 + KC, :], A["ln1_g"].rearrange("a (r q) -> (a r) q", q=P)).then_inc(cond_in, 16)
            sp.dma_start(con[:, C_ID:C_ID + P], A["constants"][:, C_ID:C_ID + P]).then_inc(cond_in, 16)
            for n, it in enumerate(STREAM):
                if n == 2:
                    sp.dma_start(x[:, :, :], A["x"][0].rearrange("(t p) d -> p t d", p=P)).then_inc(x_in, 16)
                if n >= RAW:
                    kind, i = STREAM[n - RAW]
                    if kind == "ada":
                        sp.wait_ge(ada_used, i + 1)
                    else:
                        sp.wait_ge(lo_made, i + 1)
                if it[0] == "ada":
                    pack, k = divmod(it[1], KC)
                    w, dst = A["w_ada"], raw[:, n % RAW, :]
                    if pack == 0:
                        half, k = divmod(k, 4)
                        for c in range(2):
                            r = (2 * k + c) * P
                            src = w[0, r:r + P, 0:2 * D].rearrange("p (j w) -> p j w", j=2)[:, :, half * W:(half + 1) * W]
                            sp.dma_start(dst[:, 2 * c * W:2 * (c + 1) * W].rearrange("p (j w) -> p j w", j=2), src
                                         ).then_inc(raw_in[n % RAW], 16)
                        continue
                    src = w[0, k * P:(k + 1) * P, pack * 4 * W:(pack + 1) * 4 * W]
                else:
                    m = SLABS[it[1]]
                    src = A[m["weight"]][0, m["row"]:m["row"] + m["chunks"] * P,
                                         m["col"]:m["col"] + m["cols"]].rearrange("(c p) n -> p c n", p=P)
                    dst = slab_view(raw, n % RAW, it[1]).rearrange("p (c n) -> p c n", c=m["chunks"])
                sp.dma_start(dst, src).then_inc(raw_in[n % RAW], 16)
            for n in range(2 * TB):
                t, h = divmod(n, 2)
                sp.wait_ge(out_made, n + 1)
                sp.dma_start(out[0, t * P:(t + 1) * P, h * W:(h + 1) * W], fin[:, t, h * W:(h + 1) * W]
                             ).then_inc(out_done, 16)
            sp.wait_ge(out_done, 16 * 2 * TB)

        @block.tensor
        def _(pe):
            reader = {}

            def take(*banks):
                for b in banks:
                    for s, v in reader.pop(b, ()):
                        pe.wait_ge(s, v)

            def products(out_ap, pairs):
                for n, (a, b) in enumerate(pairs):
                    last = pe.matmul(out_ap, a, b, start=(n == 0), stop=(n == len(pairs) - 1))
                return last

            def operand_ready(T, k):
                name = TILES[T]["operand"]
                if name == "mix":
                    if k < 4:
                        pe.wait_ge(mix_lo, k + 1)
                    else:
                        pe.wait_ge(turn_lo, TURNS[("diff", 0, (k - 4) // 2)] + 1)
                elif name == "p":
                    pe.wait_ge(p_lo, 1)
                elif name == "hid":
                    kind = "hid" if TILES[T]["K"] == DFF // P else "hid2"
                    pe.wait_ge(turn_lo, TURNS[(kind, k // 4, k % 4 // 2)] + 1)
                else:
                    tn = TILES[T]["name"]
                    key = {"fox": ("norm", 0), "diff": ("norm", 0), "gate": ("norm", 1), "up": ("norm", 1),
                           "w_out2": ("merge",), "ff1": ("norm", 3), "ple": ("norm", 4)}.get(tn, ("norm", 2))
                    key = ("merge", k // 4, k % 4 // 2) if key == ("merge",) else (*key, k // 2)
                    pe.wait_ge(turn_lo, TURNS[key] + 1)

            def operand(T, k, t):
                name = TILES[T]["operand"]
                big = hidT1 if TILES[T]["K"] == DFF // P else hidT2
                src = {"h": hT, "mix": mixT, "p": pT, "hid": big}[name]
                return src[:, 0, k, t * P:(t + 1) * P], src[:, 1, k, t * P:(t + 1) * P]

            for it in ORDER:
                kind, i = it
                if kind == "piece":
                    T, k, s, off = i["T"], i["k"], i["slab"], i["off"]
                    width = TILES[T]["width"]
                    if i["first"]:
                        pe.wait_ge(hi_made, s + 1)
                        pe.wait_ge(lo_made, s + 1)
                    if k == 0 and T >= 2:
                        for ready in tile_readers(T - 2):
                            pe.wait_ge(*ready)
                    operand_ready(T, k)
                    def product(k, off, t):
                        wh = whi[:, s % SPL, off:off + width]
                        wl = wlo[:, s % SPL, off:off + width]
                        ah, al = operand(T, k, t)
                        o = PS[:, bank0(T) + t, 0:width]
                        end = k == TILES[T]["K"] - 1
                        pe.matmul(o, ah, wh, start=(k == 0), stop=False)
                        pe.matmul(o, ah, wl, start=False, stop=False)
                        return pe.matmul(o, al, wh, start=False, stop=end)

                    if s == LAST_SLAB[T] and by_rows(T):
                        if not i["first"]:
                            continue
                        for k2 in range(k + 1, k + 4):
                            operand_ready(T, k2)
                        for t in range(TB):
                            for j in range(4):
                                last = product(k + j, off + j * width, t)
                            if t == 0:
                                last.then_inc(rows_done, 1)
                        last.then_inc(gemm_done, 1)
                        continue
                    for t in range(TB):
                        last = product(k, off, t)
                    if i["last"]:
                        last.then_inc(gemm_done, 1)

                elif kind == "cond":
                    pe.wait_ge(cond_in, 48)
                    pe.transpose(PS[:, 5, 0:2 * KC], vec[0:2 * KC, :], ident[0:2 * KC, 0:2 * KC]).then_inc(c_ps, 1)
                    reader[5] = [(c_col, 1)]

                elif kind == "vectors":
                    pe.wait_ge(vec_in, 16 * NROWS)
                    take(4)
                    pe.transpose(PS[:, 4, 0:V_ALL], vec[:, :], ident[0:V_ALL, 0:V_ALL]).then_inc(vec_ps, 1)
                    reader[4] = [(col_made, 1)]

                elif kind == "relbias":
                    pe.wait_ge(table_set, 1)
                    pe.wait_ge(setup_in, 16 * NSETUP)
                    take(5)
                    pe.matmul(PS[0:MOBA, 5, 0:SKEW], table[:, :], hot[:, :], start=True, stop=True).then_inc(rel_ps, 1)
                    reader[5] = [(rel_row, 1)]

                elif kind == "ada":
                    pack, k = divmod(i, KC)
                    if i == 0:
                        pe.wait_ge(cond_made, 1)
                    slot = landed(pe, it)
                    if pack == 0:
                        half, k = divmod(k, 4)
                        if k == 0:
                            take(7 - half)
                        for c in range(2):
                            for j in range(2):
                                r = 64 * half + 32 * j
                                last = pe.matmul(PS[r:r + 32, 7 - half, :], cond32[:, 2 * k + c, :],
                                                 raw[:, slot, (2 * c + j) * W:(2 * c + j + 1) * W],
                                                 start=(k + c == 0), stop=(k == 3 and c == 1))
                        if k == 3:
                            reader[7 - half] = [(mod_in, half + 1)]
                    else:
                        if k == 0:
                            take(7)
                        for j in range(4):
                            last = pe.matmul(PS[32 * j:32 * j + 32, 7, :], cond32[:, k, :],
                                             raw[:, slot, j * W:(j + 1) * W], start=(k == 0), stop=(k == KC - 1))
                        if k == KC - 1:
                            reader[7] = [(mod_in, pack + 2)]
                    last.then_inc(ada_used, 1)

                elif kind == "mod" and i < 2:
                    pe.wait_ge(mod_in, i + 1)
                    take(7 - i)
                    r = slice(64 * i, 64 * i + 64)
                    for c in range(4):
                        last = pe.transpose(PS[:, 7 - i, c * 64:(c + 1) * 64], mod[r, 0, c * P:(c + 1) * P], ident[r, r])
                    last.then_inc(mod_T, 1)
                    reader[7 - i] = [(ab_made, 1 + i)]

                elif kind == "mod":
                    for n, pk in enumerate((1, 2)):
                        pe.wait_ge(mod_in, pk + 2)
                        take(4 + n)
                        for c in range(4):
                            last = pe.transpose(PS[:, 4 + n, c * P:(c + 1) * P], mod[:, pk, c * P:(c + 1) * P], ident)
                    last.then_inc(mod_T, 1)
                    reader[4] = reader[5] = [(ab_made, 3)]

                elif kind == "grow":
                    pe.wait_ge(mod_in, 3 + i)
                    b = grow_bank(i)
                    take(b, b + 1)
                    for j in range(2):
                        r = 32 * (2 * i + j)
                        last = pe.matmul(PS[:, b + j, :], ident[:, r:r + 1].to_broadcast([P, P]), mod[:, 1 + i, :],
                                         start=True, stop=True)
                    last.then_inc(g_ps, 1)
                    reader[b] = reader[b + 1] = [((g1_row, g2_row)[i], 1)]

                elif kind == "turn":
                    q = TURNS[i]
                    src, ready, _, _ = turn_of(i)
                    b = turn_bank(q)
                    take(b)
                    for s, v in ready:
                        pe.wait_ge(s, v)
                    for c in range(2):
                        for t in range(TB):
                            o = c * S + t * P
                            last = pe.transpose(PS[:, b, o:o + P], src[:, t, c * P:(c + 1) * P], ident)
                    last.then_inc(turned, 1)
                    reader[b] = [(turn_lo, q + 1)]

                elif kind == "fgate":
                    pe.wait_ge(wfg_lo, 1)
                    pe.wait_ge(turn_lo, TURNS[("norm", 0, 3)] + 1)
                    pe.wait_ge(wfg_hi, 1)
                    take(6)
                    group = []
                    for k in range(KC):
                        wh, wl = wfgs[:, 0, k, :], wfgs[:, 1, k, :]
                        group += [(wh, hT[:, 0, k, :]), (wl, hT[:, 0, k, :]), (wh, hT[:, 1, k, :])]
                    products(PS[0:FOX, 6, 0:S], group).then_inc(fg_ps, 1)
                    reader[6] = [(cum_made, 1)]

                elif kind == "cum":
                    take(5)
                    pe.wait_ge(cum_made, 1)
                    for t in range(TB):
                        last = pe.transpose(PS[:, 5, t * FOX:(t + 1) * FOX], fgt[:, 3, t * P:(t + 1) * P],
                                            ident[0:FOX, 0:FOX])
                    last.then_inc(cumq_ps, 1)
                    reader[5] = [(cumq_in, 1)]

                elif kind == "heads":
                    q, k, _, _, ready = heads_of(i)
                    b = heads_bank(i)
                    take(b)
                    pe.wait_ge(*ready)
                    for n, src in enumerate((q, k)):
                        for t in range(TB):
                            last = pe.transpose(PS[:, b, n * S + t * P:n * S + (t + 1) * P], src[:, t, :], ident)
                    last.then_inc(heads_ps, 1)
                    reader[b] = [(heads_lo, i + 1)]

                elif kind == "scores":
                    u, slot = i, i % 2
                    pe.wait_ge(heads_lo, u + 1)
                    if u == 0:
                        pe.wait_ge(zeroed, 2)
                        pe.wait_ge(ncum_lo, 1)
                    for n in range(2):
                        take(5 + n)
                        for t, (c0, c1) in enumerate(QB):
                            qh, ql = (qT[:, slot, part, n, t * P:(t + 1) * P] for part in range(2))
                            kh, kl = (kT[:, slot, part, 0:c1 - c0] for part in range(2))
                            group = [(qh, kh), (qh, kl), (ql, kh)]
                            if kind_of(u) == "fox":
                                pick = identr[:, 2 * u + n:2 * u + n + 1].to_broadcast([P, P])
                                group += [(pick, ncum[:, part, 0:c1 - c0]) for part in range(2)]
                            last = products(PS[:, 5 + n, c0:c1], group)
                        last.then_inc(score_ps, 1)
                        reader[5 + n] = [(smax, 2 * (2 * u + n) + 2)]

                elif kind == "probsT":
                    u, n = i
                    j = turned_head(u, n)
                    a = 2 * u + n
                    if kind_of(u) == "fox":
                        pe.wait_ge(fox_p, a + 1)
                    elif kind_of(u) == "diff":
                        pe.wait_ge(diff_p, u - FOX_P + 1)
                    else:
                        pe.wait_ge(exp_done, 2 * a + 2)
                    take(probs_bank(n))
                    src = scores_sb(u)
                    for m, c in enumerate((0, P, 2 * P)):
                        last = pe.transpose(PS[:, probs_bank(n), m * P:(m + 1) * P], src[:, n, c:c + P], ident)
                    last.then_inc(probs_ps, 1)
                    reader[probs_bank(n)] = [(probs_sb, j + 1)]

                elif kind == "values":
                    u, kd = i, kind_of(i)
                    pt = probs_T(u)
                    take(5)
                    if kd == "diff":
                        j = turned_head(u, 0)
                        pe.wait_ge(probs_sb, j + 1)
                        pe.wait_ge(tok_in, 6)
                        c = (u - FOX_P) * P
                        v = tok1[:, 5, :, c:c + P]
                        products(PS[:, 5, 0:P], [(pt[:, j % 2, 0:P], v[:, 0, :])])
                        last = products(PS[:, 5, P:2 * P], [(pt[:, j % 2, P:2 * P], v[:, 0, :]),
                                                            (pt[:, j % 2, 2 * P:3 * P], v[:, 1, :])])
                        reader[5] = [(dsq_in, u - FOX_P + 1)]
                    else:
                        for n in range(2):
                            j = turned_head(u, n)
                            pe.wait_ge(probs_sb, j + 1)
                            if kd == "fox":
                                pe.wait_ge(tok_in, 3)
                                v = tok1[:, 2, :, u * P + n * HD:u * P + (n + 1) * HD]
                            else:
                                pe.wait_ge(tok2_in, 6)
                                c = (u - FOX_P - DIFF_P) * P + n * HD
                                v = tok2[:, 2, :, c:c + HD]
                            o = PS[n * HD:(n + 1) * HD, 5, 0:S]
                            pe.matmul(o, v[:, 0, :], pt[:, j % 2, 0:S], start=True, stop=False)
                            last = pe.matmul(o[:, P:S], v[:, 1, :], pt[:, j % 2, S:S + P], start=False, stop=True)
                        reader[5] = [(mix_lo, u + 1)] if kd == "fox" else [(ybT_in, u - FOX_P - DIFF_P + 1)]
                    last.then_inc(value_ps, 1)

                elif kind == "back":
                    m = i - FOX_P - DIFF_P
                    take(4)
                    pe.wait_ge(ybT_in, m + 1)
                    for t in range(TB):
                        last = pe.transpose(PS[:, 4, t * P:(t + 1) * P], ybT[:, t * P:(t + 1) * P], ident)
                    last.then_inc(back_ps, 1)
                    reader[4] = [(yb_in, m + 1)]

                elif kind == "spatial":
                    pe.wait_ge(ws_low, 1)
                    take(4, 5)
                    for gr in range(8):
                        last = pe.transpose(PS[:, 4 + gr // 4, (gr % 4) * P:(gr % 4 + 1) * P], ws[:, gr, :], ident)
                    last.then_inc(ws_ps, 1)
                    reader[4] = reader[5] = [(ws_T, 1)]

                elif kind == "sgu":
                    b = 4 + 2 * i
                    take(b, b + 1)
                    pe.wait_ge(vn_made, TB)
                    pe.wait_ge(ws_T, 1)
                    for gr in range(4 * i, 4 * i + 4):
                        o = (gr % 2) * S
                        last = pe.matmul(PS[:, b + gr % 4 // 2, o:o + S].rearrange("p (t c) -> p t c", t=TB),
                                         wsT[:, gr, :], vb[:, :, gr * P:(gr + 1) * P], start=True, stop=True)
                    last.then_inc(sgu_ps, 1)
                    reader[b] = reader[b + 1] = [(ya_in, i + 1)]

                elif kind == "pT":
                    pe.wait_ge(p_in, 16)
                    take(4)
                    for c in range(2):
                        for t in range(TB):
                            last = pe.transpose(PS[:, 4, c * S + t * P:c * S + (t + 1) * P],
                                                pin[:, t, c * P:(c + 1) * P], ident)
                    last.then_inc(p_ps, 1)
                    reader[4] = [(p_lo, 1)]

        @block.scalar
        def _(act):
            own = 0

            def squares(n, h):
                if n == 0:
                    act.wait_ge(x_in, 16)
                if n == 1:
                    act.wait_ge(rel_out, 16)
                if n in (3, 4):
                    act.wait_ge(sums_made, 4 * n + 2 * h)
                for t in range(TB):
                    if n:
                        act.wait_ge(x_done, 2 * (2 * n - 2 + h) + t + 1)
                    act.activation(squares_of(n, t, h), x[:, t, h * W:(h + 1) * W], ACT.Square,
                                   accum_out=nss[:, n, t, h:h + 1]).then_inc(sums_made, 1)


            for it in ORDER:
                kind, i = it
                if kind == "split":
                    slot = landed(act, it)
                    if i >= SPL:
                        act.wait_ge(gemm_done, i - SPL + 1)
                    act.activation(slab_view(whi, i % SPL, i), slab_view(raw, slot, i), ACT.Copy).then_inc(hi_made, 1)

                elif kind == "cond":
                    act.wait_ge(c_col, 1)
                    act.activation(cond[:, 0, :], col[:, V_C:V_C + KC], ACT.Tanh, scale=0.5).then_inc(cond_th, 1)
                    for n, v in (("ln2_g", V_LN2), ("norm_mix_g_2", V_MIX), ("norm_ffn_g_2", V_FFN),
                                 ("norm_ple_g_2", V_PLE), ("b_sgu_spatial_2", V_BS)):
                        src = A[n].rearrange("a b c -> (a b c)") if len(A[n].shape) == 3 else A[n].rearrange("a b -> (a b)")
                        act.dma_start(vec[v:v + KC, :], src.rearrange("(r q) -> r q", q=P)).then_inc(vec_in, 16)
                    for n, r in (("fox_qk_g", V_QK), ("diff_qk_g", V_QK + 2)):
                        for h in range(2):
                            act.dma_start(vec[r:r + 2, h * HD:(h + 1) * HD], A[n][0]).then_inc(vec_in, 16)
                    act.dma_start(vec[V_DN:V_DN + 1, :], A["diff_norm_g"]).then_inc(vec_in, 16)

                    act.dma_start(wfg[:, :, :], A["w_in"][0, :, 3 * W:3 * W + FOX].rearrange("(c p) h -> p c h", p=P)
                                  ).then_inc(gate_w_in, 16)

                elif kind == "setup":
                    act.wait_ge(lam_dot, 1)
                    act.activation(lam[:, 2:4], lam[:, 0:2], ACT.Exp).then_inc(lam_exp, 1)
                    act.wait_ge(gate_w_in, 16)
                    act.activation(wfgs[:, 0], wfg[:, :, :], ACT.Copy).then_inc(wfg_hi, 1)

                elif kind == "grow":
                    act.wait_ge(g_ps, i + 1)
                    row = g1row if i == 0 else g2row[:, :]
                    act.activation(row.rearrange("p (j w) -> p j w", j=2), PS[:, grow_bank(i):grow_bank(i) + 2, :], ACT.Copy
                                   ).then_inc((g1_row, g2_row)[i], 1)

                elif kind == "sums" and i != (5, 0):
                    squares(*i)

                elif kind == "norm" and i < 2:
                    act.wait_ge(norm_rs, i + 1)
                    act.activation((xn1, xnb)[i][:, 0, :], x[:, 0, :], ACT.Copy, scale=nrs[:, i, 0:1]).then_inc(xn_act, 1)

                elif kind == "part" or kind == "turn" and not is_affine(i):
                    q = TURNS[i]
                    _, _, dst, c0 = turn_of(i)
                    b = turn_bank(q)
                    hi = dst[:, 0, c0:c0 + 2, :]
                    if dst is hT and slabs_before(it, "h"):
                        act.wait_ge(gemm_done, slabs_before(it, "h"))
                    if kind == "part":
                        act.wait_ge(turn_aff, q_affine(i) + 1)
                        act.activation(hi, affine(i), ACT.Copy).then_inc(turn_hi, 1)
                    else:
                        act.wait_ge(turned, q + 1)
                        gain = gain_of(i, 0)
                        if gain is None or isinstance(gain, float):
                            act.activation(hi.rearrange("p c s -> p (c s)"), PS[:, b, :], ACT.Copy,
                                           scale=1.0 if gain is None else gain).then_inc(turn_hi, 1)
                        else:
                            for c in range(2):
                                last = act.activation(hi[:, c, :], PS[:, b, c * S:(c + 1) * S], ACT.Copy,
                                                      scale=gain_of(i, c))
                            last.then_inc(turn_hi, 1)

                elif kind == "fgate":
                    act.wait_ge(fg_abs, 2)
                    act.activation(fgt[:, 1, :], fgt[:, 1, :], ACT.Exp).then_inc(act_step, 1)
                    own += 1
                    act.wait_ge(act_step, own)
                    act.activation(fgt[:, 1, :], fgt[:, 1, :], ACT.Ln, bias=1.0).then_inc(fg_log, 1)

                elif kind == "logf":
                    act.wait_ge(cum_made, 1)
                    act.wait_ge(zeroed, 2)
                    act.activation(ncum[0:FOX, 0, :], fgt[:, 3, :], ACT.Copy, scale=-1.0).then_inc(ncum_hi, 1)

                elif kind == "heads":
                    u, slot = i, i % 2
                    _, _, gq, gk, _ = heads_of(u)
                    act.wait_ge(heads_ps, u + 1)
                    act.wait_ge(zeroed, 2)
                    if u >= 2:
                        act.wait_ge(score_ps, 2 * (u - 1))
                    for n in range(2):
                        r = slice(n * HD, (n + 1) * HD)
                        act.activation(qT[r, slot, 0, n, :], PS[r, heads_bank(u), 0:S], ACT.Copy,
                                       scale=gq if isinstance(gq, float) else gq[r, :])
                    act.activation(kT[:, slot, 0, :], PS[:, heads_bank(u), S:2 * S], ACT.Copy, scale=gk).then_inc(heads_hi, 1)

                elif kind == "scores":
                    sc = scores_sb(i)
                    for n in range(2):
                        a = 2 * i + n
                        for t, (c0, c1) in enumerate(QB):
                            act.wait_ge(smax, 2 * a + t + 1)
                            act.activation(sc[:, n, c0:c1], sc[:, n, c0:c1], ACT.Exp, bias=nmax[:, a, t:t + 1],
                                           scale=-1.0, accum_out=lsum[:, a, t:t + 1]).then_inc(exp_done, 1)

                elif kind == "probsT":
                    u, n = i
                    j = turned_head(u, n)
                    act.wait_ge(probs_ps, j + 1)
                    if j >= 2:
                        act.wait_ge(value_ps, pair_of_turned(j - 2) + 1)
                    act.activation(probs_T(u)[:, j % 2, :], PS[:, probs_bank(n), 0:3 * P], ACT.Copy).then_inc(probs_sb, 1)

                elif kind == "values":
                    u, kd = i, kind_of(i)
                    act.wait_ge(value_ps, u + 1)
                    if kd == "fox":
                        act.activation(mixT[:, 0, u, :], PS[:, 5, 0:S], ACT.Copy).then_inc(mix_hi, 1)
                    elif kd == "moba":
                        m = u - FOX_P - DIFF_P
                        if m >= 1:
                            act.wait_ge(back_ps, m)
                        act.activation(ybT, PS[:, 5, 0:S], ACT.Copy).then_inc(ybT_in, 1)
                    else:
                        h = u - FOX_P
                        act.wait_ge(od_in, h + 1)
                        for t in range(TB):
                            c = t * DIFF + h
                            last = act.activation(sq[:, t, h * P:(h + 1) * P], PS[:, 5, t * P:(t + 1) * P], ACT.Square,
                                                  accum_out=dss[:, c:c + 1])
                        last.then_inc(dsq_in, 1)

                elif kind == "spatial":
                    act.wait_ge(ws_ps, 1)
                    act.activation(wsT[:, :, :].rearrange("p (b g) s -> p b (g s)", b=2), PS[:, 4:6, :], ACT.Copy
                                   ).then_inc(ws_T, 1)

                elif kind == "pT":
                    act.wait_ge(p_ps, 1)
                    act.activation(pT[:, 0].rearrange("p c s -> p (c s)"), PS[:, 4, :], ACT.Copy).then_inc(p_hi, 1)

                elif kind == "evac":
                    T = i
                    name, n, width = TILES[T]["name"], TILES[T]["n"], TILES[T]["width"]
                    ps, cols = tile_ps(T), slice(n * W, (n + 1) * W)
                    rs, half_rs = nrs, nrs2

                    def rows(out, func, factor, n):
                        act.wait_ge(norm_rs, n + 1)
                        for t in range(TB):
                            last = act.activation(out[:, t, :], PS[:, bank0(T) + t, :], func, scale=factor[:, n, t:t + 1])
                        return last

                    if name in ("fox", "diff", "v", "u", "q", "k", "vatt", "ga", "gb", "gate", "ff1", "ple_proj"):
                        complete(act, T)
                    if name in ("fox", "diff"):
                        j = n + (0 if name == "fox" else 3)
                        act.activation(tok1[:, j], ps, ACT.Copy).then_inc(tok_in, 1)
                        if n < 2:
                            m = n + (0 if name == "fox" else 2)
                            if m:
                                act.wait_ge(hss_in, m)
                            act.activation(sq[:, :, :], ps, ACT.Square).then_inc(sq_in, 1)
                    elif name == "v":
                        rows(vb[:, :, cols], ACT.Gelu_apprx_tanh, rs, 2).then_inc(v_in, 1)
                    elif name == "u":
                        rows(ub[:, :, cols], ACT.Gelu_apprx_tanh, rs, 2).then_inc(u_in, 1)
                    elif name in ("q", "k", "vatt"):
                        j = ("q", "k", "vatt").index(name)
                        rows(tok2[:, j, :, cols], ACT.Copy, rs, 2).then_inc(tok2_in, 1)
                    elif name == "ga":
                        if n == 0:
                            act.wait_ge(ws_T, 1)
                            act.wait_ge(ws_ps, 1)
                        else:
                            act.wait_ge(ga_in, 1)
                        rows(th2, ACT.Tanh, half_rs, 2).then_inc(ga_th, 1)
                    elif name == "gb":
                        act.wait_ge(sgu_ps, 2)
                        rows(vb[:, :, cols], ACT.Tanh, half_rs, 2).then_inc(gb_in, 1)
                    elif name == "gate":
                        if n:
                            act.wait_ge(r_in, n)
                        act.activation(th1[:, :, 0:width], ps, ACT.Tanh, scale=0.5).then_inc(gate_th, 1)
                    elif name == "ff1":
                        if n >= 2:
                            act.wait_ge(turned, TURNS[("hid2", n - 2, 1)] + 1)
                        act.activation(hid2[:, n % 2], ps, ACT.Relu).then_inc(relu_in, 1)
                    elif name == "ple_proj":
                        act.activation(pp[:, :, cols], ps, ACT.Copy).then_inc(pp_in, 1)
                    elif name == "ple":
                        act.wait_ge(norm_rs, 5)
                        for t in range(TB):
                            rows_complete(act, T, t)
                            act.activation(thp[:, n, t, :], PS[:, bank0(T) + t, :], ACT.Tanh,
                                           scale=half_rs[:, 4, t:t + 1]).then_inc(ple_th, 1)
                            if (n, t) == (1, 0):
                                squares(5, 0)

        @block.vector
        def _(dve):
            own = [0]

            def then(ins):
                ins.then_inc(dve_step, 1)
                own[0] += 1
                dve.wait_ge(dve_step, own[0])

            def whole(t):
                return t.bitcast(F32)

            dve.memset(table[BUCKETS:BUCKETS + 1, :], MASKED).then_inc(table_set, 1)

            for it in ORDER:
                kind, i = it
                if kind == "split":
                    slot = landed(dve, it)
                    dve.wait_ge(hi_made, i + 1)
                    if i >= SPL:
                        dve.wait_ge(gemm_done, i - SPL + 1)
                    dve.tensor_tensor(slab_view(wlo, i % SPL, i), slab_view(raw, slot, i),
                                      whole(slab_view(whi, i % SPL, i)), ALU.subtract).then_inc(lo_made, 1)

                elif kind == "cond":
                    dve.wait_ge(c_ps, 1)
                    dve.tensor_copy(col[:, 0:2 * KC], PS[:, 5, 0:2 * KC]).then_inc(c_col, 1)
                    dve.wait_ge(c_col, 1)
                    dve.wait_ge(cond_th, 1)
                    then(dve.scalar_tensor_tensor(out=cond[:, 1, :], in0=cond[:, 0, :], scalar=1.0,
                                                  in1=col[:, V_C:V_C + KC], op0=ALU.add, op1=ALU.mult))
                    dve.tensor_scalar(cond32[:, :, :], spread(cond[:, 1, :], 32), 0.5, None, ALU.mult
                                      ).then_inc(cond_made, 1)

                elif kind == "vectors":
                    dve.wait_ge(vec_ps, 1)
                    then(dve.tensor_copy(col[:, V_LN2:V_ALL], PS[:, 4, V_LN2:V_ALL]))
                    dve.tensor_scalar(col[:, V_ALL:V_ALL + 1], col[:, V_QK:V_QK + 1], HD ** -0.5, None, ALU.mult)
                    dve.tensor_scalar(col[:, V_ALL + 1:V_ALL + 2], col[:, V_QK + 2:V_QK + 3], HD ** -0.5, None, ALU.mult)
                    dve.tensor_scalar(col[:, V_ALL + 2:V_ALL + 3], col[:, V_DN:V_DN + 1], 1.0 - LAM_INIT, None,
                                      ALU.mult).then_inc(col_made, 1)

                elif kind == "setup":
                    dve.wait_ge(cond_in, 48)
                    dve.tensor_copy(identr[:, :], ident)
                    dve.wait_ge(setup_in, 16 * NSETUP)
                    dve.memset(ones[:, :], 1.0)
                    for n in range(2):
                        last = dve.tensor_tensor_reduce(lprod[:, n, :], lamb[:, 2 * n, :], lamb[:, 2 * n + 1, :],
                                                        1.0, 0.0, ALU.mult, ALU.add, lam[:, n:n + 1])
                    last.then_inc(lam_dot, 1)
                    dve.wait_ge(lam_exp, 1)
                    dve.scalar_tensor_tensor(out=lam[:, 4:5], in0=lam[:, 2:3], scalar=LAM_INIT, in1=lam[:, 3:4],
                                             op0=ALU.add, op1=ALU.subtract).then_inc(lam_made, 1)
                    dve.wait_ge(gate_w_in, 16)
                    dve.wait_ge(wfg_hi, 1)
                    dve.tensor_tensor(wfgs[:, 1], wfg[:, :, :], whole(wfgs[:, 0]), ALU.subtract).then_inc(wfg_lo, 1)

                elif kind == "relbias":
                    dve.wait_ge(rel_ps, 1)
                    dve.tensor_copy(relrow[:, :], PS[0:MOBA, 5, 0:SKEW]).then_inc(rel_row, 1)

                elif kind == "ada" and (i % KC == KC - 1 or i == 3):
                    if i == 3:
                        dve.wait_ge(bias_in, 16 * 4)
                    dve.wait_ge(ada_used, i + 1)
                    if i < KC:
                        half = i // 4
                        r = slice(64 * half, 64 * half + 64)
                        dve.tensor_tensor(mod[r, 0, :], PS[r, 7 - half, :], mod[r, 0, :], ALU.add).then_inc(mod_in, 1)
                    else:
                        pack = i // KC
                        dve.wait_ge(late_bias_in, 16 * 4)
                        dve.tensor_tensor(mod[:, pack, :], PS[:, 7, :], mod[:, pack, :], ALU.add).then_inc(mod_in, 1)

                elif kind == "mod":
                    dve.wait_ge(mod_T, i + 1)
                    if i < 2:
                        k = slice(4 * i, 4 * i + 4)
                        both = PS[:, 7 - i, 0:S].rearrange("p (c j r) -> p c j r", c=4, j=2)
                        dve.tensor_copy(AB[:, 1, k], both[:, :, 0, 0])
                        dve.scalar_tensor_tensor(out=AB[:, 0, k], in0=both[:, :, 1, 0], scalar=1.0,
                                                 in1=col[:, V_LN1 + 4 * i:V_LN1 + 4 * i + 4], op0=ALU.add, op1=ALU.mult
                                                 ).then_inc(ab_made, 1)
                    else:
                        def columns(b, j0):
                            return PS[:, b, :].rearrange("p (c j r) -> p j c r", c=4, j=4)[:, j0:j0 + 2, :, 0]

                        dve.tensor_copy(AB[:, 3, :].rearrange("p (j c) -> p j c", j=2), columns(4, 2))
                        dve.scalar_tensor_tensor(out=AB[:, 2, :].rearrange("p (j c) -> p j c", j=2), in0=columns(5, 0),
                                                 scalar=1.0,
                                                 in1=col[:, V_LN2:V_LN2 + KC].rearrange("p (j c) -> p j c", j=2),
                                                 op0=ALU.add, op1=ALU.mult).then_inc(ab_made, 1)

                elif kind == "norm" and i < 2:
                    dve.wait_ge(norm_rs, i + 1)
                    dve.tensor_scalar((xn1, xnb)[i][:, 1, :], x[:, 1, :], nrs[:, i, 1:2], None, ALU.mult
                                      ).then_inc(xn_dve, 1)

                elif kind == "final":
                    dve.wait_ge(gfin_in, 16)
                    for t in range(TB):
                        dve.wait_ge(norm_rs, 6 + t)
                        for h in range(2):
                            cols = slice(h * W, (h + 1) * W)
                            dve.scalar_tensor_tensor(out=fin[:, t, cols], in0=x[:, t, cols], scalar=nrs[:, 5, t:t + 1],
                                                     in1=gfin[:, cols], op0=ALU.mult, op1=ALU.mult
                                                     ).then_inc(out_made, 1)

                elif kind == "turn" and is_affine(i):
                    q, b, c0 = TURNS[i], turn_bank(TURNS[i]), 2 * i[2]
                    dve.wait_ge(turned, q + 1)
                    dve.wait_ge(ab_made, 1 + i[2] // 2 if i[1] == 0 else 3)
                    if i[2] >= 2:
                        dve.wait_ge(turn_lo, q - 1)
                    for c in range(2):
                        k = c0 + c
                        last = dve.tensor_scalar(affine(i)[:, c, :], PS[:, b, c * S:(c + 1) * S],
                                                 AB[:, 2 * i[1], k:k + 1], AB[:, 2 * i[1] + 1, k:k + 1],
                                                 ALU.mult, ALU.add)
                    last.then_inc(turn_aff, 1)

                elif kind in ("part", "turn"):
                    q = TURNS[i]
                    _, _, dst, c0 = turn_of(i)
                    b = turn_bank(q)
                    if dst is hT and slabs_before(it, "h"):
                        dve.wait_ge(gemm_done, slabs_before(it, "h"))
                    dve.wait_ge(turned, q + 1)
                    lo, hi = dst[:, 1, c0:c0 + 2, :], whole(dst[:, 0, c0:c0 + 2, :])
                    if kind == "part":
                        dve.wait_ge(turn_hi, q + 1)
                        dve.wait_ge(turn_aff, q_affine(i) + 1)
                        dve.tensor_tensor(lo, affine(i), hi, ALU.subtract).then_inc(turn_lo, 1)
                    else:
                        dve.wait_ge(turn_hi, q + 1)
                        gain = gain_of(i, 0)
                        if gain is None or isinstance(gain, float):
                            dve.scalar_tensor_tensor(out=lo.rearrange("p c s -> p (c s)"), in0=PS[:, b, :],
                                                     scalar=1.0 if gain is None else gain,
                                                     in1=hi.rearrange("p c s -> p (c s)"),
                                                     op0=ALU.mult, op1=ALU.subtract).then_inc(turn_lo, 1)
                        else:
                            for c in range(2):
                                last = dve.scalar_tensor_tensor(out=lo[:, c, :], in0=PS[:, b, c * S:(c + 1) * S],
                                                                scalar=gain_of(i, c), in1=hi[:, c, :],
                                                                op0=ALU.mult, op1=ALU.subtract)
                            last.then_inc(turn_lo, 1)

                elif kind == "fgate":
                    dve.wait_ge(fg_ps, 1)
                    dve.tensor_scalar(fgt[:, 0, :], PS[0:FOX, 6, 0:S], bf[:, :], None, ALU.add).then_inc(fg_abs, 1)
                    dve.wait_ge(fg_abs, 1)
                    dve.scalar_tensor_tensor(out=fgt[:, 1, :], in0=fgt[:, 0, :], scalar=-1.0, in1=fgt[:, 0, :],
                                             op0=ALU.mult, op1=ALU.min).then_inc(fg_abs, 1)

                elif kind == "logf":
                    dve.wait_ge(fg_log, 1)
                    then(dve.scalar_tensor_tensor(out=fgt[:, 2, :], in0=fgt[:, 0, :], scalar=0.0, in1=fgt[:, 1, :],
                                                  op0=ALU.min, op1=ALU.subtract))
                    dve.tensor_tensor_scan(fgt[:, 3, :], ones[:, :], fgt[:, 2, :], 0.0, ALU.mult, ALU.add
                                           ).then_inc(cum_made, 1)
                    dve.wait_ge(ncum_hi, 1)
                    dve.wait_ge(cum_made, 1)
                    dve.scalar_tensor_tensor(out=ncum[0:FOX, 1, :], in0=fgt[:, 3, :], scalar=-1.0,
                                             in1=whole(ncum[0:FOX, 0, :]), op0=ALU.mult, op1=ALU.subtract
                                             ).then_inc(ncum_lo, 1)

                elif kind == "cum":
                    dve.wait_ge(cumq_ps, 1)
                    dve.tensor_copy(cumq[:, :, :].rearrange("p t h -> p (t h)"), PS[:, 5, 0:TB * FOX]).then_inc(cumq_in, 1)

                elif kind == "unit":
                    j = (0, 1, 3, 4)[i]
                    dve.wait_ge(hrs_made, i + 1)
                    dve.wait_ge(tok_in, j + 1)
                    t = tok1[:, j].rearrange("p t (h d) -> p (t h) d", d=HD)
                    dve.tensor_tensor(t, t, spread(hrs[:, i, :], HD), ALU.mult).then_inc(qk_ready, 1)

                elif kind == "heads":
                    u, slot = i, i % 2
                    _, _, gq, gk, _ = heads_of(u)
                    dve.wait_ge(heads_ps, u + 1)
                    dve.wait_ge(heads_hi, u + 1)
                    for n in range(2):
                        r = slice(n * HD, (n + 1) * HD)
                        dve.scalar_tensor_tensor(out=qT[r, slot, 1, n, :], in0=PS[r, heads_bank(u), 0:S],
                                                 scalar=gq if isinstance(gq, float) else gq[r, :],
                                                 in1=whole(qT[r, slot, 0, n, :]), op0=ALU.mult, op1=ALU.subtract)
                    dve.scalar_tensor_tensor(out=kT[:, slot, 1, :], in0=PS[:, heads_bank(u), S:2 * S], scalar=gk,
                                             in1=whole(kT[:, slot, 0, :]), op0=ALU.mult, op1=ALU.subtract
                                             ).then_inc(heads_lo, 1)

                elif kind == "scores":
                    u, kd, sc = i, kind_of(i), scores_sb(i)
                    if u == 0:
                        dve.wait_ge(rel_out, 16)
                    for n in range(2):
                        a = 2 * u + n
                        dve.wait_ge(score_ps, a + 1)
                        if u >= 2 and (kd != "moba" or kind_of(u - 2) == "moba"):
                            dve.wait_ge(probs_ps, turned_head(u - 2, n if kind_of(u - 2) != "diff" else 0) + 1)
                        if kd == "fox":
                            if a == 0:
                                dve.wait_ge(setup_in, 16 * NSETUP)
                                dve.wait_ge(cumq_in, 1)
                            if a >= 2:
                                dve.wait_ge(smax, 2 * (a - 2) + 2)
                            dve.tensor_scalar(mcum[:, a % 2, 0:P], mask[:, P:2 * P], cumq[:, 0, a:a + 1], None, ALU.add)
                            dve.tensor_scalar(mcum[:, a % 2, P:3 * P], mask, cumq[:, 1, a:a + 1], None, ALU.add
                                              ).then_inc(mcum_in, 1)
                            dve.wait_ge(mcum_in, a + 1)
                            bias = [mcum[:, a % 2, c0:c1] for c0, c1 in QB]
                        elif kd == "diff":
                            dve.wait_ge(alibi_in, 16)
                            bias = [alibi[:, u - FOX_P, P:2 * P], alibi[:, u - FOX_P, :]]
                        else:
                            if u == FOX_P + DIFF_P:
                                dve.wait_ge(rel_in, 16)
                            h = a - 2 * (FOX_P + DIFF_P)
                            bias = [toep[:, h, 0:P], toep[:, h, :]]
                        for t, (c0, c1) in enumerate(QB):
                            made, score = sc[:, n, c0:c1], PS[:, 5 + n, c0:c1]
                            if kd == "moba":
                                made, score = backwards(made), backwards(score)
                            dve.tensor_tensor_reduce(made, score, bias[t], -1.0, 3e38,
                                                     ALU.add, ALU.min, nmax[:, a, t:t + 1]).then_inc(smax, 1)
                    for n in range(2):
                        a = 2 * u + n
                        dve.wait_ge(exp_done, 2 * a + 2)
                        then(dve.reciprocal(rinv[:, a, :], lsum[:, a, :]))
                        if kd == "fox":
                            for t, (c0, c1) in enumerate(QB):
                                last = dve.tensor_scalar(sc[:, n, c0:c1], sc[:, n, c0:c1], rinv[:, a, t:t + 1], None,
                                                         ALU.mult)
                            last.then_inc(fox_p, 1)
                    if kd == "diff":
                        a = 2 * u
                        if u == FOX_P:
                            dve.wait_ge(lam_made, 1)
                        then(dve.tensor_scalar(rinv[:, a + 1, :], rinv[:, a + 1, :], lam[:, 4:5], None, ALU.mult))
                        for t, (c0, c1) in enumerate(QB):
                            last = dve.tensor_scalar(sc[:, 1, c0:c1], sc[:, 1, c0:c1], rinv[:, a + 1, t:t + 1], None,
                                                     ALU.mult)
                        then(last)
                        for t, (c0, c1) in enumerate(QB):
                            last = dve.scalar_tensor_tensor(out=sc[:, 0, c0:c1], in0=sc[:, 0, c0:c1],
                                                            scalar=rinv[:, a, t:t + 1], in1=sc[:, 1, c0:c1],
                                                            op0=ALU.mult, op1=ALU.subtract)
                        last.then_inc(diff_p, 1)

                elif kind == "values":
                    u, kd = i, kind_of(i)
                    if kd == "fox":
                        dve.wait_ge(value_ps, u + 1)
                        dve.wait_ge(mix_hi, u + 1)
                        dve.tensor_tensor(mixT[:, 1, u, :], PS[:, 5, 0:S], whole(mixT[:, 0, u, :]), ALU.subtract
                                          ).then_inc(mix_lo, 1)
                    elif kd == "diff":
                        h = u - FOX_P
                        dve.wait_ge(value_ps, u + 1)
                        dve.tensor_copy(od[:, :, h * P:(h + 1) * P], PS[:, 5, 0:S].rearrange("p (t d) -> p t d", t=TB)
                                        ).then_inc(od_in, 1)

                elif kind == "diffnorm":
                    dve.wait_ge(drs_made, 1)
                    dve.wait_ge(od_in, DIFF)
                    o = od.rearrange("p t (h d) -> p (t h) d", h=DIFF)
                    dve.tensor_tensor(o, o, spread(drs[:, :], P), ALU.mult).then_inc(od_made, 1)

                elif kind == "back":
                    m = i - FOX_P - DIFF_P
                    dve.wait_ge(back_ps, m + 1)
                    inv = rinv[:, 2 * i:2 * i + 2, :].rearrange("p n t -> p t n")
                    dve.tensor_tensor(tok2[:, 0, :, m * P:(m + 1) * P].rearrange("p t (n d) -> p t n d", n=2),
                                      PS[:, 4, 0:S].rearrange("p (t n d) -> p t n d", t=TB, n=2), spread(inv, HD),
                                      ALU.mult).then_inc(yb_in, 1)

                elif kind == "layernorm":
                    dve.wait_ge(v_in, 2)
                    for t in range(TB):
                        for h in range(2):
                            last = dve.bn_stats(bn[:, t, h, :], vb[:, t, h * W:(h + 1) * W])
                    then(last)
                    for t in range(TB):
                        last = dve.bn_aggr(mv[:, t, :], bn[:, t].rearrange("p h s -> p (h s)"))
                    last.then_inc(mv_made, 1)
                    dve.wait_ge(mv_made, 1)
                    dve.wait_ge(vrs_made, 1)
                    for t in range(TB):
                        dve.tensor_scalar(vb[:, t, :], vb[:, t, :], mv[:, t, 0:1], vrs[:, t:t + 1],
                                          ALU.subtract, ALU.mult).then_inc(vc_made, 1)

                elif kind == "sgu":
                    dve.wait_ge(u_in, 2)
                    dve.wait_ge(sgu_ps, i + 1)
                    b = 4 + 2 * i
                    for gr in range(4 * i, 4 * i + 4):
                        c = (gr % 2) * S
                        uc = ub[:, :, gr * P:(gr + 1) * P]
                        last = dve.scalar_tensor_tensor(
                            out=uc, in0=PS[:, b + gr % 4 // 2, c:c + S].rearrange("p (t c) -> p t c", t=TB),
                            scalar=col[:, V_BS + gr:V_BS + gr + 1], in1=uc, op0=ALU.add, op1=ALU.mult)
                    last.then_inc(ya_in, 1)

                elif kind == "merge":
                    cols = slice(i * W, (i + 1) * W)
                    y = tok2[:, 0, :, cols]
                    dve.wait_ge(yb_in, 4 * (i + 1))
                    dve.wait_ge(gb_in, i + 1)
                    dve.wait_ge(ga_in, i + 1)
                    then(dve.scalar_tensor_tensor(out=y, in0=vb[:, :, cols], scalar=1.0, in1=y, op0=ALU.add,
                                                  op1=ALU.mult))
                    dve.tensor_tensor(y, y, ub[:, :, cols], ALU.add).then_inc(merged, 1)

                elif kind == "pT":
                    dve.wait_ge(p_ps, 1)
                    dve.wait_ge(p_hi, 1)
                    dve.tensor_tensor(pT[:, 1].rearrange("p c s -> p (c s)"), PS[:, 4, :],
                                      whole(pT[:, 0]).rearrange("p c s -> p (c s)"), ALU.subtract).then_inc(p_lo, 1)

                elif kind == "evac":
                    T = i
                    name, n, width = TILES[T]["name"], TILES[T]["n"], TILES[T]["width"]
                    ps, cols = tile_ps(T), slice(n * W, (n + 1) * W)
                    if name in ("fox", "diff") and n < 2:
                        m = n + (0 if name == "fox" else 2)
                        dve.wait_ge(sq_in, m + 1)
                        dve.tensor_reduce(hss[:, m, :], sq[:, :, :].rearrange("p t (h d) -> p (t h) d", d=HD), AX,
                                          ALU.add).then_inc(hss_in, 1)
                    elif name in ("w_out", "down"):
                        row, tmp, m = (g1row, sq, n) if name == "w_out" else (g2row[:, :], tmpb, 2 + n)
                        dve.wait_ge(g1_row if name == "w_out" else g2_row, 1)
                        if name == "w_out":
                            dve.wait_ge(dsq_in, DIFF)
                        if n:
                            dve.wait_ge(x_done, 2 * m)
                        for t in range(TB):
                            rows_complete(dve, T, t)
                            dve.tensor_tensor(tmp[:, t, :], ps[:, t, :], row[:, cols], ALU.mult).then_inc(scaled, 1)
                            dve.wait_ge(scaled, 2 * m + t + 1)
                            dve.tensor_tensor(x[:, t, cols], x[:, t, cols], tmp[:, t, :], ALU.add).then_inc(x_done, 1)
                    elif name == "w_out2":
                        complete(dve, T)
                        for t in range(TB):
                            dve.tensor_tensor(x[:, t, cols], x[:, t, cols], ps[:, t, :], ALU.add).then_inc(x_done, 1)
                    elif name == "ff2":
                        complete(dve, T)
                        dve.wait_ge(norm_rs, 4)
                        for t in range(TB):
                            dve.scalar_tensor_tensor(out=x[:, t, cols], in0=PS[:, bank0(T) + t, :],
                                                     scalar=nrs2[:, 3, t:t + 1], in1=x[:, t, cols],
                                                     op0=ALU.mult, op1=ALU.add).then_inc(x_done, 1)
                    elif name == "gate":
                        dve.wait_ge(gate_th, n + 1)
                        th = th1[:, :, 0:width]
                        dve.scalar_tensor_tensor(out=hid1[:, n % 2, :, 0:width], in0=th, scalar=1.0, in1=ps,
                                                 op0=ALU.add, op1=ALU.mult).then_inc(r_in, 1)
                    elif name == "up":
                        complete(dve, T)
                        dve.wait_ge(r_in, n + 1)
                        o = hid1[:, n % 2, :, 0:width]
                        dve.scalar_tensor_tensor(out=o, in0=o, scalar=0.5, in1=ps, op0=ALU.mult, op1=ALU.mult
                                                 ).then_inc(hid_in, 1)
                    elif name == "ga":
                        dve.wait_ge(ga_th, n + 1)
                        dve.wait_ge(ya_in, 2)
                        uc = ub[:, :, cols]
                        dve.scalar_tensor_tensor(out=uc, in0=th2, scalar=1.0, in1=uc, op0=ALU.add, op1=ALU.mult
                                                 ).then_inc(ga_in, 1)
                    elif name == "ff1":
                        dve.wait_ge(relu_in, n + 1)
                        h = hid2[:, n % 2]
                        dve.tensor_tensor(h, h, h, ALU.mult).then_inc(hid2_in, 1)
                    elif name == "ple":
                        dve.wait_ge(pp_in, 2)
                        for t in range(TB):
                            dve.wait_ge(ple_th, 2 * n + t + 1)
                            then(dve.scalar_tensor_tensor(out=thp[:, n, t, :], in0=thp[:, n, t, :], scalar=1.0,
                                                          in1=pp[:, t, cols], op0=ALU.add, op1=ALU.mult))
                            dve.scalar_tensor_tensor(out=x[:, t, cols], in0=thp[:, n, t, :], scalar=0.5,
                                                     in1=x[:, t, cols], op0=ALU.mult, op1=ALU.add).then_inc(x_done, 1)

        @block.gpsimd
        def _(pool):
            own = [0]

            def then(ins):
                ins.then_inc(pool_step, 1)
                own[0] += 1
                pool.wait_ge(pool_step, own[0])

            def inverse_root(dst, sums, width):
                then(pool.tensor_scalar(dst, sums, 1.0 / width, EPS, ALU.mult, ALU.add))
                n = dst.shape[-1]
                return pool.tensor_tensor(dst, dst, expo[:, 0:n], ALU.pow)

            bias = A["b_ada"]
            for j in range(4):
                r = slice(32 * j, 32 * j + 32)
                half, scale = divmod(j, 2)
                pool.dma_start(mod[r, 0, :], bass.AP(tensor=bias.tensor, offset=bias.offset + scale * D + half * W,
                                                    ap=[[0, 32], [1, W]])).then_inc(bias_in, 16)
            pool.dma_start(lamb[:, :, :], A["diff_lam"].to_broadcast([P, 4, HD])).then_inc(setup_in, 16)
            pool.dma_start(hot[:, :], A["constants"][0:BUCKETS + 1, C_HOT:C_ALL]).then_inc(setup_in, 16)
            pool.dma_start(table[0:BUCKETS, :], A["rel_bias_2"]).then_inc(setup_in, 16)
            pool.dma_start(bf[:, :], A["b_f"].rearrange("a h -> h a")).then_inc(setup_in, 16)
            pool.dma_start(con[:, C_MASK:C_ALIBI], A["constants"][:, C_MASK:C_ALIBI]).then_inc(setup_in, 16)
            then(pool.memset(expo[:, :], -0.5))
            then(pool.memset(qT[HD:P, :, :, 0, :].rearrange("p a b s -> p (a b) s").bitcast(F32), 0.0))
            pool.memset(qT[0:HD, :, :, 1, :].rearrange("p a b s -> p (a b) s").bitcast(F32), 0.0).then_inc(zeroed, 1)
            pool.wait_ge(zeroed, 1)
            pool.memset(ncum[:, :, :].bitcast(F32), 0.0).then_inc(zeroed, 1)

            for it in ORDER:
                kind, i = it
                if kind == "relbias":
                    pool.wait_ge(rel_row, 1)
                    pool.dma_start(skew.ap(), relrow[:, :]).then_inc(rel_out, 16)
                    for j in range(4):
                        pool.dma_start(mod[32 * j:32 * j + 32, 1:3, :],
                                       bass.AP(tensor=bias.tensor, offset=bias.offset + (4 + j) * W,
                                               ap=[[0, 32], [4 * W, 2], [1, W]])).then_inc(late_bias_in, 16)
                    pool.dma_start(alibi[:, :, :], A["constants"][:, C_ALIBI:C_HOT].rearrange("p (h k) -> p h k", h=DIFF)
                                   ).then_inc(alibi_in, 16)

                elif kind == "final":
                    for t in range(TB):
                        c = slice(t, t + 1)
                        pool.wait_ge(sums_made, 4 * 5 + 2 + t + 1)
                        then(pool.tensor_tensor(nss[:, 5, c, 0], nss[:, 5, c, 0], nss[:, 5, c, 1], ALU.add))
                        inverse_root(nrs[:, 5, c], nss[:, 5, c, 0], D).then_inc(norm_rs, 1)

                elif kind == "norm":
                    n = i
                    pool.wait_ge(sums_made, 4 * n + 4)
                    then(pool.tensor_tensor(nss[:, n, :, 0], nss[:, n, :, 0], nss[:, n, :, 1], ALU.add))
                    last = inverse_root(nrs[:, n, :], nss[:, n, :, 0], D)
                    if n in (2, 3, 4):
                        then(last)
                        if n == 3:
                            last = pool.tensor_tensor(nrs2[:, n, :], nrs[:, n, :], nrs[:, n, :], ALU.mult)
                        else:
                            last = pool.tensor_scalar(nrs2[:, n, :], nrs[:, n, :], 0.5, None, ALU.mult)
                    last.then_inc(norm_rs, 1)
                    if n == 2:
                        pool.wait_ge(gemm_done, slabs_before(("norm", 2), "hid"))
                        pool.wait_ge(x_done, 8)
                        pool.dma_start(ws[:, :, :], A["w_sgu_spatial_2"][0].rearrange("g t s -> t g s")
                                       ).then_inc(ws_in, 16)
                        for n, name in enumerate(("ln_v_g_2", "ln_v_b_2")):
                            pool.dma_start(lngb[:, n, :], A[name].to_broadcast([P, D])).then_inc(ln_in, 16)
                    elif n == 3:
                        pool.wait_ge(score_ps, 2 * PAIRS)
                        pool.dma_start(pin[:, :, :], A["p_2"][0, 0].rearrange("(t p) f -> p t f", p=P)).then_inc(p_in, 16)
                    elif n == 4:
                        pool.wait_ge(gemm_done, slabs_before(("norm", 4), "hid"))
                        pool.dma_start(gfin[:, :], A["norm_final_g_2"].rearrange("(a d) -> a d", a=1).to_broadcast([P, D])
                                       ).then_inc(gfin_in, 16)

                elif kind == "unit":
                    pool.wait_ge(hss_in, i + 1)
                    inverse_root(hrs[:, i, :], hss[:, i, :], HD).then_inc(hrs_made, 1)

                elif kind == "diffnorm":
                    pool.wait_ge(dsq_in, DIFF)
                    inverse_root(drs[:, :], dss[:, :], 2 * HD).then_inc(drs_made, 1)

                elif kind == "spatial":
                    pool.wait_ge(ws_in, 16)
                    pool.affine_select(out=ws[:, :, :], in_=ws[:, :, :], compare_op=ALU.is_ge, fill=0.0, base=0,
                                       pattern=[[0, 8], [-1, P]], channel_multiplier=1).then_inc(ws_low, 1)

                elif kind == "layernorm":
                    pool.wait_ge(mv_made, 1)
                    then(pool.tensor_scalar(vrs[:, :], mv[:, :, 1], 1.0, EPS, ALU.mult, ALU.add))
                    pool.tensor_tensor(vrs[:, :], vrs[:, :], expo[:, 0:TB], ALU.pow).then_inc(vrs_made, 1)
                    pool.wait_ge(ln_in, 32)
                    for t in range(TB):
                        pool.wait_ge(vc_made, t + 1)
                        then(pool.tensor_tensor(vb[:, t, :], vb[:, t, :], lngb[:, 0, :], ALU.mult))
                        pool.tensor_tensor(vb[:, t, :], vb[:, t, :], lngb[:, 1, :], ALU.add).then_inc(vn_made, 1)
                    pool.wait_ge(vn_made, TB)
                    pool.wait_ge(rel_out, 16)
                    pool.dma_start(toep[:, :, :], bass.AP(tensor=skew, offset=0,
                                                          ap=[[1, P], [SKEW, MOBA], [1, 2 * P]])).then_inc(rel_in, 16)


def q_affine(key):
    return 4 * key[1] + key[2]


def constants():
    c = np.zeros((P, C_ALL), np.float32)
    c[:, C_ID:C_ID + P] = np.eye(P)
    dist = P + np.arange(P)[:, None] - np.arange(2 * P)[None, :]
    c[:, C_MASK:C_MASK + 2 * P] = np.where(dist >= 0, 0.0, MASKED)
    for h in range(DIFF):
        slope = 2.0 ** (-8.0 * (h + 1) / DIFF)
        c[:, C_ALIBI + h * 2 * P:C_ALIBI + (h + 1) * 2 * P] = np.where(dist >= 0, -slope * dist, MASKED)
    far = np.arange(SKEW) - (P - 1)
    exact = BUCKETS // 2
    n = np.maximum(far, exact).astype(np.float32)
    large = exact + (np.log(n / np.float32(exact)) / np.float32(np.log(1024 / exact)) * np.float32(BUCKETS - exact)
                     ).astype(np.int32)
    bucket = np.where(far < 0, BUCKETS, np.where(far < exact, np.maximum(far, 0), np.minimum(large, BUCKETS - 1)))
    c[bucket, C_HOT + np.arange(SKEW)] = 1.0
    return c


_INS = ["x", "c", "ln1_g", "ln2_g", "w_ada", "b_ada", "w_in", "b_f", "fox_qk_g", "diff_qk_g", "diff_lam",
        "diff_norm_g", "w_out", "w_gate", "w_up", "w_down", "p_2", "norm_mix_g_2", "w_in_2", "w_sgu_spatial_2",
        "b_sgu_spatial_2", "ln_v_g_2", "ln_v_b_2", "rel_bias_2", "w_out_2", "norm_ffn_g_2", "w_ff1_2", "w_ff2_2",
        "norm_ple_g_2", "w_ple_gate_2", "w_ple_proj_2", "norm_final_g_2"]


def kernel(**inputs):
    import concourse.bacc as bacc
    from concourse.bass_utils import run_bass_kernel_spmd

    nc = bacc.Bacc("TRN2", target_bir_lowering=False, num_devices=1)
    arrays, args = {}, {}
    for name in _INS + ["constants"]:
        a = constants() if name == "constants" else np.ascontiguousarray(inputs[name])
        arrays[f"in_{name}"] = a
        args[name] = nc.dram_tensor(f"in_{name}", a.shape, mybir.dt.from_np(a.dtype), kind="ExternalInput").ap()
    result = nc.dram_tensor("out_x", (1, S, D), F32, kind="ExternalOutput").ap()
    build(nc, args, result)
    r = run_bass_kernel_spmd(nc, [arrays], core_ids=[0])
    return r.results[0]["out_x"]
```
